# Optimizing a Trainium2 kernel written in Bass

```python
import jax, jax.numpy as jnp
from jax import lax
import numpy as np

D_MODEL = 1024
BATCH = 1
SEQ = 512
DEPTH = 4

F32 = jnp.float32
CHUNK = 64
NORM_EPS = 1e-6
N_MIXERS = 3
N_LAYERS_A = (DEPTH + 2) // 3
N_LAYERS_B = (DEPTH + 1) // 3
N_LAYERS_C = DEPTH // 3

RW_HEAD = 64
RW_HEADS = D_MODEL // RW_HEAD
RW_WIDTH = RW_HEADS * RW_HEAD
RW_DECAY_LORA = 64
RW_AAA_LORA = 64
RW_GN_EPS = 64e-5
RW_WIDTHS = (RW_WIDTH, RW_WIDTH, RW_WIDTH, RW_WIDTH, RW_DECAY_LORA, RW_AAA_LORA)
RW_IN = 4 * RW_WIDTH + RW_DECAY_LORA + RW_AAA_LORA

SW_HEAD = 64
SW_Q_HEADS = D_MODEL // SW_HEAD
SW_KV_HEADS = 4
SW_GROUP = SW_Q_HEADS // SW_KV_HEADS
SW_WIDTH = SW_Q_HEADS * SW_HEAD
SW_KV_WIDTH = SW_KV_HEADS * SW_HEAD
SW_WINDOW = 128
SW_WINDOW_CHUNKS = SW_WINDOW // CHUNK
SW_IN = 2 * SW_WIDTH + 2 * SW_KV_WIDTH
ROPE_THETA = 500000.0
ROPE_DIM = SW_HEAD // 4

ML_HEADS = 4
ML_WIDTH = D_MODEL
ML_V_HEAD = ML_WIDTH // ML_HEADS
ML_QK_HEAD = ML_V_HEAD // 2
ML_CONV = 4
ML_GN_EPS = 1e-6
ML_IN = 3 * ML_WIDTH + 2 * ML_HEADS

kernel_name = 'hybrid_rwkv7_swa_sink_mlstm_encoder'

def _split(x, widths):
    out, start = [], 0
    for w in widths:
        out.append(x[..., start:start + w])
        start += w
    return out

def rms_norm(x, g):
    xf = x.astype(F32)
    y = xf * lax.rsqrt(jnp.mean(xf * xf, axis=-1, keepdims=True) + NORM_EPS)
    return (y * g.astype(F32)).astype(x.dtype)

def head_norm(h, g, b, eps):
    mu = jnp.mean(h, axis=-1, keepdims=True)
    var = jnp.mean(jnp.square(h - mu), axis=-1, keepdims=True)
    y = (h - mu) * lax.rsqrt(var + eps) * g.astype(F32)
    if b is not None:
        y = y + b.astype(F32)
    return y

def partial_rope(x, pos):
    half = ROPE_DIM // 2
    inv = jnp.power(jnp.asarray(ROPE_THETA, F32), -jnp.arange(half, dtype=F32) * (2.0 / ROPE_DIM))
    ang = pos.astype(F32)[:, None] * inv[None, :]
    cos = jnp.cos(ang)[None, :, None, :]
    sin = jnp.sin(ang)[None, :, None, :]
    x1, x2, rest = x[..., :half], x[..., half:ROPE_DIM], x[..., ROPE_DIM:]
    return jnp.concatenate([x1 * cos - x2 * sin, x2 * cos + x1 * sin, rest], axis=-1)

def rwkv7_mixer(h, w_in, mu, w0, w2, a0, a2, k_k, k_a, r_k, ln_g, ln_b, w_out):
    B, T, _ = h.shape
    dx = jnp.pad(h, ((0, 0), (1, 0), (0, 0)))[:, :-1] - h
    mu_cols = jnp.repeat(mu.T, np.array(RW_WIDTHS), axis=1, total_repeat_length=RW_IN)
    proj = h @ w_in + dx @ (w_in * mu_cols)
    r, k, v, g, w_lo, a_lo = _split(proj, RW_WIDTHS)
    w_log = -jax.nn.softplus(-(w0.astype(F32) + jnp.tanh(w_lo.astype(F32)) @ w2.astype(F32))) - 0.5
    decay = jnp.exp(-jnp.exp(w_log))
    a = jax.nn.sigmoid(a0.astype(F32) + a_lo.astype(F32) @ a2.astype(F32))
    to_heads = lambda t: t.astype(F32).reshape(B, T, RW_HEADS, RW_HEAD)
    r, k, v, decay, a = to_heads(r), to_heads(k), to_heads(v), to_heads(decay), to_heads(a)
    kk = k * k_k.astype(F32)
    kk = kk / jnp.maximum(jnp.sqrt(jnp.sum(kk * kk, axis=-1, keepdims=True)), 1e-12)
    k = k * (1.0 + (a - 1.0) * k_a.astype(F32))
    b_vec = kk * a

    def step(S, inp):
        r_t, w_t, k_t, v_t, kk_t, b_t = inp
        sa = jnp.einsum('bhvk,bhk->bhv', S, -kk_t)
        S = S * w_t[:, :, None, :] + sa[..., None] * b_t[:, :, None, :] + v_t[..., None] * k_t[:, :, None, :]
        return S, jnp.einsum('bhvk,bhk->bhv', S, r_t)

    xs = tuple(jnp.moveaxis(t, 1, 0) for t in (r, decay, k, v, kk, b_vec))
    S0 = jnp.zeros((B, RW_HEADS, RW_HEAD, RW_HEAD), F32)
    _, y = lax.scan(step, S0, xs)
    y = jnp.moveaxis(y, 0, 1)
    y = head_norm(y, ln_g, ln_b, RW_GN_EPS)
    y = y + jnp.sum(r * k * r_k.astype(F32), axis=-1, keepdims=True) * v
    y = y.reshape(B, T, RW_WIDTH) * jax.nn.silu(g.astype(F32))
    return y.astype(h.dtype) @ w_out

def swa_sink_mixer(h, w_in, sinks, w_out):
    B, T, _ = h.shape
    n_chunks = T // CHUNK
    proj = h @ w_in
    q, k, v, g = _split(proj, (SW_WIDTH, SW_KV_WIDTH, SW_KV_WIDTH, SW_WIDTH))
    pos = jnp.arange(T)
    q = partial_rope(q.astype(F32).reshape(B, T, SW_Q_HEADS, SW_HEAD), pos)
    k = partial_rope(k.astype(F32).reshape(B, T, SW_KV_HEADS, SW_HEAD), pos)
    v = v.astype(F32).reshape(B, T, SW_KV_HEADS, SW_HEAD)
    qc = q.reshape(B, n_chunks, CHUNK, SW_KV_HEADS, SW_GROUP, SW_HEAD)
    kc = k.reshape(B, n_chunks, CHUNK, SW_KV_HEADS, SW_HEAD)
    vc = v.reshape(B, n_chunks, CHUNK, SW_KV_HEADS, SW_HEAD)
    pad = SW_WINDOW_CHUNKS - 1
    kp = jnp.pad(kc, ((0, 0), (pad, 0), (0, 0), (0, 0), (0, 0)))
    vp = jnp.pad(vc, ((0, 0), (pad, 0), (0, 0), (0, 0), (0, 0)))
    kb = jnp.concatenate([kp[:, o:o + n_chunks] for o in range(SW_WINDOW_CHUNKS)], axis=2)
    vb = jnp.concatenate([vp[:, o:o + n_chunks] for o in range(SW_WINDOW_CHUNKS)], axis=2)
    key_chunk = jnp.arange(n_chunks)[:, None] - pad + (jnp.arange(SW_WINDOW_CHUNKS * CHUNK) // CHUNK)[None, :]
    valid = key_chunk >= 0
    s = jnp.einsum('bcqhgd,bckhd->bhgcqk', qc, kb) * (SW_HEAD ** -0.5)
    s = jnp.where(valid[:, None, :], s, -jnp.inf)
    sink = sinks.astype(F32).reshape(SW_KV_HEADS, SW_GROUP)[None, :, :, None, None, None]
    m = jnp.maximum(jnp.max(s, axis=-1, keepdims=True), sink)
    p = jnp.exp(s - m)
    p = p / (jnp.sum(p, axis=-1, keepdims=True) + jnp.exp(sink - m))
    o = jnp.einsum('bhgcqk,bckhd->bcqhgd', p, vb).reshape(B, T, SW_WIDTH)
    o = o * jax.nn.silu(g.astype(F32))
    return o.astype(h.dtype) @ w_out

def mlstm_chunkwise(q, k, v, log_i, log_f):
    B, T, H, dk = q.shape
    dv = v.shape[-1]
    n_chunks, L = T // CHUNK, CHUNK
    qc = q.reshape(B, n_chunks, L, H, dk)
    kc = k.reshape(B, n_chunks, L, H, dk)
    vc = v.reshape(B, n_chunks, L, H, dv)
    li = log_i.reshape(B, n_chunks, L, H)
    b = jnp.cumsum(log_f.reshape(B, n_chunks, L, H), axis=2)
    g = b[:, :, -1]
    w_end = g[:, :, None, :] - b + li
    m_loc = jnp.max(w_end, axis=2)
    e = jnp.exp(w_end - m_loc[:, :, None, :])
    dC = jnp.einsum('bcjh,bcjhk,bcjhv->bchkv', e, kc, vc)
    dn = jnp.einsum('bcjh,bcjhk->bchk', e, kc)

    def step(carry, inp):
        C, n, m = carry
        g_c, m_c, dC_c, dn_c = inp
        m_new = jnp.maximum(g_c + m, m_c)
        a_old = jnp.exp(g_c + m - m_new)
        a_new = jnp.exp(m_c - m_new)
        C_new = a_old[..., None, None] * C + a_new[..., None, None] * dC_c
        n_new = a_old[..., None] * n + a_new[..., None] * dn_c
        return (C_new, n_new, m_new), (C, n, m)

    init = (jnp.zeros((B, H, dk, dv), F32), jnp.zeros((B, H, dk), F32), jnp.zeros((B, H), F32))
    seq_in = tuple(jnp.moveaxis(t, 1, 0) for t in (g, m_loc, dC, dn))
    _, (C0, n0, m0) = lax.scan(step, init, seq_in)
    C0 = jnp.moveaxis(C0, 0, 1)
    n0 = jnp.moveaxis(n0, 0, 1)
    m0 = jnp.moveaxis(m0, 0, 1)
    causal = jnp.tril(jnp.ones((L, L), dtype=bool))
    D = b[:, :, :, None, :] - b[:, :, None, :, :] + li[:, :, None, :, :]
    D = jnp.where(causal[None, None, :, :, None], D, -jnp.inf)
    inter = b + m0[:, :, None, :]
    m_t = jnp.maximum(inter, jnp.max(D, axis=3))
    P = jnp.exp(D - m_t[:, :, :, None, :]) * jnp.einsum('bcthd,bcjhd->bctjh', qc, kc)
    s_inter = jnp.exp(inter - m_t)
    num = jnp.einsum('bctjh,bcjhv->bcthv', P, vc) + s_inter[..., None] * jnp.einsum('bcthk,bchkv->bcthv', qc, C0)
    den = jnp.sum(P, axis=3) + s_inter * jnp.einsum('bcthk,bchk->bcth', qc, n0)
    out = num / jnp.maximum(jnp.abs(den), jnp.exp(-m_t))[..., None]
    return out.reshape(B, T, H, dv)

def mlstm_mixer(h, w_in, conv_w, conv_b, w_q, w_k, i_bias, f_bias, gn_g, skip, w_out):
    B, T, _ = h.shape
    proj = h @ w_in
    u, v, z, i_pre, f_pre = _split(proj, (ML_WIDTH, ML_WIDTH, ML_WIDTH, ML_HEADS, ML_HEADS))
    c = lax.conv_general_dilated(u, conv_w[:, None, :], window_strides=(1,), padding=[(ML_CONV - 1, 0)],
                                 dimension_numbers=('NWC', 'WIO', 'NWC'), feature_group_count=ML_WIDTH)
    c = jax.nn.silu((c + conv_b).astype(F32))
    ch = c.reshape(B, T, ML_HEADS, ML_V_HEAD)
    q = jnp.einsum('bthe,hed->bthd', ch, w_q.astype(F32))
    k = jnp.einsum('bthe,hed->bthd', ch, w_k.astype(F32)) * (ML_QK_HEAD ** -0.5)
    v = v.astype(F32).reshape(B, T, ML_HEADS, ML_V_HEAD)
    log_i = i_pre.astype(F32) + i_bias.astype(F32)
    log_f = jax.nn.log_sigmoid(f_pre.astype(F32) + f_bias.astype(F32))
    hm = mlstm_chunkwise(q, k, v, log_i, log_f)
    hm = head_norm(hm, gn_g, None, ML_GN_EPS).reshape(B, T, ML_WIDTH)
    y = (hm + skip.astype(F32) * c) * jax.nn.silu(z.astype(F32))
    return y.astype(h.dtype) @ w_out

def _normal(key, shape, scale):
    return scale * jax.random.normal(key, shape, F32)

def setup_inputs(seed: int = 0) -> dict:
    key = jax.random.key(seed)
    ks = jax.random.split(key, 28)
    nA, nB, nC = N_LAYERS_A, N_LAYERS_B, N_LAYERS_C
    return {
        'x': _normal(ks[0], (BATCH, SEQ, D_MODEL), 1.0),
        'norm_g': 1.0 + _normal(ks[1], (DEPTH, D_MODEL), 0.02),
        'final_g': 1.0 + _normal(ks[2], (D_MODEL,), 0.02),
        'rw_w_in': _normal(ks[3], (nA, D_MODEL, RW_IN), D_MODEL ** -0.5),
        'rw_mu': jax.random.uniform(ks[4], (nA, len(RW_WIDTHS), D_MODEL), F32),
        'rw_w0': -4.0 + 3.0 * jax.random.uniform(ks[5], (nA, RW_WIDTH), F32),
        'rw_w2': _normal(ks[6], (nA, RW_DECAY_LORA, RW_WIDTH), 0.1),
        'rw_a0': _normal(ks[7], (nA, RW_WIDTH), 0.1),
        'rw_a2': _normal(ks[8], (nA, RW_AAA_LORA, RW_WIDTH), 0.1),
        'rw_k_k': 0.85 + _normal(ks[9], (nA, RW_HEADS, RW_HEAD), 0.05),
        'rw_k_a': 1.0 + _normal(ks[10], (nA, RW_HEADS, RW_HEAD), 0.05),
        'rw_r_k': _normal(ks[11], (nA, RW_HEADS, RW_HEAD), 0.1),
        'rw_ln_g': 1.0 + _normal(ks[12], (nA, RW_HEADS, RW_HEAD), 0.05),
        'rw_ln_b': _normal(ks[13], (nA, RW_HEADS, RW_HEAD), 0.02),
        'rw_w_out': _normal(ks[14], (nA, RW_WIDTH, D_MODEL), RW_WIDTH ** -0.5),
        'sw_w_in': _normal(ks[15], (nB, D_MODEL, SW_IN), D_MODEL ** -0.5),
        'sw_sinks': _normal(ks[16], (nB, SW_Q_HEADS), 1.0),
        'sw_w_out': _normal(ks[17], (nB, SW_WIDTH, D_MODEL), SW_WIDTH ** -0.5),
        'ml_w_in': _normal(ks[18], (nC, D_MODEL, ML_IN), D_MODEL ** -0.5),
        'ml_conv_w': _normal(ks[19], (nC, ML_CONV, ML_WIDTH), ML_CONV ** -0.5),
        'ml_conv_b': _normal(ks[20], (nC, ML_WIDTH), 0.02),
        'ml_w_q': _normal(ks[21], (nC, ML_HEADS, ML_V_HEAD, ML_QK_HEAD), ML_V_HEAD ** -0.5),
        'ml_w_k': _normal(ks[22], (nC, ML_HEADS, ML_V_HEAD, ML_QK_HEAD), ML_V_HEAD ** -0.5),
        'ml_i_bias': _normal(ks[23], (nC, ML_HEADS), 0.1),
        'ml_f_bias': 3.0 + 3.0 * jax.random.uniform(ks[24], (nC, ML_HEADS), F32),
        'ml_gn_g': 1.0 + _normal(ks[25], (nC, ML_HEADS, ML_V_HEAD), 0.05),
        'ml_skip': 1.0 + _normal(ks[26], (nC, ML_WIDTH), 0.05),
        'ml_w_out': _normal(ks[27], (nC, ML_WIDTH, D_MODEL), ML_WIDTH ** -0.5),
    }

def reference(x, norm_g, final_g, rw_w_in, rw_mu, rw_w0, rw_w2, rw_a0, rw_a2, rw_k_k, rw_k_a, rw_r_k,
              rw_ln_g, rw_ln_b, rw_w_out, sw_w_in, sw_sinks, sw_w_out, ml_w_in, ml_conv_w, ml_conv_b,
              ml_w_q, ml_w_k, ml_i_bias, ml_f_bias, ml_gn_g, ml_skip, ml_w_out):
    h = x
    for layer in range(DEPTH):
        kind, j = layer % N_MIXERS, layer // N_MIXERS
        hn = rms_norm(h, norm_g[layer])
        if kind == 0:
            y = rwkv7_mixer(hn, rw_w_in[j], rw_mu[j], rw_w0[j], rw_w2[j], rw_a0[j], rw_a2[j], rw_k_k[j],
                            rw_k_a[j], rw_r_k[j], rw_ln_g[j], rw_ln_b[j], rw_w_out[j])
        elif kind == 1:
            y = swa_sink_mixer(hn, sw_w_in[j], sw_sinks[j], sw_w_out[j])
        else:
            y = mlstm_mixer(hn, ml_w_in[j], ml_conv_w[j], ml_conv_b[j], ml_w_q[j], ml_w_k[j], ml_i_bias[j],
                            ml_f_bias[j], ml_gn_g[j], ml_skip[j], ml_w_out[j])
        h = h + y.astype(h.dtype)
    return rms_norm(h, final_g)


_drawn_inputs = setup_inputs


def setup_inputs(seed=0):
    import zlib

    import numpy as np

    out = dict(_drawn_inputs(seed))
    spreads = {}
    factors = {'final_g': 21.599,
     'rw_k_k': 7.776,
     'rw_ln_b': 3.406,
     'sw_sinks': 8.0,
     'ml_conv_b': 3.234,
     'ml_i_bias': 200.0,
     'ml_skip': 3.396,
     'ml_gn_g': 2.945}
    for name, (base, spread) in spreads.items():
        noise = np.random.default_rng([zlib.crc32(name.encode()), seed]).standard_normal(out[name].shape)
        drawn = base * np.exp(spread * noise) if base else spread * noise
        out[name] = __import__('jax').numpy.asarray(drawn.astype(out[name].dtype))
    for name, factor in factors.items():
        out[name] = (out[name] * factor).astype(out[name].dtype)
    return out
```

```python
import math
from contextlib import ExitStack

import numpy as np

import concourse.bass as bass
from concourse import mybir

F32 = mybir.dt.float32
ALU = mybir.AluOpType
ACT = mybir.ActivationFunctionType
AX = mybir.AxisListType

P = 128
T = 512
D = 1024
KT = D // P
NT = T // P
C = 64
NC = T // C
NH = 16
DECAY = math.exp(-0.5)
NEG = -1.0e30
SLOTS = 4

C_ID, C_BONES, C_GMASK, C_XMASK, C_TRI, C_ROPE = 0, 128, 256, 384, 448, 576
C_END = 640
RW_NORM, RW_MU, RW_W0, RW_A0, RW_KK, RW_KA, RW_RK, RW_LNG, RW_LNB = 0, 8, 56, 64, 72, 80, 88, 96, 104
SW_NORM, ML_NORM, ML_CW, ML_CB, ML_GN, ML_SKIP = 0, 8, 16, 48, 56, 64
MU_R, MU_K, MU_V, MU_G, MU_W, MU_A = (RW_MU + 8 * n for n in range(6))

A_H = 0
A_CONST = A_H + 4096
A_PT = A_CONST + C_END
A_SMALL = A_PT + 384
A_RING = A_SMALL + 96
A_BUF = A_RING + SLOTS * 1024
A_TMP = A_BUF + 7 * 4096
A_END = 53100
B_R, B_K, B_A, B_L, B_V, B_G, B_KK = (A_BUF + 4096 * n for n in range(7))
A_XT = A_TMP
A_DX = A_XT + KT * (T + 1)
A_T5 = A_DX + 4096


def constants():
    c = np.zeros((P, C_END), np.float32)
    r = np.arange(P)
    c[:, C_ID:C_ID + P] = np.eye(P)
    c[:, C_BONES:C_BONES + P] = (r[:, None] // C == r[None, :] // C)
    s, t = (r % C)[:, None], np.arange(C)[None, :]
    c[:, C_GMASK:C_GMASK + C] = t > s
    c[:, C_GMASK + C:C_GMASK + P] = t >= s
    c[:, C_XMASK:C_XMASK + C] = (s >= 32) & (t < 32)
    c[:, C_TRI:C_TRI + P] = np.where(r[None, :] >= r[:, None], 0.0, NEG)
    inv = np.power(np.float32(500000.0), -np.arange(8, dtype=np.float32) * np.float32(2.0 / 16))
    for a in range(NT):
        ang = (a * P + r).astype(np.float32)[:, None] * inv[None, :]
        c[:, C_ROPE + a * 8:C_ROPE + a * 8 + 8] = np.cos(ang)
        c[:, C_ROPE + 32 + a * 8:C_ROPE + 40 + a * 8] = np.sin(ang)
    return c


def more_constants():
    c = np.ones((P, 5 * T), np.float32)
    c[:, 0:T:C] = 0.0
    c[:, T:2 * T:P] = 0.0
    c[:, 2 * T:] = 0.0
    c[:, 2 * T:3 * T:P] = NEG
    for h in range(4):
        c[h, 3 * T + h * P:3 * T + (h + 1) * P] = 1.0
    return c


class Count:

    def __init__(self, handle):
        self.handle, self.base = handle, 0

    def at(self, n):
        return self.base + n


class Machine:

    def __init__(self, nc, ctx):
        self.nc = nc
        self.arena = ctx.enter_context(nc.sbuf_tensor("arena", [P, A_END], F32))
        self.bank = [ctx.enter_context(nc.psum_tensor(f"bank{n}", [P, 512], F32)) for n in range(8)]
        self.ctx = ctx
        self.sems = {}
        self.slot_full = [ctx.enter_context(nc.semaphore(f"slot{n}_full")) for n in range(SLOTS)]
        self.used_by = []
        self.weights = []
        self.issued = 0

    def sem(self, name):
        if name not in self.sems:
            self.sems[name] = Count(self.ctx.enter_context(self.nc.semaphore(name)))
        return self.sems[name]

    def view(self, at, *shape, rows=slice(0, P)):
        n = int(np.prod(shape))
        flat = self.arena[rows, at:at + n]
        if len(shape) == 1:
            return flat
        names = "abc"[:len(shape)]
        return flat.rearrange(f"p ({' '.join(names)}) -> p {' '.join(names)}",
                              **{k: v for k, v in zip(names[1:], shape[1:])})

    def slot(self, n):
        return A_RING + (n % SLOTS) * 1024

    def load_weights(self, eng, upto):
        for n in range(self.issued, min(upto, len(self.weights))):
            if n >= SLOTS:
                eng.wait_ge(*self.used_by[n - SLOTS])
            src, shape = self.weights[n]
            eng.dma_start(self.view(self.slot(n), *shape), src).then_inc(self.slot_full[n % SLOTS], 16)
        self.issued = max(self.issued, min(upto, len(self.weights)))

    def weights_arrived(self, pe, n):
        pe.wait_ge(self.slot_full[n % SLOTS], 16 * (n // SLOTS + 1))


def stage_load(m, x, consts, rw, sw_ml, w):
    nc = m.nc
    loaded, zeroed, turned, copied = m.sem("loaded"), m.sem("zeroed"), m.sem("turned"), m.sem("copied")
    stage = m.view(A_T5, 3, P)
    with nc.Block() as block:
        @block.sync
        def _(sp):
            sp.dma_start(m.view(A_CONST, C_END), consts).then_inc(loaded.handle, 16)
            sp.dma_start(m.view(A_H, NT, D), x.rearrange("o (a p) d -> p (o a) d", p=P)).then_inc(loaded.handle, 16)
            sp.wait_ge(zeroed.handle, 1)
            n = 2
            for s, rows in ((0, rw[0]), (2, rw[1]), (1, sw_ml)):
                for at, src in rows:
                    k = src.shape[0]
                    sp.dma_start(stage[at:at + k, s, :], src).then_inc(loaded.handle, 16)
                    n += 1
            loaded.total = 16 * n
            m.load_weights(sp, SLOTS)

        @block.vector
        def _(dve):
            nc.vector.memset(stage[:, :, :], 0.0).then_inc(zeroed.handle, 1)
            dve.wait_ge(turned.handle, 1)
            nc.vector.tensor_copy(m.view(A_PT, 384), m.bank[0][:, 0:384]).then_inc(copied.handle, 1)

        @block.tensor
        def _(pe):
            pe.wait_ge(loaded.handle, loaded.total)
            for s in range(3):
                last = nc.tensor.transpose(m.bank[0][:, s * P:(s + 1) * P], stage[:, s, :], m.view(A_CONST + C_ID, P))
            last.then_inc(turned.handle, 1)


def stage_norm(m, gcol, xn_at, out_at):
    nc = m.nc
    h = m.view(A_H, NT, D)
    xn = m.view(xn_at, NT, D)
    xt = m.view(out_at, KT, T + 1)
    ss = m.view(A_SMALL, NT)
    squared, root, inverse, scaled, turned, evac = (
        m.sem(n) for n in ("norm_squared", "norm_root", "norm_inverse", "norm_scaled", "norm_turned", "norm_evac"))
    with nc.Block() as block:
        @block.scalar
        def _(act):
            for a in range(NT):
                ins = nc.scalar.activation(xn[:, a, :], h[:, a, :], ACT.Square, accum_out=ss[:, a:a + 1])
            ins.then_inc(squared.handle, 1)
            act.wait_ge(inverse.handle, inverse.at(1))
            nc.scalar.activation(ss, ss, ACT.Sqrt).then_inc(root.handle, 1)

        @block.vector
        def _(dve):
            nc.vector.memset(xt[:, :, 0:1], 0.0)
            dve.wait_ge(squared.handle, squared.at(1))
            nc.vector.tensor_scalar(ss, ss, 1.0 / D, 1e-6, ALU.mult, ALU.add).then_inc(inverse.handle, 1)
            dve.wait_ge(root.handle, root.at(1))
            nc.vector.reciprocal(ss, ss).then_inc(inverse.handle, 1)
            dve.wait_ge(inverse.handle, inverse.at(2))
            for a in range(NT):
                nc.vector.tensor_scalar(xn[:, a, :], h[:, a, :], ss[:, a:a + 1], None, ALU.mult).then_inc(scaled.handle, 1)
            for k in range(KT):
                dve.wait_ge(turned.handle, turned.at(k + 1))
                nc.vector.tensor_scalar(xt[:, k, 1:T + 1], m.bank[k][:, :], m.view(A_PT + gcol + k, 1), None,
                                        ALU.mult)

        @block.tensor
        def _(pe):
            for k in range(KT):
                for a in range(NT):
                    if k == 0:
                        pe.wait_ge(scaled.handle, scaled.at(a + 1))
                    last = nc.tensor.transpose(m.bank[k][:, a * P:(a + 1) * P], xn[:, a, k * P:(k + 1) * P],
                                               m.view(A_CONST + C_ID, P))
                last.then_inc(turned.handle, 1)
    squared.base += 1
    root.base += 1
    inverse.base += 2
    scaled.base += NT
    turned.base += KT


def rw_project(m, prm, w2a2, reset_src, n0):
    nc = m.nc
    xt = m.view(A_XT, KT, T + 1)
    dx = m.view(A_DX, KT, T)
    R, K, A, L, V, G, KK = (m.view(b, KT, T) for b in (B_R, B_K, B_A, B_L, B_V, B_G, B_KK))
    lora = m.view(A_T5, T)
    sig = [m.view(A_T5 + 512 * (1 + n), T) for n in range(2)]
    sq = [m.view(A_T5 + 512 * (3 + n), T) for n in range(2)]
    rt = m.view(A_T5 + 512 * 5, T)
    reset = m.view(A_T5 + 512 * 6, T)
    w2a2_sb = m.view(B_R, D)
    omka = m.view(A_SMALL + 16, 8)
    bones = m.view(A_CONST + C_BONES, P)
    col = lambda at, k: m.view(prm + at + k, 1)
    tiles = [("lora", 0)]
    for j in range(KT):
        tiles += [("decay", j), ("a", j)]
    for j in range(KT + 1):
        tiles += [("k", j)] * (j < KT) + [("n2", j - 1)] * (j > 0)
    tiles += [(n, j) for n in ("r", "v", "g") for j in range(KT)]
    place = {t: n for n, t in enumerate(tiles)}
    dx_ready, mixed, pe_done, act_done, g_done, dve_kk, chain, act_chain, aux = (
        m.sem(n) for n in ("dx_ready", "mixed", "tile_done", "act_evacuated", "g_gated", "kk_squared",
                           "dve_chain", "act_chain", "aux_loaded"))
    root_used, sig_used = m.sem("root_used"), m.sem("sig_used")
    mixes = ["w", "a", "k", "r", "v", "g"]
    mix_at = {"w": G, "a": V, "k": G, "r": V, "v": G, "g": dx}
    mu_at = {"w": MU_W, "a": MU_A, "k": MU_K, "r": MU_R, "v": MU_V, "g": MU_G}
    ndve = [0]

    m.used_by += [(pe_done.handle, pe_done.at(place[t] + 1)) for t in tiles if t[0] not in ("decay", "a", "n2")]

    def freed(eng, n):
        if n >= 8:
            if tiles[n - 8][0] == "g":
                eng.wait_ge(g_done.handle, g_done.at(tiles[n - 8][1] + 1))
            else:
                eng.wait_ge(act_done.handle, act_done.at(n - 8 + 1))

    with nc.Block() as block:
        @block.sync
        def _(sp):
            sp.dma_start(w2a2_sb[0:64, :], w2a2[0]).then_inc(aux.handle, 16)
            sp.dma_start(w2a2_sb[64:128, :], w2a2[1]).then_inc(aux.handle, 16)
            sp.dma_start(reset, reset_src).then_inc(aux.handle, 16)
            m.load_weights(sp, n0 + 33)

        @block.vector
        def _(dve):
            def link(ins):
                ndve[0] += 1
                ins.then_inc(chain.handle, 1)
                dve.wait_ge(chain.handle, chain.at(ndve[0]))

            def mix(g):
                if g in "kr":
                    dve.wait_ge(pe_done.handle, pe_done.at(1))
                if g == "v":
                    dve.wait_ge(pe_done.handle, pe_done.at(place["k", 7] + 1))
                for k in range(KT):
                    nc.vector.scalar_tensor_tensor(out=mix_at[g][:, k, :], in0=dx[:, k, :], scalar=col(mu_at[g], k),
                                                   in1=xt[:, k, 1:T + 1], op0=ALU.mult, op1=ALU.add)\
                        .then_inc(mixed.handle, 1)

            link(nc.vector.tensor_tensor(dx, xt[:, :, 0:T], xt[:, :, 1:T + 1], ALU.subtract))
            link(nc.vector.tensor_scalar(omka, m.view(prm + RW_KA, 8), -1.0, 1.0, ALU.mult, ALU.add))
            mix("w")
            mix("a")
            mix("k")
            dve.wait_ge(aux.handle, aux.at(48))
            for j in range(KT):
                dve.wait_ge(act_done.handle, act_done.at(place["decay", j] + 1))
                nc.vector.tensor_tensor_scan(out=L[:, j, :], data0=reset, data1=sig[j % 2], initial=0.0,
                                             op0=ALU.mult, op1=ALU.add).then_inc(sig_used.handle, 1)
            mix("r")
            for j in range(KT + 1):
                if j < KT:
                    dve.wait_ge(act_done.handle, act_done.at(place["k", j] + 1))
                    link(nc.vector.tensor_scalar(KK[:, j, :], K[:, j, :], col(RW_KK, j), None, ALU.mult))
                    if j >= 2:
                        dve.wait_ge(pe_done.handle, pe_done.at(place["n2", j - 2] + 1))
                    nc.vector.tensor_tensor(sq[j % 2], KK[:, j, :], KK[:, j, :], ALU.mult).then_inc(dve_kk.handle, 1)
                if j > 0:
                    i = j - 1
                    dve.wait_ge(act_done.handle, act_done.at(place["n2", i] + 1))
                    link(nc.vector.tensor_scalar(rt, rt, 1e-12, None, ALU.max))
                    link(nc.vector.reciprocal(rt, rt))
                    nc.vector.tensor_tensor(KK[:, i, :], KK[:, i, :], rt, ALU.mult).then_inc(root_used.handle, 1)
            mix("v")
            mix("g")
            dve.wait_ge(root_used.handle, root_used.at(KT))
            for j in range(KT):
                link(nc.vector.tensor_scalar(sq[0], A[:, j, :], col(RW_KA, j), omka[:, j:j + 1], ALU.mult, ALU.add))
                nc.vector.tensor_tensor(K[:, j, :], K[:, j, :], sq[0], ALU.mult)
                link(nc.vector.tensor_tensor(A[:, j, :], A[:, j, :], KK[:, j, :], ALU.mult))
            for j in range(KT):
                dve.wait_ge(act_done.handle, act_done.at(place["g", j] + 1))
                nc.vector.tensor_tensor(G[:, j, :], m.bank[place["g", j] % 8][:, :], G[:, j, :], ALU.mult)\
                    .then_inc(g_done.handle, 1)

        @block.scalar
        def _(act):
            for n, (what, j) in enumerate(tiles):
                bank = m.bank[n % 8]
                act.wait_ge(pe_done.handle, pe_done.at(n + 1))
                if what == "lora":
                    nc.scalar.activation(lora[0:64, :], bank[0:64, :], ACT.Tanh).then_inc(act_chain.handle, 1)
                    out = nc.scalar.activation(lora[64:128, :], bank[64:128, :], ACT.Copy)
                    act.wait_ge(act_chain.handle, act_chain.at(1))
                elif what == "decay":
                    if j >= 2:
                        act.wait_ge(sig_used.handle, sig_used.at(j - 1))
                    out = nc.scalar.activation(sig[j % 2], bank[:, :], ACT.Sigmoid, bias=col(RW_W0, j))
                elif what == "a":
                    out = nc.scalar.activation(A[:, j, :], bank[:, :], ACT.Sigmoid, bias=col(RW_A0, j))
                elif what == "n2":
                    if j >= 1:
                        act.wait_ge(root_used.handle, root_used.at(j))
                    out = nc.scalar.activation(rt, bank[:, :], ACT.Sqrt)
                elif what == "g":
                    out = nc.scalar.activation(G[:, j, :], bank[:, :], ACT.Sigmoid)
                else:
                    out = nc.scalar.activation({"k": K, "r": R, "v": V}[what][:, j, :], bank[:, :], ACT.Copy)
                out.then_inc(act_done.handle, 1)

        @block.tensor
        def _(pe):
            w = n0
            for n, (what, j) in enumerate(tiles):
                bank = m.bank[n % 8]
                freed(pe, n)
                if what == "lora":
                    m.weights_arrived(pe, w)
                    slot = m.view(m.slot(w), KT, P)
                    pe.wait_ge(mixed.handle, mixed.at(2 * KT))
                    for k in range(KT):
                        nc.tensor.matmul(bank[0:64, :], slot[:, k, 0:64], mix_at["w"][:, k, :], start=k == 0, stop=k == KT - 1,
                                         skip_group_check=True)
                        last = nc.tensor.matmul(bank[64:128, :], slot[:, k, 64:128], mix_at["a"][:, k, :], start=k == 0,
                                                stop=k == KT - 1, skip_group_check=True)
                    w += 1
                elif what in ("decay", "a"):
                    if n == 1:
                        pe.wait_ge(act_done.handle, act_done.at(1))
                        pe.wait_ge(aux.handle, aux.at(48))
                    h = slice(0, 64) if what == "decay" else slice(64, 128)
                    last = nc.tensor.matmul(bank[:, :], w2a2_sb[h, j * P:(j + 1) * P], lora[h, :], start=True, stop=True)
                elif what == "n2":
                    pe.wait_ge(dve_kk.handle, dve_kk.at(j + 1))
                    last = nc.tensor.matmul(bank[:, :], bones, sq[j % 2], start=True, stop=True)
                else:
                    m.weights_arrived(pe, w)
                    slot = m.view(m.slot(w), KT, P)
                    for k in range(KT):
                        if j == 0:
                            pe.wait_ge(mixed.handle, mixed.at(KT * mixes.index(what) + k + 1))
                        last = nc.tensor.matmul(bank[:, :], slot[:, k, :], mix_at[what][:, k, :], start=k == 0,
                                                stop=k == KT - 1)
                    w += 1
                last.then_inc(pe_done.handle, 1)
    dx_ready.base += 0
    mixed.base += 6 * KT
    pe_done.base += len(tiles)
    act_done.base += len(tiles)
    g_done.base += KT
    dve_kk.base += KT
    chain.base += ndve[0]
    act_chain.base += 1
    aux.base += 48
    root_used.base += KT
    sig_used.base += KT


BC = 4
Q = 32
A_TU = A_RING
A_GS = A_TMP
A_S = A_GS + BC * 2048
A_AD = A_S + 512
A_STAGE = A_AD + 1024
A_ARZ = A_STAGE
A_BK = A_ARZ + 2048
A_EP = A_BK + 1024
A_EPI = A_EP + 8 * (C + 1)
A_A32 = A_STAGE
A_T32, A_TT, A_UU, A_PROD = (A_STAGE + 1024 * n for n in (1, 2, 3, 4))
A_Z = A_AD
A_VV = A_Z + 2048
A_XS = A_VV + 1024
A_US = A_XS + 512
A_RHS = A_US + 512
A_PC = A_SMALL + 24
LO, HI = slice(0, 64), slice(64, 128)


def wide(ap, n):
    return ap.unsqueeze(1).to_broadcast([ap.shape[0], n, ap.shape[1]])


def heads(buf, par):
    return buf.rearrange("p (k h) c -> p k h c", h=2)[:, :, par, :]


def rw_pairs(m, b):
    nc = m.nc
    R, K, BB, L, KK = (m.view(at, KT, T) for at in (B_R, B_K, B_A, B_L, B_KK))
    arz = m.view(A_ARZ, NH, P)
    gs = [m.view(A_GS + 2048 * i, NH, P) for i in range(BC)]
    bk = m.view(A_BK, KT, P)
    ep = m.view(A_EP, KT, C + 1)
    epi = m.view(A_EPI, KT, C)
    ad = m.view(A_AD, Q, BC * KT)
    ident, gmask = m.view(A_CONST + C_ID, P), m.view(A_CONST + C_GMASK, P)
    cleared, exp_ready, scaled, staged, b_scaled, k_scaled, b_staged = (m.sem(n) for n in (
        "cleared", "exp_ready", "ar_scaled", "ark_staged", "b_scaled", "k_scaled", "b_staged"))
    g_done, g_evac, bkt_done, bkt_evac = (m.sem(n) for n in ("g_done", "g_evac", "bkt_done", "bkt_evac"))
    span = lambda i: slice((BC * b + i) * C, (BC * b + i + 1) * C)

    with nc.Block() as block:
        @block.gpsimd
        def _(pool):
            nc.gpsimd.memset(ep[:, :, 0:1], 1.0).then_inc(cleared.handle, 1)
            for i in range(BC):
                t = span(i)
                pool.wait_ge(exp_ready.handle, exp_ready.at(i + 1))
                nc.gpsimd.tensor_tensor(BB[:, :, t], BB[:, :, t], epi, ALU.mult).then_inc(b_scaled.handle, 1)
                pool.wait_ge(scaled.handle, scaled.at(i + 1))
                nc.gpsimd.tensor_tensor(R[:, :, t], R[:, :, t], K[:, :, t], ALU.mult)
                nc.gpsimd.tensor_tensor(K[:, :, t], K[:, :, t], epi, ALU.mult).then_inc(k_scaled.handle, 1)

        @block.scalar
        def _(act):
            def exps(i):
                if i >= 1:
                    act.wait_ge(scaled.handle, scaled.at(i))
                    act.wait_ge(k_scaled.handle, k_scaled.at(i))
                nc.scalar.activation(ep[:, :, 1:C + 1], L[:, :, span(i)], ACT.Exp, scale=-DECAY)
                nc.scalar.activation(epi, L[:, :, span(i)], ACT.Exp, scale=DECAY).then_inc(exp_ready.handle, 1)

            def stage_b(i):
                act.wait_ge(b_scaled.handle, b_scaled.at(i + 1))
                if i >= 1:
                    act.wait_ge(bkt_done.handle, bkt_done.at(2 * i))
                nc.scalar.activation(bk[LO, :, 0:C], BB[LO, :, span(i)], ACT.Copy)
                nc.scalar.activation(bk[HI, :, C:P], BB[HI, :, span(i)], ACT.Copy).then_inc(b_staged.handle, 1)

            act.wait_ge(cleared.handle, cleared.at(1))
            exps(0)
            stage_b(0)
            for i in range(BC):
                if i + 1 < BC:
                    exps(i + 1)
                    stage_b(i + 1)
                for q in range(2):
                    act.wait_ge(bkt_done.handle, bkt_done.at(2 * i + q + 1))
                    bank = m.bank[4 + q][:, :].rearrange("p (k c) -> p k c", c=P)
                    nc.scalar.activation(BB[:, 4 * q:4 * q + 4, span(i)], bank[:, :, 0:C], ACT.Copy)
                    nc.scalar.activation(K[:, 4 * q:4 * q + 4, span(i)], bank[:, :, C:P], ACT.Copy)\
                        .then_inc(bkt_evac.handle, 1)
                act.wait_ge(g_evac.handle, g_evac.at(4 * i + 4))
                for g in range(4):
                    rows, half = slice(Q * g, Q * g + Q), g % 2
                    nc.scalar.activation(ad[rows, :, KT * i:KT * i + KT],
                                         heads(gs[i], g // 2)[rows, :, Q * half:Q * half + Q].rearrange("p k c -> p c k"),
                                         ACT.Copy)

        @block.vector
        def _(dve):
            def scale(i):
                dve.wait_ge(exp_ready.handle, exp_ready.at(i + 1))
                t = span(i)
                nc.vector.tensor_copy(m.view(A_PC + KT * i, KT).unsqueeze(2), ep[:, :, C:C + 1])
                nc.vector.tensor_tensor(KK[:, :, t], KK[:, :, t], ep[:, :, 0:C], ALU.mult)
                nc.vector.tensor_tensor(L[:, :, t], R[:, :, t], ep[:, :, 1:C + 1], ALU.mult).then_inc(scaled.handle, 1)

            def stage_ar(i):
                dve.wait_ge(scaled.handle, scaled.at(i + 1))
                for par, rows in ((0, LO), (1, HI)):
                    nc.vector.tensor_copy(heads(arz, par)[rows, :, 0:C], KK[rows, :, span(i)])
                    nc.vector.tensor_copy(heads(arz, par)[rows, :, C:P], L[rows, :, span(i)])

            def stage_k(i):
                dve.wait_ge(k_scaled.handle, k_scaled.at(i + 1))
                nc.vector.tensor_copy(bk[LO, :, C:P], K[LO, :, span(i)])
                nc.vector.tensor_copy(bk[HI, :, 0:C], K[HI, :, span(i)]).then_inc(staged.handle, 1)

            nc.vector.memset(heads(arz, 0)[HI], 0.0)
            nc.vector.memset(heads(arz, 1)[LO], 0.0)
            if b == 0:
                nc.vector.memset(m.view(A_S, 512), 0.0)
                nc.vector.memset(m.view(A_TU, BC * 1024), 0.0)
            dve.wait_ge(cleared.handle, cleared.at(1))
            scale(0)
            stage_ar(0)
            stage_k(0)
            for i in range(BC):
                if i + 1 < BC:
                    scale(i + 1)
                for q in range(4):
                    dve.wait_ge(g_done.handle, g_done.at(4 * i + q + 1))
                    if q == 3 and i + 1 < BC:
                        stage_ar(i + 1)
                    nc.vector.tensor_tensor(gs[i][:, 4 * q:4 * q + 4, :], m.bank[q][:, :].rearrange("p (k c) -> p k c", c=P),
                                            wide(gmask, 4), ALU.mult).then_inc(g_evac.handle, 1)
                if i + 1 < BC:
                    dve.wait_ge(bkt_done.handle, bkt_done.at(2 * i + 2))
                    stage_k(i + 1)

        @block.tensor
        def _(pe):
            for i in range(BC):
                pe.wait_ge(staged.handle, staged.at(i + 1))
                pe.wait_ge(b_staged.handle, b_staged.at(i + 1))
                for q in range(4):
                    if i >= 1:
                        pe.wait_ge(g_evac.handle, g_evac.at(4 * (i - 1) + q + 1))
                    for k in range(2):
                        last = nc.tensor.matmul(m.bank[q][:, 256 * k:256 * k + 256], bk[:, 2 * q + k, :],
                                                arz[:, 4 * q + 2 * k:4 * q + 2 * k + 2, :], start=True, stop=True,
                                                skip_group_check=True)
                    last.then_inc(g_done.handle, 1)
                for q in range(2):
                    if i >= 1:
                        pe.wait_ge(bkt_evac.handle, bkt_evac.at(2 * (i - 1) + q + 1))
                    for k in range(4):
                        last = nc.tensor.transpose(m.bank[4 + q][:, P * k:P * k + P], bk[:, 4 * q + k, :], ident)
                    last.then_inc(bkt_done.handle, 1)
    for s, n in ((cleared, 1), (exp_ready, BC), (scaled, BC), (staged, BC), (b_scaled, BC), (k_scaled, BC), (b_staged, BC),
                 (g_done, 4 * BC), (g_evac, 4 * BC), (bkt_done, 2 * BC), (bkt_evac, 2 * BC)):
        s.base += n


def rw_invert(m):
    nc = m.nc
    N = BC * KT
    ad, a32, t32, tt, uu = (m.view(at, Q, Q) for at in (A_AD, A_A32, A_T32, A_TT, A_UU))
    tu = m.view(A_TU, N, P)
    step, t_turned, u_turned = (m.sem(n) for n in ("inverse_step", "t_turned", "u_turned"))
    count = [0]
    with nc.Block() as block:
        @block.vector
        def _(dve):
            def link(ins):
                count[0] += 1
                ins.then_inc(step.handle, 1)
                dve.wait_ge(step.handle, step.at(count[0]))

            nc.vector.transpose(a32, ad)
            link(nc.vector.memset(t32, 0.0))
            link(nc.vector.memset(m.view(A_T32, Q * Q)[:, 0:Q * Q:Q + 1], 1.0))
            for s in range(Q - 1):
                n = Q - 1 - s
                prod = m.view(A_PROD, n, s + 1)
                link(nc.vector.tensor_tensor(prod, a32[:, s + 1:Q, s:s + 1].to_broadcast([P, n, s + 1]),
                                             wide(t32[:, s, 0:s + 1], n), ALU.mult))
                link(nc.vector.tensor_tensor(t32[:, s + 1:Q, 0:s + 1], t32[:, s + 1:Q, 0:s + 1], prod, ALU.subtract))
            nc.vector.transpose(tt, t32.rearrange("p t s -> p s t")).then_inc(t_turned.handle, 1)
            nc.vector.transpose(uu, t32).then_inc(u_turned.handle, 1)
            dve.wait_ge(u_turned.handle, u_turned.at(1))
            for g in (2, 3):
                rows, at = slice(Q * g, Q * g + Q), C + Q * (g % 2)
                nc.vector.tensor_copy(tu[rows, :, at:at + Q], uu[rows].rearrange("p c n -> p n c"))

        @block.scalar
        def _(act):
            act.wait_ge(t_turned.handle, t_turned.at(1))
            for g in range(4):
                rows, at = slice(Q * g, Q * g + Q), Q * (g % 2)
                nc.scalar.activation(tu[rows, :, at:at + Q], tt[rows].rearrange("p c n -> p n c"), ACT.Copy)
            act.wait_ge(u_turned.handle, u_turned.at(1))
            for g in (0, 1):
                rows, at = slice(Q * g, Q * g + Q), C + Q * (g % 2)
                nc.scalar.activation(tu[rows, :, at:at + Q], uu[rows].rearrange("p c n -> p n c"), ACT.Copy)
    step.base += count[0]
    t_turned.base += 1
    u_turned.base += 1


def rw_carry(m, b):
    nc = m.nc
    K, BB, L, V, KK = (m.view(at, KT, T) for at in (B_K, B_A, B_L, B_V, B_KK))
    gs = [m.view(A_GS + 2048 * i, NH, P) for i in range(BC)]
    tu = [m.view(A_TU + 1024 * i, KT, P) for i in range(BC)]
    z = [m.view(A_Z + 1024 * n, NH, C) for n in range(2)]
    vv = m.view(A_VV, KT, P)
    xs, us, rhs, S = (m.view(at, KT, C) for at in (A_XS, A_US, A_RHS, A_S))
    ident, xmask = m.view(A_CONST + C_ID, P), m.view(A_CONST + C_XMASK, C)
    z_cleared, vv_ready, v_done, v_evac, x_done, xs_ready, xu_done, us_ready, link = (m.sem(n) for n in (
        "z_cleared", "vv_ready", "v_done", "v_evac", "x_done", "xs_ready", "xu_done", "us_ready", "s_added"))
    rhs_done, rhs_evac, sa_done, sa_evac, y_done, y_evac, s_done, s_ready = (m.sem(n) for n in (
        "rhs_done", "rhs_evac", "sa_done", "sa_evac", "y_done", "y_evac", "s_done", "s_ready"))
    span = lambda i: slice((BC * b + i) * C, (BC * b + i + 1) * C)
    pairs = [slice(4 * g, 4 * g + 4) for g in range(2)]
    side = ((0, LO), (1, HI))
    quarter = lambda bank: bank[:, 0:256].rearrange("p (k c) -> p k c", c=C)

    with nc.Block() as block:
        @block.gpsimd
        def _(pool):
            nc.gpsimd.memset(vv[:, :, :], 0.0)
            nc.gpsimd.memset(m.view(A_Z, 2048), 0.0).then_inc(z_cleared.handle, 1)
            pool.wait_ge(z_cleared.handle, z_cleared.at(1))
            for i in range(BC):
                if i >= 1:
                    pool.wait_ge(v_done.handle, v_done.at(2 * i))
                nc.gpsimd.tensor_copy(vv[LO, :, C:P], V[LO, :, span(i)])
                nc.gpsimd.tensor_copy(vv[HI, :, 0:C], V[HI, :, span(i)]).then_inc(vv_ready.handle, 1)
                if i >= 2:
                    pool.wait_ge(s_done.handle, s_done.at(2 * (i - 1)))
                    nc.gpsimd.memset(heads(z[i % 2], 0)[LO], 0.0)
                    nc.gpsimd.memset(heads(z[i % 2], 1)[HI], 0.0).then_inc(z_cleared.handle, 1)

        @block.scalar
        def _(act):
            def values(i):
                if i >= 2:
                    act.wait_ge(s_done.handle, s_done.at(2 * (i - 1)))
                for q in range(2):
                    act.wait_ge(v_done.handle, v_done.at(2 * i + q + 1))
                    bank = m.bank[q][:, :].rearrange("p (k c) -> p k c", c=P)
                    nc.scalar.activation(heads(z[i % 2], 0)[HI, pairs[q], :], bank[HI, :, 0:C], ACT.Copy)
                    nc.scalar.activation(heads(z[i % 2], 1)[LO, pairs[q], :], bank[LO, :, C:P], ACT.Copy)\
                        .then_inc(v_evac.handle, 1)

            act.wait_ge(z_cleared.handle, z_cleared.at(1))
            values(0)
            for i in range(BC):
                for g in range(2):
                    act.wait_ge(rhs_done.handle, rhs_done.at(2 * i + g + 1))
                    nc.scalar.activation(rhs[:, pairs[g], :], quarter(m.bank[4 + g]), ACT.Copy, scale=-1.0)\
                        .then_inc(rhs_evac.handle, 1)
                if i + 1 < BC:
                    values(i + 1)
                for g in range(2):
                    act.wait_ge(sa_done.handle, sa_done.at(2 * i + g + 1))
                    nc.scalar.activation(heads(z[i % 2], 0)[LO, pairs[g], :], quarter(m.bank[6 + g])[LO], ACT.Copy)
                    nc.scalar.activation(heads(z[i % 2], 1)[HI, pairs[g], :], quarter(m.bank[6 + g])[HI], ACT.Copy)\
                        .then_inc(sa_evac.handle, 1)
                for g in range(2):
                    act.wait_ge(y_done.handle, y_done.at(2 * i + g + 1))
                    nc.scalar.activation(KK[:, pairs[g], span(i)], quarter(m.bank[4 + g]), ACT.Copy)\
                        .then_inc(y_evac.handle, 1)

        @block.vector
        def _(dve):
            def mask_x(i):
                for g in range(2):
                    dve.wait_ge(x_done.handle, x_done.at(2 * i + g + 1))
                    nc.vector.tensor_tensor(xs[:, pairs[g], :], quarter(m.bank[2 + g]), wide(xmask, 4), ALU.mult)\
                        .then_inc(xs_ready.handle, 1)

            def complete_u(i):
                for g in range(2):
                    dve.wait_ge(xu_done.handle, xu_done.at(2 * i + g + 1))
                    nc.vector.tensor_tensor(us[:, pairs[g], :], tu[i][:, pairs[g], C:P], quarter(m.bank[g]), ALU.subtract)\
                        .then_inc(us_ready.handle, 1)

            mask_x(0)
            complete_u(0)
            for i in range(BC):
                if i + 1 < BC:
                    mask_x(i + 1)
                for g in range(2):
                    dve.wait_ge(s_done.handle, s_done.at(2 * i + g + 1))
                    nc.vector.tensor_tensor(S[:, pairs[g], :], S[:, pairs[g], :], quarter(m.bank[6 + g]), ALU.add)\
                        .then_inc(link.handle, 1)
                    dve.wait_ge(link.handle, link.at(2 * i + g + 1))
                    pc = m.view(A_PC + KT * i, KT)[:, pairs[g]].unsqueeze(2).to_broadcast([P, 4, C])
                    nc.vector.tensor_tensor(S[:, pairs[g], :], S[:, pairs[g], :], pc, ALU.mult).then_inc(s_ready.handle, 1)
                if i + 1 < BC:
                    complete_u(i + 1)

        @block.tensor
        def _(pe):
            mm = lambda out, a, b, start=True, stop=True: nc.tensor.matmul(out, a, b, start=start, stop=stop,
                                                                          skip_group_check=True)

            def turn_values(i):
                pe.wait_ge(vv_ready.handle, vv_ready.at(i + 1))
                for q in range(2):
                    if i >= 1:
                        pe.wait_ge(us_ready.handle, us_ready.at(2 * (i - 1) + q + 1))
                    for k in range(4):
                        last = nc.tensor.transpose(m.bank[q][:, P * k:P * k + P], vv[:, 4 * q + k, :], ident)
                    last.then_inc(v_done.handle, 1)

            def x(i):
                for g in range(2):
                    if i >= 1:
                        pe.wait_ge(xs_ready.handle, xs_ready.at(2 * (i - 1) + g + 1))
                    for k in range(4):
                        for par, rows in side:
                            p = 4 * g + k
                            last = mm(m.bank[2 + g][rows, C * k:C * k + C], gs[i][rows, 2 * p + par, 0:C], tu[i][rows, p, 0:C])
                    last.then_inc(x_done.handle, 1)

            def xu(i):
                for g in range(2):
                    pe.wait_ge(xs_ready.handle, xs_ready.at(2 * i + g + 1))
                    pe.wait_ge(v_evac.handle, v_evac.at(2 * i + g + 1))
                    for k in range(4):
                        for par, rows in side:
                            p = 4 * g + k
                            last = mm(m.bank[g][rows, C * k:C * k + C], xs[rows, p, :], tu[i][rows, p, C:P])
                    last.then_inc(xu_done.handle, 1)

            turn_values(0)
            x(0)
            xu(0)
            for i in range(BC):
                t = span(i)
                if i >= 2:
                    pe.wait_ge(z_cleared.handle, z_cleared.at(i))
                for g in range(2):
                    pe.wait_ge(v_evac.handle, v_evac.at(2 * i + g + 1))
                    if i >= 1:
                        pe.wait_ge(s_ready.handle, s_ready.at(2 * (i - 1) + g + 1))
                        pe.wait_ge(y_evac.handle, y_evac.at(2 * (i - 1) + g + 1))
                    for k in range(4):
                        p = 4 * g + k
                        for par, rows in side:
                            mm(m.bank[4 + g][rows, C * k:C * k + C], KK[rows, p, t], S[rows, p, :], True, False)
                        for par, rows in side:
                            last = mm(m.bank[4 + g][rows, C * k:C * k + C], gs[i][:, 2 * p + par, 0:C],
                                      z[i % 2][:, 2 * p + par, :], False, True)
                    last.then_inc(rhs_done.handle, 1)
                if i + 1 < BC:
                    turn_values(i + 1)
                for g in range(2):
                    pe.wait_ge(rhs_evac.handle, rhs_evac.at(2 * i + g + 1))
                    pe.wait_ge(us_ready.handle, us_ready.at(2 * i + g + 1))
                    for k in range(4):
                        p = 4 * g + k
                        for par, rows in side:
                            last = mm(m.bank[6 + g][rows, C * k:C * k + C], us[rows, p, :], rhs[rows, p, :])
                    last.then_inc(sa_done.handle, 1)
                if i + 1 < BC:
                    x(i + 1)
                for g in range(2):
                    pe.wait_ge(sa_evac.handle, sa_evac.at(2 * i + g + 1))
                    for k in range(4):
                        p = 4 * g + k
                        for par, rows in side:
                            mm(m.bank[4 + g][rows, C * k:C * k + C], S[rows, p, :], L[rows, p, t], True, False)
                        for par, rows in side:
                            last = mm(m.bank[4 + g][rows, C * k:C * k + C], z[i % 2][:, 2 * p + par, :],
                                      gs[i][:, 2 * p + par, C:P], False, True)
                    last.then_inc(y_done.handle, 1)
                    for k in range(4):
                        p = 4 * g + k
                        for par, rows in side:
                            last = mm(m.bank[6 + g][rows, C * k:C * k + C], (BB, K)[par][:, p, t], z[i % 2][:, 2 * p + par, :])
                    last.then_inc(s_done.handle, 1)
                if i + 1 < BC:
                    xu(i + 1)
    vv_ready.base += BC
    z_cleared.base += BC - 1
    for s in (v_done, v_evac, x_done, xs_ready, xu_done, us_ready, link, rhs_done, rhs_evac, sa_done, sa_evac, y_done,
              y_evac, s_done, s_ready):
        s.base += 2 * BC


def rw_gate(m, prm, n0):
    nc = m.nc
    R, V, G, Y = (m.view(b, KT, T) for b in (B_R, B_V, B_G, B_KK))
    sq = m.view(B_A, KT, T)
    sd = m.view(B_L, KT, T)
    bones_rk = m.view(A_TMP, KT, P)
    bones = m.view(A_CONST + C_BONES, P)
    eps = m.view(A_SMALL + 40, 1)
    col = lambda at, k: m.view(prm + at + k, 1)
    tiles = [("mean", j) for j in range(KT)] + [(w, j) for j in range(KT) for w in ("var", "bonus")]
    place = {t: n for n, t in enumerate(tiles)}
    done, rr, centred, squared, root, gated, chain = (m.sem(n) for n in (
        "sums_done", "rr_ready", "centred", "squared", "root_ready", "bonus_used", "dve_chain"))
    count = [0]
    with nc.Block() as block:
        @block.sync
        def _(sp):
            m.load_weights(sp, n0 + SLOTS)

        @block.scalar
        def _(act):
            act.wait_ge(rr.handle, rr.at(1))
            for j in range(KT):
                act.wait_ge(centred.handle, centred.at(j + 1))
                nc.scalar.activation(sq[:, j, :], Y[:, j, :], ACT.Square).then_inc(squared.handle, 1)
            for j in range(KT):
                n = place["var", j]
                act.wait_ge(done.handle, done.at(n + 1))
                nc.scalar.activation(sd[:, j, :], m.bank[n % 8][:, :], ACT.Sqrt, bias=eps, scale=1.0 / C)\
                    .then_inc(root.handle, 1)

        @block.vector
        def _(dve):
            def link(ins):
                count[0] += 1
                ins.then_inc(chain.handle, 1)
                dve.wait_ge(chain.handle, chain.at(count[0]))

            nc.vector.memset(eps, 64e-5).then_inc(rr.handle, 1)
            for j in range(KT):
                dve.wait_ge(done.handle, done.at(j + 1))
                nc.vector.scalar_tensor_tensor(out=Y[:, j, :], in0=m.bank[j][:, :], scalar=-1.0 / C, in1=Y[:, j, :],
                                               op0=ALU.mult, op1=ALU.add).then_inc(centred.handle, 1)
            for j in range(KT):
                nc.vector.tensor_scalar(bones_rk[:, j, :], bones, col(RW_RK, j), None, ALU.mult).then_inc(rr.handle, 1)
            for j in range(KT):
                dve.wait_ge(root.handle, root.at(j + 1))
                link(nc.vector.reciprocal(sd[:, j, :], sd[:, j, :]))
                nc.vector.scalar_tensor_tensor(out=Y[:, j, :], in0=Y[:, j, :], scalar=col(RW_LNG, j), in1=sd[:, j, :],
                                               op0=ALU.mult, op1=ALU.mult)
                n = place["bonus", j]
                dve.wait_ge(done.handle, done.at(n + 1))
                ins = nc.vector.tensor_tensor(V[:, j, :], m.bank[n % 8][:, :], V[:, j, :], ALU.mult)
                ins.then_inc(gated.handle, 1)
                dve.wait_ge(gated.handle, gated.at(j + 1))
                link(nc.vector.scalar_tensor_tensor(out=Y[:, j, :], in0=Y[:, j, :], scalar=col(RW_LNB, j), in1=V[:, j, :],
                                                    op0=ALU.add, op1=ALU.add))
                nc.vector.tensor_tensor(Y[:, j, :], Y[:, j, :], G[:, j, :], ALU.mult)

        @block.tensor
        def _(pe):
            for n, (what, j) in enumerate(tiles):
                if what == "var":
                    pe.wait_ge(squared.handle, squared.at(j + 1))
                    if j >= 4:
                        pe.wait_ge(root.handle, root.at(j - 3))
                if what == "bonus":
                    pe.wait_ge(rr.handle, rr.at(j + 2))
                    if j >= 4:
                        pe.wait_ge(gated.handle, gated.at(j - 3))
                    else:
                        pe.wait_ge(centred.handle, centred.at(2 * j + 2))
                src = {"mean": Y, "var": sq, "bonus": R}[what][:, j, :]
                nc.tensor.matmul(m.bank[n % 8][:, :], bones_rk[:, j, :] if what == "bonus" else bones, src, start=True,
                                 stop=True).then_inc(done.handle, 1)
    for s, n in ((done, len(tiles)), (rr, KT + 1), (centred, KT), (squared, KT), (root, KT), (gated, KT), (chain, count[0])):
        s.base += n


def stage_out(m, y_at, n0):
    nc = m.nc
    Y = m.view(y_at, KT, T)
    h = m.view(A_H, NT, D)
    done, rows_used = m.sem("out_done"), m.sem("out_rows_used")
    m.used_by += [(rows_used.handle, rows_used.at(k + 1)) for k in range(KT - 1)] + [(done.handle, done.at(8))]
    with nc.Block() as block:
        @block.sync
        def _(sp):
            m.load_weights(sp, n0 + KT + SLOTS)

        @block.tensor
        def _(pe):
            for k in range(KT):
                m.weights_arrived(pe, n0 + k)
                slot = m.view(m.slot(n0 + k), D)
                for a in range(NT):
                    for half in range(2):
                        last = nc.tensor.matmul(m.bank[2 * a + half][:, :], Y[:, k, a * P:(a + 1) * P],
                                                slot[:, half * 512:half * 512 + 512], start=k == 0, stop=k == KT - 1)
                        if k == KT - 1:
                            last.then_inc(done.handle, 1)
                if k < KT - 1:
                    last.then_inc(rows_used.handle, 1)

        @block.vector
        def _(dve):
            for n in range(8):
                dve.wait_ge(done.handle, done.at(n + 1))
                part = h[:, n // 2, 512 * (n % 2):512 * (n % 2) + 512]
                nc.vector.tensor_tensor(part, part, m.bank[n][:, :], ALU.add)
    done.base += 8
    rows_used.base += KT - 1


def stage_store(m, final_g, out):
    nc = m.nc
    h = m.view(A_H, NT, D)
    tmp = m.view(B_R, NT, D)
    fg = m.view(B_K, D)
    ss = m.view(A_SMALL, NT)
    loaded, squared, root, inverse, ready, stored = (m.sem(n) for n in (
        "final_g_loaded", "norm_squared", "norm_root", "norm_inverse", "result_ready", "stored"))
    with nc.Block() as block:
        @block.scalar
        def _(act):
            for a in range(NT):
                ins = nc.scalar.activation(tmp[:, a, :], h[:, a, :], ACT.Square, accum_out=ss[:, a:a + 1])
            ins.then_inc(squared.handle, 1)
            act.wait_ge(inverse.handle, inverse.at(1))
            nc.scalar.activation(ss, ss, ACT.Sqrt).then_inc(root.handle, 1)

        @block.vector
        def _(dve):
            dve.wait_ge(squared.handle, squared.at(1))
            nc.vector.tensor_scalar(ss, ss, 1.0 / D, 1e-6, ALU.mult, ALU.add).then_inc(inverse.handle, 1)
            dve.wait_ge(root.handle, root.at(1))
            nc.vector.reciprocal(ss, ss).then_inc(inverse.handle, 1)
            dve.wait_ge(inverse.handle, inverse.at(2))
            dve.wait_ge(loaded.handle, loaded.at(16))
            for a in range(NT):
                nc.vector.scalar_tensor_tensor(out=h[:, a, :], in0=h[:, a, :], scalar=ss[:, a:a + 1], in1=fg,
                                               op0=ALU.mult, op1=ALU.mult).then_inc(ready.handle, 1)

        @block.sync
        def _(sp):
            sp.dma_start(fg, final_g.unsqueeze(0).to_broadcast([P, D])).then_inc(loaded.handle, 16)
            for a in range(NT):
                sp.wait_ge(ready.handle, ready.at(a + 1))
                sp.dma_start(out[0, a * P:(a + 1) * P, :], h[:, a, :]).then_inc(stored.handle, 16)
            sp.wait_ge(stored.handle, 16 * NT)


S_QKV = B_R
S_VS = S_QKV + 6144
S_QT = S_VS + 768
S_KT = S_QT + 4096
S_G = S_KT + 1024
S_Y = S_G + 4096
S_P = S_Y + 4096
S_PT = S_P + 2048
S_SK = S_PT + 1024
S_ROPE = S_SK + 64
SW_KV = 4


def sw_project(m, sinks, n0):
    nc = m.nc
    xt = m.view(A_XT, KT, T + 1)
    qkv = m.view(S_QKV, NT, 1536)
    vs = m.view(S_VS, 3, 256)
    qt, kt, G = m.view(S_QT, 8, T), m.view(S_KT, 2, T), m.view(S_G, KT, T)
    sk = m.view(S_SK, 8)
    rope = [m.view(S_ROPE + 160 * n, 20, 8) for n in range(4)]
    rtab = m.view(A_CONST + C_ROPE, 2, NT, 8)
    ident = m.view(A_CONST + C_ID, P)
    rows_used, q_done, qkv_evac, g_done, sig_done, g_used, turned, turn_evac, chain, sink, rotated = (m.sem(n) for n in (
        "sw_rows_used", "qkv_done", "qkv_evac", "tile_done", "act_evacuated", "g_gated", "qk_turned", "qk_evac",
        "dve_chain", "sinks_loaded", "rotated"))
    m.used_by += [(rows_used.handle, rows_used.at(k + 1)) for k in range(7)] + [(q_done.handle, q_done.at(8))]
    m.used_by += [(rows_used.handle, rows_used.at(7 + k + 1)) for k in range(3)] + [(q_done.handle, q_done.at(12))]
    m.used_by += [(g_done.handle, g_done.at(k + 1)) for k in range(KT)]
    count = [0]
    with nc.Block() as block:
        @block.sync
        def _(sp):
            sp.dma_start(sk[0:64, :], sinks[0:8].unsqueeze(0).to_broadcast([64, 8])).then_inc(sink.handle, 16)
            sp.dma_start(sk[64:128, :], sinks[8:16].unsqueeze(0).to_broadcast([64, 8])).then_inc(sink.handle, 16)
            m.load_weights(sp, n0 + 20 + SLOTS)

        @block.tensor
        def _(pe):
            w = n0
            for k in range(KT):
                m.weights_arrived(pe, w)
                slot = m.view(m.slot(w), D)
                for n in range(8):
                    last = nc.tensor.matmul(m.bank[n][:, :], xt[:, k, 1 + (n // 2) * P:1 + (n // 2 + 1) * P],
                                            slot[:, 512 * (n % 2):512 * (n % 2) + 512], start=k == 0, stop=k == KT - 1)
                    if k == KT - 1:
                        last.then_inc(q_done.handle, 1)
                if k < KT - 1:
                    last.then_inc(rows_used.handle, 1)
                w += 1
            for k2 in range(KT // 2):
                m.weights_arrived(pe, w)
                slot = m.view(m.slot(w), 2, 512)
                for n in range(NT):
                    if k2 == 0:
                        pe.wait_ge(qkv_evac.handle, qkv_evac.at(n + 1))
                    for k in range(2):
                        last = nc.tensor.matmul(m.bank[n][:, :], xt[:, 2 * k2 + k, 1 + n * P:1 + (n + 1) * P], slot[:, k, :],
                                                start=(k2, k) == (0, 0), stop=(k2, k) == (KT // 2 - 1, 1))
                    if k2 == KT // 2 - 1:
                        last.then_inc(q_done.handle, 1)
                if k2 < KT // 2 - 1:
                    last.then_inc(rows_used.handle, 1)
                w += 1
            for j in range(KT):
                m.weights_arrived(pe, w)
                slot = m.view(m.slot(w), KT, P)
                if j < 4:
                    pe.wait_ge(qkv_evac.handle, qkv_evac.at(4 + j + 1))
                else:
                    pe.wait_ge(g_used.handle, g_used.at(j - 3))
                for k in range(KT):
                    last = nc.tensor.matmul(m.bank[4 + j % 4][:, :], slot[:, k, :], xt[:, k, 1:T + 1], start=k == 0,
                                            stop=k == KT - 1)
                last.then_inc(g_done.handle, 1)
                w += 1
            for n in range(10):
                if n < 4:
                    pe.wait_ge(qkv_evac.handle, qkv_evac.at(12))
                    pe.wait_ge(rotated.handle, rotated.at(NT))
                else:
                    pe.wait_ge(turn_evac.handle, turn_evac.at(n - 3))
                for a in range(NT):
                    last = nc.tensor.transpose(m.bank[n % 4][:, a * P:(a + 1) * P], qkv[:, a, n * P:(n + 1) * P], ident)
                last.then_inc(turned.handle, 1)

        @block.scalar
        def _(act):
            for n in range(8):
                act.wait_ge(q_done.handle, q_done.at(n + 1))
                nc.scalar.activation(qkv[:, n // 2, 0:D].rearrange("p (h f c) -> p h f c", f=2, c=C)[:, :, n % 2, :],
                                     m.bank[n][:, :].rearrange("p (h c) -> p h c", c=C), ACT.Copy).then_inc(qkv_evac.handle, 1)
            for n in range(4):
                act.wait_ge(q_done.handle, q_done.at(8 + n + 1))
                for f in range(2):
                    nc.scalar.activation(qkv[:, n, D:D + 256].rearrange("p (h f c) -> p h f c", f=2, c=C)[:, :, f, :],
                                         m.bank[n][:, P * f:P * f + P].rearrange("p (h c) -> p h c", c=C), ACT.Copy)
                nc.scalar.activation(qkv[:, n, D + 256:D + 512], m.bank[n][:, 256:512], ACT.Copy).then_inc(qkv_evac.handle, 1)
            for j in range(KT):
                act.wait_ge(g_done.handle, g_done.at(j + 1))
                nc.scalar.activation(G[:, j, :], m.bank[4 + j % 4][:, :], ACT.Sigmoid).then_inc(sig_done.handle, 1)
            for n in range(10):
                act.wait_ge(turned.handle, turned.at(n + 1))
                nc.scalar.activation(qt[:, n, :] if n < 8 else kt[:, n - 8, :], m.bank[n % 4][:, :], ACT.Copy)\
                    .then_inc(turn_evac.handle, 1)

        @block.vector
        def _(dve):
            def link(ins):
                count[0] += 1
                ins.then_inc(chain.handle, 1)
                dve.wait_ge(chain.handle, chain.at(count[0]))

            for a in range(NT):
                dve.wait_ge(qkv_evac.handle, qkv_evac.at(8 + a + 1))
                qk = qkv[:, a, 0:1280].rearrange("p (h c) -> p h c", c=C)
                x1, x2 = qk[:, :, 0:8], qk[:, :, 8:16]
                cos, sin = (rtab[:, n, a, :].unsqueeze(1).to_broadcast([P, 20, 8]) for n in range(2))
                for n, (u, v) in enumerate(((x1, cos), (x2, sin), (x2, cos), (x1, sin))):
                    ins = nc.vector.tensor_tensor(rope[n], u, v, ALU.mult)
                link(ins)
                nc.vector.tensor_tensor(x1, rope[0], rope[1], ALU.subtract)
                nc.vector.tensor_tensor(x2, rope[2], rope[3], ALU.add).then_inc(rotated.handle, 1)
                dve.wait_ge(rotated.handle, rotated.at(a + 1))
            for i in range(3):
                nc.vector.tensor_copy(vs[0:64, i, :], qkv[64:128, i, 1280:1536])
                nc.vector.tensor_copy(vs[64:128, i, :], qkv[0:64, i + 1, 1280:1536])
            for j in range(KT):
                dve.wait_ge(sig_done.handle, sig_done.at(j + 1))
                nc.vector.tensor_tensor(G[:, j, :], m.bank[4 + j % 4][:, :], G[:, j, :], ALU.mult).then_inc(g_used.handle, 1)
    for s, n in ((rows_used, 10), (q_done, 12), (qkv_evac, 12), (g_done, KT), (sig_done, KT), (g_used, KT), (turned, 10),
                 (turn_evac, 10), (chain, count[0]), (sink, 32), (rotated, NT)):
        s.base += n


def sw_attend(m):
    nc = m.nc
    qkv = m.view(S_QKV, NT, 1536)
    vs = m.view(S_VS, 3, 256)
    qt, kt, G, Y = m.view(S_QT, 8, T), m.view(S_KT, 2, T), m.view(S_G, KT, T), m.view(S_Y, KT, T)
    prob = [m.view(S_P + 1024 * n, 8, P) for n in range(2)]
    pt = m.view(S_PT, 8, P)
    sk = m.view(S_SK, 8)
    small = [m.view(S_ROPE + 64 * n, 8, 8) for n in range(2)]
    ident = m.view(A_CONST + C_ID, P)
    s_done, s_max, s_exp, es_done, normed, p_turned, p_evac, o_done, o_evac, chain, sink = (m.sem(n) for n in (
        "scores_done", "score_max", "scores_exp", "sink_exp", "probs_normed", "probs_turned", "probs_evac", "o_done",
        "o_evac", "dve_chain", "sinks_loaded"))
    count = [0]
    keys = lambda c: C if c == 0 else P
    with nc.Block() as block:
        def gate(dve, c):
            dve.wait_ge(o_done.handle, o_done.at(c + 1))
            nc.vector.tensor_tensor(Y[:, :, c * C:(c + 1) * C], m.bank[6 + c % 2][:, :].rearrange("p (k t) -> p k t", t=C),
                                    G[:, :, c * C:(c + 1) * C], ALU.mult).then_inc(o_evac.handle, 1)

        def evac(act, c):
            for q in range(2):
                act.wait_ge(p_turned.handle, p_turned.at(2 * c + q + 1))
                if q == 0 and c >= 1:
                    act.wait_ge(o_done.handle, o_done.at(c))
                nc.scalar.activation(pt[0:keys(c), 4 * q:4 * q + 4, :], m.bank[4 + q][0:keys(c), :], ACT.Copy)\
                    .then_inc(p_evac.handle, 1)

        @block.tensor
        def _(pe):
            def scores(c):
                if c >= 2:
                    pe.wait_ge(s_exp.handle, s_exp.at(c - 1))
                for h in range(8):
                    bank = m.bank[2 * (c % 2) + h // 4]
                    for f, rows in ((0, slice(0, 64)), (1, slice(64, 128))):
                        last = nc.tensor.matmul(bank[rows, P * (h % 4):P * (h % 4) + keys(c)], qt[rows, h, c * C:(c + 1) * C],
                                                kt[rows, h // 4, (c + 1) * C - keys(c):(c + 1) * C], start=True, stop=True,
                                                skip_group_check=True)
                last.then_inc(s_done.handle, 1)

            scores(0)
            for c in range(NC):
                if c + 1 < NC:
                    scores(c + 1)
                pe.wait_ge(normed.handle, normed.at(c + 1))
                for q in range(2):
                    if c >= 1:
                        pe.wait_ge(p_evac.handle, p_evac.at(2 * c - 1 + q))
                    for k in range(4):
                        last = nc.tensor.transpose(m.bank[4 + q][0:keys(c), P * k:P * k + P], prob[c % 2][:, 4 * q + k, 0:keys(c)],
                                                   ident)
                    last.then_inc(p_turned.handle, 1)
                if c >= 2:
                    pe.wait_ge(o_evac.handle, o_evac.at(c - 1))
                v = qkv[:, c // 2, 1280:1536] if c % 2 or c == 0 else vs[:, c // 2 - 1, :]
                pe.wait_ge(p_evac.handle, p_evac.at(2 * c + 2))
                for h in range(8):
                    for f in range(2):
                        out = slice(64 * (h % 2), 64 * (h % 2) + 64)
                        kv = h // 4 + 2 * f
                        at = C * (h // 2 + 4 * f)
                        last = nc.tensor.matmul(m.bank[6 + c % 2][out, at:at + C], v[0:keys(c), C * kv:C * kv + C],
                                                pt[0:keys(c), h, C * f:C * f + C], start=True, stop=True, skip_group_check=True)
                last.then_inc(o_done.handle, 1)

        @block.scalar
        def _(act):
            for c in range(NC):
                p, st = prob[c % 2], small[c % 2]
                act.wait_ge(s_max.handle, s_max.at(c + 1))
                if c >= 2:
                    act.wait_ge(p_turned.handle, p_turned.at(2 * (c - 1)))
                nc.scalar.activation(st[:, 2, :], st[:, 1, :], ACT.Exp)
                for h in range(8):
                    bank = m.bank[2 * (c % 2) + h // 4]
                    last = nc.scalar.activation(p[:, h, 0:keys(c)], bank[:, P * (h % 4):P * (h % 4) + keys(c)], ACT.Exp,
                                                bias=st[:, 0, h:h + 1], scale=C ** -0.5, accum_out=st[:, 3, h:h + 1])
                last.then_inc(s_exp.handle, 1)
                if c >= 1:
                    evac(act, c - 1)
            evac(act, NC - 1)


        @block.vector
        def _(dve):
            def link(ins):
                count[0] += 1
                ins.then_inc(chain.handle, 1)
                dve.wait_ge(chain.handle, chain.at(count[0]))

            def maxima(c):
                st = small[c % 2]
                dve.wait_ge(s_done.handle, s_done.at(c + 1))
                for q in range(2):
                    bank = m.bank[2 * (c % 2) + q][:, :].rearrange("p (h k) -> p h k", k=P)[:, :, 0:keys(c)]
                    ins = nc.vector.tensor_reduce(st[:, 0, 4 * q:4 * q + 4], bank, AX.X, ALU.max)
                link(ins)
                link(nc.vector.tensor_scalar(st[:, 0, :], st[:, 0, :], C ** -0.5, None, ALU.mult))
                link(nc.vector.tensor_tensor(st[:, 0, :], st[:, 0, :], sk, ALU.max))
                link(nc.vector.tensor_tensor(st[:, 1, :], sk, st[:, 0, :], ALU.subtract))
                nc.vector.tensor_scalar(st[:, 0, :], st[:, 0, :], -1.0, None, ALU.mult).then_inc(s_max.handle, 1)

            dve.wait_ge(sink.handle, sink.at(0))
            maxima(0)
            for c in range(NC):
                st, p = small[c % 2], prob[c % 2]
                if c + 1 < NC:
                    maxima(c + 1)
                dve.wait_ge(s_exp.handle, s_exp.at(c + 1))
                link(nc.vector.tensor_tensor(st[:, 3, :], st[:, 3, :], st[:, 2, :], ALU.add))
                link(nc.vector.reciprocal(st[:, 3, :], st[:, 3, :]))
                nc.vector.tensor_tensor(p[:, :, 0:keys(c)], p[:, :, 0:keys(c)], st[:, 3, :].unsqueeze(2).to_broadcast([P, 8, keys(c)]),
                                        ALU.mult).then_inc(normed.handle, 1)
                if c >= 1:
                    gate(dve, c - 1)
            gate(dve, NC - 1)

    for s, n in ((s_done, NC), (s_max, NC), (s_exp, NC), (normed, NC), (p_turned, 2 * NC), (p_evac, 2 * NC), (o_done, NC),
                 (o_evac, NC), (chain, count[0])):
        s.base += n


ML_H, ML_V = 4, 256
M_U = B_R
M_C = M_U + KT * (T + 3)
M_Z = M_C + 4096
M_V = M_Z + 4096
M_HM = M_V + NT * ML_H * (ML_V + 1)
M_Q = M_HM + 4096
M_K = M_Q + 2048
M_QS = M_K + 2048
M_E = M_QS + 2048
M_SI = M_E + 2048
M_KTOK = M_SI + 2048
M_STATE = M_KTOK + 2048
M_SM = M_STATE + ML_H * (ML_V + 1)
M_XT = A_END - KT * (T + 1)
M_ROWS = M_HM
M_Y = M_U


def ml_project(m, w_if, i_bias, f_bias, rows_src, n0):
    nc = m.nc
    xt = m.view(M_XT, KT, T + 1)
    U = m.view(M_U, KT, T + 3)
    cc, Z = m.view(M_C, KT, T), m.view(M_Z, KT, T)
    V = m.view(M_V, NT * ML_H, ML_V + 1)
    q, k = m.view(M_Q, ML_H, T), m.view(M_K, ML_H, T)
    tmp = m.view(M_E, T)
    sig = [m.view(M_SI + 512 * n, T) for n in range(2)]
    gw = m.view(M_ROWS, KT, 8)
    gates = m.view(M_SM, NT, 8)
    bias = m.view(M_SM + 32, 2, rows=slice(0, 4))
    consts = m.view(M_ROWS + 64, 3, T, rows=slice(0, 4))
    gi = m.view(M_ROWS + 64 + 3 * T, 2, T, rows=slice(0, 4))
    ident = m.view(A_CONST + C_ID, P)
    prm = A_PT + 128
    col = lambda at, j: m.view(prm + at + j, 1)
    done, act_done, z_used, conv_done, sig_ready, rows_used, aux, v_done, chain, c_ready, sig_free = (m.sem(n) for n in (
        "tile_done", "act_evacuated", "g_gated", "conv_done", "sig_ready", "out_rows_used", "aux_loaded", "v_rows_done",
        "dve_chain", "c_ready", "sig_used"))
    v_evac = m.sem("v_rows_evac")
    tiles = [("gates", 0), ("gates_t", 0)] + [("u", j) for j in range(KT)] + [("z", j) for j in range(KT)]
    tiles += [(w, h) for w in "qk" for h in range(ML_H)]
    place = {t: n for n, t in enumerate(tiles)}
    m.used_by += [(done.handle, done.at(place["u", j] + 1)) for j in range(KT)]
    m.used_by += [(done.handle, done.at(place["z", j] + 1)) for j in range(KT)]
    m.used_by += [(done.handle, done.at(place[w, 3] + 1)) for w in "qk"]
    m.used_by += [(rows_used.handle, rows_used.at(n + 1)) for n in range(7)] + [(v_done.handle, v_done.at(8))]
    count = [0]
    with nc.Block() as block:
        def conv_sig(act, j):
            act.wait_ge(conv_done.handle, conv_done.at(j + 1))
            if j >= 2:
                act.wait_ge(c_ready.handle, c_ready.at(j - 1))
            nc.scalar.activation(sig[j % 2], cc[:, j, :], ACT.Sigmoid, bias=col(ML_CB, j)).then_inc(sig_ready.handle, 1)

        @block.sync
        def _(sp):
            with nc.allow_non_contiguous_dma(reason="eight columns of gate weights, four biases"):
                sp.dma_start(gw, w_if.rearrange("(k p) n -> p k n", p=P)).then_inc(aux.handle, 16)
                sp.dma_start(bias[:, 0:1], i_bias.unsqueeze(1)).then_inc(aux.handle, 16)
                sp.dma_start(bias[:, 1:2], f_bias.unsqueeze(1)).then_inc(aux.handle, 16)
            sp.dma_start(consts, rows_src).then_inc(aux.handle, 16)
            m.load_weights(sp, n0 + 26 + SLOTS)

        @block.tensor
        def _(pe):
            w = n0
            pe.wait_ge(aux.handle, aux.at(64))
            for n, (what, j) in enumerate(tiles):
                bank = m.bank[n % 8]
                if n >= 8:
                    before = tiles[n - 8]
                    if before[0] == "z":
                        pe.wait_ge(z_used.handle, z_used.at(before[1] + 1))
                    else:
                        pe.wait_ge(act_done.handle, act_done.at(n - 7))
                if what == "gates":
                    for a in range(NT):
                        for c in range(KT):
                            last = nc.tensor.matmul(bank[:, 8 * a:8 * a + 8], xt[:, c, 1 + a * P:1 + (a + 1) * P], gw[:, c, :],
                                                    start=c == 0, stop=c == KT - 1)
                elif what == "gates_t":
                    pe.wait_ge(act_done.handle, act_done.at(1))
                    for f in range(2):
                        for a in range(NT):
                            last = nc.tensor.transpose((bank if f == 0 else m.bank[7])[0:4, a * P:(a + 1) * P],
                                                       gates[:, a, 4 * f:4 * f + 4], ident)
                elif what in "uz":
                    if (what, j) == ("u", 5):
                        pe.wait_ge(act_done.handle, act_done.at(2))
                    m.weights_arrived(pe, w)
                    slot = m.view(m.slot(w), KT, P)
                    for c in range(KT):
                        last = nc.tensor.matmul(bank[:, :], slot[:, c, :], xt[:, c, 1:T + 1], start=c == 0, stop=c == KT - 1)
                    w += 1
                else:
                    if j == 0:
                        m.weights_arrived(pe, w)
                        slot = m.view(m.slot(w), KT, P)
                        w += 1
                    pe.wait_ge(c_ready.handle, c_ready.at(KT))
                    for e in range(2):
                        last = nc.tensor.matmul(bank[:, :], slot[:, 2 * j + e, :], cc[:, 2 * j + e, :], start=e == 0, stop=e == 1)
                last.then_inc(done.handle, 1)
            pe.wait_ge(act_done.handle, act_done.at(len(tiles)))
            pe.wait_ge(z_used.handle, z_used.at(KT))
            for c in range(KT):
                m.weights_arrived(pe, w)
                slot = m.view(m.slot(w), D)
                for n in range(8):
                    last = nc.tensor.matmul(m.bank[n][:, :], xt[:, c, 1 + (n // 2) * P:1 + (n // 2 + 1) * P],
                                            slot[:, 512 * (n % 2):512 * (n % 2) + 512], start=c == 0, stop=c == KT - 1)
                    if c == KT - 1:
                        last.then_inc(v_done.handle, 1)
                if c < KT - 1:
                    last.then_inc(rows_used.handle, 1)
                w += 1

        @block.scalar
        def _(act):
            for n, (what, j) in enumerate(tiles):
                bank = m.bank[n % 8]
                act.wait_ge(done.handle, done.at(n + 1))
                if what == "gates":
                    out = nc.scalar.activation(m.view(M_SM, 32), bank[:, 0:32], ACT.Copy)
                elif what == "gates_t":
                    act.wait_ge(aux.handle, aux.at(64))
                    nc.scalar.activation(gi[:, 0, :], bank[0:4, :], ACT.Identity, bias=bias[:, 0:1])
                    out = nc.scalar.activation(gi[:, 1, :], m.bank[7][0:4, :], ACT.Identity, bias=bias[:, 1:2])
                elif what == "u":
                    out = nc.scalar.activation(U[:, j, 3:T + 3], bank[:, :], ACT.Copy)
                elif what == "z":
                    if j >= 1:
                        conv_sig(act, j - 1)
                    out = nc.scalar.activation(Z[:, j, :], bank[:, :], ACT.Sigmoid)
                elif what == "q":
                    out = nc.scalar.activation(q[:, j, :], bank[:, :], ACT.Copy)
                else:
                    out = nc.scalar.activation(k[:, j, :], bank[:, :], ACT.Copy, scale=P ** -0.5)
                out.then_inc(act_done.handle, 1)
                if (what, j) == ("z", KT - 1):
                    conv_sig(act, KT - 1)
            for n in range(8):
                act.wait_ge(v_done.handle, v_done.at(n + 1))
                nc.scalar.activation(V[:, 2 * n:2 * n + 2, 0:ML_V], m.bank[n][:, :].rearrange("p (h c) -> p h c", h=2), ACT.Copy)


        @block.vector
        def _(dve):
            def link(ins):
                count[0] += 1
                ins.then_inc(chain.handle, 1)
                dve.wait_ge(chain.handle, chain.at(count[0]))

            nc.vector.memset(V[:, :, ML_V:ML_V + 1], 1.0)
            link(nc.vector.memset(U[:, :, 0:3], 0.0))

            def gate(j):
                dve.wait_ge(sig_ready.handle, sig_ready.at(j + 1))
                nc.vector.scalar_tensor_tensor(out=cc[:, j, :], in0=cc[:, j, :], scalar=col(ML_CB, j), in1=sig[j % 2],
                                               op0=ALU.add, op1=ALU.mult).then_inc(c_ready.handle, 1)

            def z_gate(j):
                n = place["z", j]
                dve.wait_ge(act_done.handle, act_done.at(n + 1))
                nc.vector.tensor_tensor(Z[:, j, :], m.bank[n % 8][:, :], Z[:, j, :], ALU.mult).then_inc(z_used.handle, 1)

            for j in range(KT):
                dve.wait_ge(act_done.handle, act_done.at(place["u", j] + 1))
                link(nc.vector.tensor_scalar(cc[:, j, :], U[:, j, 0:T], col(ML_CW, j), None, ALU.mult))
                for i in range(1, 4):
                    ins = nc.vector.scalar_tensor_tensor(out=cc[:, j, :], in0=U[:, j, i:i + T], scalar=col(ML_CW + 8 * i, j),
                                                         in1=cc[:, j, :], op0=ALU.mult, op1=ALU.add)
                    if i < 3:
                        link(ins)
                ins.then_inc(conv_done.handle, 1)
            for j in range(KT):
                z_gate(j)
                gate(j)
    for s, n in ((done, len(tiles)), (act_done, len(tiles)), (z_used, KT), (conv_done, KT), (sig_ready, KT), (rows_used, 7),
                 (aux, 64), (v_done, 8), (chain, count[0]), (c_ready, KT)):
        s.base += n


def ml_gates(m):
    nc = m.nc
    one = slice(0, 4)
    consts = m.view(M_ROWS + 64, 3, T, rows=one)
    at = M_ROWS + 64 + 3 * T
    li, lf, b, mx = (m.view(at + n * T, T, rows=one) for n in range(4))
    sel = consts[:, 2, :].rearrange("p (h n) -> p h n", n=P)
    small = m.view(M_SM + 40, 20, rows=one)
    m0 = small[:, 0:5]
    E, SI = m.view(M_E, ML_H, T), m.view(M_SI, ML_H, T)
    q, qs = m.view(M_Q, ML_H, T), m.view(M_QS, ML_H, T)
    cols = m.view(M_SM, NT, 8)
    tri = m.view(A_CONST + C_TRI, P)
    ident = m.view(A_CONST + C_ID, P)
    chain, ready, act_ready, turned, spread, evac, expd = (m.sem(n) for n in (
        "dve_chain", "gates_ready", "gates_act", "gates_turned", "gates_spread", "gates_evac", "gates_exp"))
    last_of = lambda x: x.rearrange("p (c t) -> p c t", t=P)[:, :, P - 1]
    count = [0]
    with nc.Block() as block:
        @block.vector
        def _(dve):
            def link(ins):
                count[0] += 1
                ins.then_inc(chain.handle, 1)
                dve.wait_ge(chain.handle, chain.at(count[0]))

            nc.vector.scalar_tensor_tensor(out=b, in0=lf, scalar=-1.0, in1=lf, op0=ALU.mult, op1=ALU.max).then_inc(ready.handle, 1)
            link(nc.vector.tensor_scalar(lf, lf, 0.0, None, ALU.min))
            dve.wait_ge(act_ready.handle, act_ready.at(2))
            link(nc.vector.tensor_tensor(lf, lf, mx, ALU.subtract))
            link(nc.vector.tensor_tensor_scan(out=b, data0=consts[:, 0, :], data1=lf, initial=0.0, op0=ALU.mult, op1=ALU.add))
            link(nc.vector.tensor_tensor(li, li, b, ALU.subtract))
            link(nc.vector.tensor_tensor_scan(out=mx, data0=consts[:, 1, :], data1=li, initial=NEG, op0=ALU.add, op1=ALU.max))
            link(nc.vector.memset(m0[:, 0:1], 0.0))
            link(nc.vector.tensor_copy(small[:, 5:9], last_of(mx)))
            link(nc.vector.tensor_copy(small[:, 9:13], last_of(b)))
            link(nc.vector.tensor_tensor_scan(out=m0[:, 1:5], data0=small[:, 5:9], data1=small[:, 9:13], initial=0.0,
                                              op0=ALU.max, op1=ALU.add))
            mxc, lfc = (x.rearrange("p (c t) -> p c t", t=P) for x in (mx, lf))
            m0w = m0[:, 0:4].unsqueeze(2).to_broadcast([4, NT, P])
            link(nc.vector.tensor_tensor(mxc, mxc, m0w, ALU.max))
            link(nc.vector.tensor_tensor(lfc, m0w, mxc, ALU.subtract))
            link(nc.vector.scalar_tensor_tensor(out=b, in0=b, scalar=-1.0, in1=mx, op0=ALU.mult, op1=ALU.subtract))
            nc.vector.tensor_scalar(mx, mx, -1.0, None, ALU.mult).then_inc(ready.handle, 1)
            for h in range(ML_H):
                dve.wait_ge(spread.handle, spread.at(h + 1))
                nc.vector.tensor_tensor(E[:, h, :].rearrange("p (c t) -> p c t", t=P),
                                        m.bank[1 + h][:, :].rearrange("p (c t) -> p c t", t=P),
                                        tri.unsqueeze(1).to_broadcast([P, NT, P]), ALU.add).then_inc(evac.handle, 1)
            for h in range(ML_H):
                dve.wait_ge(expd.handle, expd.at(h + 1))
                nc.vector.tensor_tensor(qs[:, h, :], q[:, h, :], SI[:, h, :], ALU.mult)

        @block.scalar
        def _(act):
            act.wait_ge(ready.handle, ready.at(1))
            nc.scalar.activation(mx, b, ACT.Exp, scale=-1.0).then_inc(act_ready.handle, 1)
            act.wait_ge(act_ready.handle, act_ready.at(1))
            nc.scalar.activation(mx, mx, ACT.Ln, bias=1.0).then_inc(act_ready.handle, 1)
            act.wait_ge(turned.handle, turned.at(1))
            bank = m.bank[0][:, 0:32].rearrange("p (c n) -> p c n", n=8)
            nc.scalar.activation(cols[:, :, 0:4], bank[:, :, 0:4], ACT.Copy).then_inc(act_ready.handle, 1)
            nc.scalar.activation(cols[:, :, 4:8], bank[:, :, 4:8], ACT.Exp)
            act.wait_ge(act_ready.handle, act_ready.at(3))
            for h in range(ML_H):
                act.wait_ge(spread.handle, spread.at(ML_H + h + 1))
                nc.scalar.activation(SI[:, h, :], m.bank[(5 + h) % 8][:, :], ACT.Exp).then_inc(expd.handle, 1)
            for h in range(ML_H):
                act.wait_ge(evac.handle, evac.at(h + 1))
                for c in range(NT):
                    nc.scalar.activation(E[:, h, c * P:(c + 1) * P], E[:, h, c * P:(c + 1) * P], ACT.Exp, bias=cols[:, c, h:h + 1])

        @block.tensor
        def _(pe):
            pe.wait_ge(ready.handle, ready.at(2))
            for c in range(NT):
                for n, row in enumerate((li, b)):
                    last = nc.tensor.transpose(m.bank[0][:, 8 * c + 4 * n:8 * c + 4 * n + 4], row[:, c * P:(c + 1) * P],
                                               ident[0:4, 0:4])
            last.then_inc(turned.handle, 1)
            for n in range(8):
                h = n % ML_H
                if n == 7:
                    pe.wait_ge(act_ready.handle, act_ready.at(3))
                    pe.wait_ge(expd.handle, expd.at(1))
                nc.tensor.matmul(m.bank[(1 + n) % 8][:, :], sel[:, h, :], (mx if n < ML_H else lf), start=True, stop=True)\
                    .then_inc(spread.handle, 1)

        @block.sync
        def _(sp):
            pass
    for s, n in ((chain, count[0]), (ready, 2), (act_ready, 3), (turned, 1), (spread, 8), (evac, ML_H), (expd, ML_H)):
        s.base += n


def ml_chunks(m):
    nc = m.nc
    W1 = ML_V + 1
    V = m.view(M_V, NT * ML_H, W1)
    hm = m.view(M_HM, NT, D)
    q, k, qs = m.view(M_Q, ML_H, T), m.view(M_K, ML_H, T), m.view(M_QS, ML_H, T)
    E, SI = m.view(M_E, ML_H, T), m.view(M_SI, ML_H, T)
    ktok = m.view(M_KTOK, NT * ML_H, P)
    state = m.view(M_STATE, ML_H, W1)
    cols = m.view(M_SM, NT, 8)
    stats = m.view(M_SM + 64, 16, 6)
    den = m.view(M_SM + 40, 16)
    ident = m.view(A_CONST + C_ID, P)
    kt_done, kt_evac, qk_done, p_ready, num_done, num_evac, ds_done, st_ready, chain, zero = (m.sem(n) for n in (
        "ktok_turned", "ktok_evac", "qk_done", "p_ready", "num_done", "num_evac", "ds_done", "state_ready", "dve_chain",
        "state_zeroed"))
    count = [0]
    units = [(c, h) for c in range(NT) for h in range(ML_H)]
    with nc.Block() as block:
        @block.tensor
        def _(pe):
            for h in range(ML_H):
                if h >= 2:
                    pe.wait_ge(kt_evac.handle, kt_evac.at(h - 1))
                for c in range(NT):
                    last = nc.tensor.transpose(m.bank[h % 2][:, c * P:(c + 1) * P], k[:, h, c * P:(c + 1) * P], ident)
                last.then_inc(kt_done.handle, 1)
            pe.wait_ge(kt_evac.handle, kt_evac.at(ML_H))
            pe.wait_ge(zero.handle, zero.at(1))

            def product(n):
                c, h = units[n]
                if n >= 2:
                    pe.wait_ge(p_ready.handle, p_ready.at(n - 1))
                t = slice(c * P, (c + 1) * P)
                nc.tensor.matmul(m.bank[n % 2][:, 0:P], k[:, h, t], q[:, h, t], start=True, stop=True).then_inc(qk_done.handle, 1)

            product(0)
            for n, (c, h) in enumerate(units):
                t = slice(c * P, (c + 1) * P)
                if n + 1 < len(units):
                    product(n + 1)
                if n >= 2:
                    pe.wait_ge(st_ready.handle, st_ready.at(n - 1))
                nc.tensor.matmul(m.bank[4 + n % 2][:, 0:W1], ktok[:, ML_H * c + h, :], V[:, n, :], start=True, stop=True)\
                    .then_inc(ds_done.handle, 1)
                pe.wait_ge(p_ready.handle, p_ready.at(n + 1))
                if n >= 2:
                    pe.wait_ge(num_evac.handle, num_evac.at(n - 1))
                if c >= 1:
                    pe.wait_ge(st_ready.handle, st_ready.at(n - ML_H + 1))
                nc.tensor.matmul(m.bank[2 + n % 2][:, 0:W1], E[:, h, t], V[:, n, :], start=True, stop=False)
                nc.tensor.matmul(m.bank[2 + n % 2][:, 0:W1], qs[:, h, t], state[:, h, :], start=False, stop=True)\
                    .then_inc(num_done.handle, 1)

        @block.scalar
        def _(act):
            for h in range(ML_H):
                act.wait_ge(kt_done.handle, kt_done.at(h + 1))
                for c in range(NT):
                    last = nc.scalar.activation(ktok[:, ML_H * c + h, :], m.bank[h % 2][:, c * P:(c + 1) * P], ACT.Copy,
                                                scale=E[:, h, c * P + P - 1:c * P + P])
                last.then_inc(kt_evac.handle, 1)

        @block.vector
        def _(dve):
            def link(ins):
                count[0] += 1
                ins.then_inc(chain.handle, 1)
                dve.wait_ge(chain.handle, chain.at(count[0]))

            nc.vector.memset(state[:, :, :], 0.0).then_inc(zero.handle, 1)
            dve.wait_ge(kt_evac.handle, kt_evac.at(ML_H))
            dve.wait_ge(zero.handle, zero.at(1))

            def weigh(n):
                c, h = units[n]
                dve.wait_ge(qk_done.handle, qk_done.at(n + 1))
                t = slice(c * P, (c + 1) * P)
                nc.vector.tensor_tensor(E[:, h, t], m.bank[n % 2][:, 0:P], E[:, h, t], ALU.mult).then_inc(p_ready.handle, 1)

            weigh(0)
            for n, (c, h) in enumerate(units):
                if n + 1 < len(units):
                    weigh(n + 1)
                bank = m.bank[2 + n % 2]
                dve.wait_ge(num_done.handle, num_done.at(n + 1))
                link(nc.vector.tensor_scalar(den[:, n:n + 1], bank[:, ML_V:W1], -1.0, None, ALU.mult))
                link(nc.vector.scalar_tensor_tensor(out=den[:, n:n + 1], in0=bank[:, ML_V:W1], scalar=cols[:, c, 4 + h:5 + h],
                                                    in1=den[:, n:n + 1], op0=ALU.max, op1=ALU.max))
                link(nc.vector.reciprocal(den[:, n:n + 1], den[:, n:n + 1]))
                out = hm[:, c, ML_V * h:ML_V * (h + 1)]
                nc.vector.tensor_scalar(out, bank[:, 0:ML_V], den[:, n:n + 1], None, ALU.mult).then_inc(num_evac.handle, 1)
                dve.wait_ge(num_evac.handle, num_evac.at(n + 1))
                nc.vector.bn_stats(stats[:, n, :], out)
                dve.wait_ge(ds_done.handle, ds_done.at(n + 1))
                nc.vector.scalar_tensor_tensor(out=state[:, h, :], in0=state[:, h, :], scalar=SI[:, h, c * P + P - 1:c * P + P],
                                               in1=m.bank[4 + n % 2][:, 0:W1], op0=ALU.mult, op1=ALU.add).then_inc(st_ready.handle, 1)
                dve.wait_ge(st_ready.handle, st_ready.at(n + 1))
    for s, n in ((kt_done, ML_H), (kt_evac, ML_H), (qk_done, 16), (p_ready, 16), (num_done, 16), (num_evac, 16), (ds_done, 16),
                 (st_ready, 16), (chain, count[0]), (zero, 1)):
        s.base += n


def ml_gate(m):
    nc = m.nc
    hm = m.view(M_HM, NT, D)
    cc, Z, Y = m.view(M_C, KT, T), m.view(M_Z, KT, T), m.view(M_Y, KT, T)
    stats = m.view(M_SM + 64, 16, 6)
    mv = m.view(M_SM + 160, 16, 2)
    ident = m.view(A_CONST + C_ID, P)
    prm = A_PT + 128
    col = lambda at, j: m.view(prm + at + j, 1)
    var, root, normed, turned, y_used, chain = (m.sem(n) for n in (
        "norm_inverse", "norm_root", "hm_normed", "norm_turned", "y_evac", "dve_chain"))
    count = [0]
    with nc.Block() as block:
        @block.vector
        def _(dve):
            def link(ins):
                count[0] += 1
                ins.then_inc(chain.handle, 1)
                dve.wait_ge(chain.handle, chain.at(count[0]))

            for n in range(16):
                ins = nc.vector.bn_aggr(mv[:, n, :], stats[:, n, :])
            link(ins)
            nc.vector.tensor_scalar(mv[:, :, 1], mv[:, :, 1], 1e-6, None, ALU.add).then_inc(var.handle, 1)
            for j in range(KT):
                ins = nc.vector.tensor_scalar(cc[:, j, :], cc[:, j, :], col(ML_SKIP, j), None, ALU.mult)
            dve.wait_ge(root.handle, root.at(1))
            link(nc.vector.reciprocal(mv[:, :, 1], mv[:, :, 1]))
            for n in range(16):
                part = hm[:, n // 4, ML_V * (n % 4):ML_V * (n % 4 + 1)]
                nc.vector.tensor_scalar(part, part, mv[:, n, 0:1], mv[:, n, 1:2], ALU.subtract, ALU.mult).then_inc(normed.handle, 1)
            for j in range(KT):
                dve.wait_ge(turned.handle, turned.at(j + 1))
                link(nc.vector.scalar_tensor_tensor(out=Y[:, j, :], in0=m.bank[j][:, :], scalar=col(ML_GN, j), in1=cc[:, j, :],
                                                    op0=ALU.mult, op1=ALU.add))
                nc.vector.tensor_tensor(Y[:, j, :], Y[:, j, :], Z[:, j, :], ALU.mult)

        @block.scalar
        def _(act):
            act.wait_ge(var.handle, var.at(1))
            nc.scalar.activation(mv[:, :, 1], mv[:, :, 1], ACT.Sqrt).then_inc(root.handle, 1)

        @block.tensor
        def _(pe):
            pe.wait_ge(normed.handle, normed.at(16))
            for j in range(KT):
                for a in range(NT):
                    last = nc.tensor.transpose(m.bank[j][:, a * P:(a + 1) * P], hm[:, a, j * P:(j + 1) * P], ident)
                last.then_inc(turned.handle, 1)
    for s, n in ((var, 1), (root, 1), (normed, 16), (turned, KT), (chain, count[0])):
        s.base += n


LAYERS = "rsmr"


def encoder(nc, x, norm_g, final_g, rw_w_in, rw_mu, rw_w0, rw_w2, rw_a0, rw_a2, rw_k_k, rw_k_a, rw_r_k, rw_ln_g,
            rw_ln_b, rw_w_out, sw_w_in, sw_sinks, sw_w_out, ml_w_in, ml_conv_w, ml_conv_b, ml_w_q, ml_w_k, ml_i_bias,
            ml_f_bias, ml_gn_g, ml_skip, ml_w_out, consts, consts2, out):
    rows = lambda ap: ap.rearrange("(k c) -> k c", c=P)
    heads = lambda ap: ap.rearrange("h c -> (h c)").rearrange("(k c) -> k c", c=P)
    rw_rows = []
    for j, layer in ((0, 0), (1, 3)):
        rw_rows.append([(RW_NORM, rows(norm_g[layer])),
                        (RW_MU, rw_mu[j].rearrange("g d -> (g d)").rearrange("(k c) -> k c", c=P)),
                        (RW_W0, rows(rw_w0[j])), (RW_A0, rows(rw_a0[j])), (RW_KK, heads(rw_k_k[j])),
                        (RW_KA, heads(rw_k_a[j])), (RW_RK, heads(rw_r_k[j])), (RW_LNG, heads(rw_ln_g[j])),
                        (RW_LNB, heads(rw_ln_b[j]))])
    sw_ml = [(SW_NORM, rows(norm_g[1])), (ML_NORM, rows(norm_g[2])),
             (ML_CW, ml_conv_w[0].rearrange("t d -> (t d)").rearrange("(k c) -> k c", c=P)),
             (ML_CB, rows(ml_conv_b[0])), (ML_GN, heads(ml_gn_g[0])), (ML_SKIP, rows(ml_skip[0]))]
    with ExitStack() as ctx:
        m = Machine(nc, ctx)
        tile = lambda w, at, n=P: (w[:, at:at + n].rearrange("(k p) n -> p k n", p=P), (KT, n))
        row = lambda w, k: (w[k * P:(k + 1) * P, :], (D,))
        plan = []
        for n, kind in enumerate(LAYERS):
            plan.append(len(m.weights))
            if kind == "r":
                j = 1 if n == 3 else 0
                w = rw_w_in[j]
                m.weights.append(tile(w, 4 * D))
                for g in (1, 0, 2, 3):
                    m.weights += [tile(w, g * D + k * P) for k in range(KT)]
                plan.append(len(m.weights))
                m.weights += [row(rw_w_out[j], k) for k in range(KT)]
            elif kind == "s":
                w = sw_w_in[0]
                m.weights += [row(w[:, 0:D], k) for k in range(KT)]
                m.weights += [(w[2 * k * P:2 * (k + 1) * P, D:D + 512].rearrange("(k p) n -> p k n", p=P), (2, 512))
                              for k in range(KT // 2)]
                m.weights += [tile(w, D + 512 + k * P) for k in range(KT)]
                plan.append(len(m.weights))
                m.weights += [row(sw_w_out[0], k) for k in range(KT)]
            else:
                w = ml_w_in[0]
                m.weights += [tile(w, k * P) for k in range(KT)] + [tile(w, 2 * D + k * P) for k in range(KT)]
                m.weights += [(v.rearrange("h (e p) d -> p (h e) d", p=P), (KT, P)) for v in (ml_w_q[0], ml_w_k[0])]
                m.weights += [row(w[:, D:2 * D], k) for k in range(KT)]
                plan.append(len(m.weights))
                m.weights += [row(ml_w_out[0], k) for k in range(KT)]
        stage_load(m, x, consts, rw_rows, sw_ml, plan)
        for n, kind in enumerate(LAYERS):
            if kind == "r":
                j = 1 if n == 3 else 0
                prm = A_PT + 256 * j
                a, b = plan[2 * n:2 * n + 2]
                stage_norm(m, 256 * j + RW_NORM, B_R, A_XT)
                rw_project(m, prm, (rw_w2[j], rw_a2[j]), consts2[:, 0:T], a)
                for batch in range(NC // BC):
                    rw_pairs(m, batch)
                    rw_invert(m)
                    rw_carry(m, batch)
                rw_gate(m, prm, b)
                stage_out(m, B_KK, b)
            elif kind == "s":
                a, b = plan[2 * n:2 * n + 2]
                stage_norm(m, 128 + SW_NORM, B_R, A_XT)
                sw_project(m, sw_sinks[0], a)
                sw_attend(m)
                stage_out(m, S_Y, b)
            else:
                a, b = plan[2 * n:2 * n + 2]
                stage_norm(m, 128 + ML_NORM, B_R, M_XT)
                ml_project(m, ml_w_in[0][:, 3 * D:3 * D + 8], ml_i_bias[0], ml_f_bias[0],
                           consts2[0:4, T:4 * T].rearrange("p (a t) -> p a t", a=3), a)
                ml_gates(m)
                ml_chunks(m)
                ml_gate(m)
                stage_out(m, M_Y, b)
        stage_store(m, final_g, out)


_INS = ["x", "norm_g", "final_g", "rw_w_in", "rw_mu", "rw_w0", "rw_w2", "rw_a0", "rw_a2", "rw_k_k", "rw_k_a", "rw_r_k",
        "rw_ln_g", "rw_ln_b", "rw_w_out", "sw_w_in", "sw_sinks", "sw_w_out", "ml_w_in", "ml_conv_w", "ml_conv_b",
        "ml_w_q", "ml_w_k", "ml_i_bias", "ml_f_bias", "ml_gn_g", "ml_skip", "ml_w_out"]


def kernel(**inputs):
    import numpy as _np
    import concourse.bacc as _bacc
    from concourse import mybir as _mybir
    from concourse.bass_utils import run_bass_kernel_spmd as _run

    nc = _bacc.Bacc("TRN2", target_bir_lowering=False, num_devices=1)
    arrays, args = {}, []
    given = {name: _np.ascontiguousarray(inputs[name]) for name in _INS}
    given["masks"], given["rows"] = constants(), more_constants()
    for name, a in given.items():
        arrays[f"in_{name}"] = a
        args.append(nc.dram_tensor(f"in_{name}", a.shape, _mybir.dt.from_np(a.dtype), kind="ExternalInput").ap())
    args.append(nc.dram_tensor("out_h", (1, T, D), _mybir.dt.float32, kind="ExternalOutput").ap())
    encoder(nc, *args)
    r = _run(nc, [arrays], core_ids=[0])
    return r.results[0]["out_h"]
```

```python
import math
from contextlib import ExitStack

import numpy as np

import concourse.bass as bass
from concourse import mybir

F32 = mybir.dt.float32
ALU = mybir.AluOpType
ACT = mybir.ActivationFunctionType
AX = mybir.AxisListType

P = 128
T = 512
D = 1024
KT = D // P
NT = T // P
C = 64
NC = T // C
NH = 16
DECAY = math.exp(-0.5)
NEG = -1.0e30
SLOTS = 4

C_ID, C_BONES, C_GMASK, C_XMASK, C_TRI, C_ROPE = 0, 128, 256, 384, 448, 576
C_END = 640
RW_NORM, RW_MU, RW_W0, RW_A0, RW_KK, RW_KA, RW_RK, RW_LNG, RW_LNB = 0, 8, 56, 64, 72, 80, 88, 96, 104
SW_NORM, ML_NORM, ML_CW, ML_CB, ML_GN, ML_SKIP = 0, 8, 16, 48, 56, 64
MU_R, MU_K, MU_V, MU_G, MU_W, MU_A = (RW_MU + 8 * n for n in range(6))

A_H = 0
A_CONST = A_H + 4096
A_PT = A_CONST + C_END
A_SMALL = A_PT + 384
A_RING = A_SMALL + 96
A_BUF = A_RING + SLOTS * 1024
A_TMP = A_BUF + 7 * 4096
A_END = 53100
B_R, B_K, B_A, B_L, B_V, B_G, B_KK = (A_BUF + 4096 * n for n in range(7))
A_XT = A_TMP
A_DX = A_XT + KT * (T + 1)
A_T5 = A_DX + 4096


def constants():
    c = np.zeros((P, C_END), np.float32)
    r = np.arange(P)
    c[:, C_ID:C_ID + P] = np.eye(P)
    c[:, C_BONES:C_BONES + P] = (r[:, None] // C == r[None, :] // C)
    s, t = (r % C)[:, None], np.arange(C)[None, :]
    c[:, C_GMASK:C_GMASK + C] = t > s
    c[:, C_GMASK + C:C_GMASK + P] = t >= s
    c[:, C_XMASK:C_XMASK + C] = (s >= 32) & (t < 32)
    c[:, C_TRI:C_TRI + P] = np.where(r[None, :] >= r[:, None], 0.0, NEG)
    inv = np.power(np.float32(500000.0), -np.arange(8, dtype=np.float32) * np.float32(2.0 / 16))
    for a in range(NT):
        ang = (a * P + r).astype(np.float32)[:, None] * inv[None, :]
        c[:, C_ROPE + a * 8:C_ROPE + a * 8 + 8] = np.cos(ang)
        c[:, C_ROPE + 32 + a * 8:C_ROPE + 40 + a * 8] = np.sin(ang)
    return c


def more_constants():
    c = np.ones((P, 5 * T), np.float32)
    c[:, 0:T:C] = 0.0
    c[:, T:2 * T:P] = 0.0
    c[:, 2 * T:] = 0.0
    c[:, 2 * T:3 * T:P] = NEG
    for h in range(4):
        c[h, 3 * T + h * P:3 * T + (h + 1) * P] = 1.0
    return c


class Count:

    def __init__(self, handle):
        self.handle, self.base = handle, 0

    def at(self, n):
        return self.base + n


class Machine:

    def __init__(self, nc, ctx):
        self.nc = nc
        self.arena = ctx.enter_context(nc.sbuf_tensor("arena", [P, A_END], F32))
        self.bank = [ctx.enter_context(nc.psum_tensor(f"bank{n}", [P, 512], F32)) for n in range(8)]
        self.ctx = ctx
        self.sems = {}
        self.slot_full = [ctx.enter_context(nc.semaphore(f"slot{n}_full")) for n in range(SLOTS)]
        self.used_by = []
        self.weights = []
        self.issued = 0

    def sem(self, name):
        if name not in self.sems:
            self.sems[name] = Count(self.ctx.enter_context(self.nc.semaphore(name)))
        return self.sems[name]

    def view(self, at, *shape, rows=slice(0, P)):
        n = int(np.prod(shape))
        flat = self.arena[rows, at:at + n]
        if len(shape) == 1:
            return flat
        names = "abc"[:len(shape)]
        return flat.rearrange(f"p ({' '.join(names)}) -> p {' '.join(names)}",
                              **{k: v for k, v in zip(names[1:], shape[1:])})

    def slot(self, n):
        return A_RING + (n % SLOTS) * 1024

    def load_weights(self, eng, upto):
        for n in range(self.issued, min(upto, len(self.weights))):
            if n >= SLOTS:
                eng.wait_ge(*self.used_by[n - SLOTS])
            src, shape = self.weights[n]
            eng.dma_start(self.view(self.slot(n), *shape), src).then_inc(self.slot_full[n % SLOTS], 16)
        self.issued = max(self.issued, min(upto, len(self.weights)))

    def weights_arrived(self, pe, n):
        pe.wait_ge(self.slot_full[n % SLOTS], 16 * (n // SLOTS + 1))


def stage_load(m, x, consts, rw, sw_ml, w):
    nc = m.nc
    loaded, zeroed, turned, copied = m.sem("loaded"), m.sem("zeroed"), m.sem("turned"), m.sem("copied")
    stage = m.view(A_T5, 3, P)
    with nc.Block() as block:
        @block.sync
        def _(sp):
            sp.dma_start(m.view(A_CONST, C_END), consts).then_inc(loaded.handle, 16)
            sp.dma_start(m.view(A_H, NT, D), x.rearrange("o (a p) d -> p (o a) d", p=P)).then_inc(loaded.handle, 16)
            sp.wait_ge(zeroed.handle, 1)
            n = 2
            for s, rows in ((0, rw[0]), (2, rw[1]), (1, sw_ml)):
                for at, src in rows:
                    k = src.shape[0]
                    sp.dma_start(stage[at:at + k, s, :], src).then_inc(loaded.handle, 16)
                    n += 1
            loaded.total = 16 * n
            m.load_weights(sp, SLOTS)

        @block.vector
        def _(dve):
            nc.vector.memset(stage[:, :, :], 0.0).then_inc(zeroed.handle, 1)
            dve.wait_ge(turned.handle, 1)
            nc.vector.tensor_copy(m.view(A_PT, 384), m.bank[0][:, 0:384]).then_inc(copied.handle, 1)

        @block.tensor
        def _(pe):
            pe.wait_ge(loaded.handle, loaded.total)
            for s in range(3):
                last = nc.tensor.transpose(m.bank[0][:, s * P:(s + 1) * P], stage[:, s, :], m.view(A_CONST + C_ID, P))
            last.then_inc(turned.handle, 1)


def stage_norm(m, gcol, xn_at, out_at):
    nc = m.nc
    h = m.view(A_H, NT, D)
    xn = m.view(xn_at, NT, D)
    xt = m.view(out_at, KT, T + 1)
    ss = m.view(A_SMALL, NT)
    squared, root, inverse, scaled, turned, evac = (
        m.sem(n) for n in ("norm_squared", "norm_root", "norm_inverse", "norm_scaled", "norm_turned", "norm_evac"))
    with nc.Block() as block:
        @block.scalar
        def _(act):
            for a in range(NT):
                ins = nc.scalar.activation(xn[:, a, :], h[:, a, :], ACT.Square, accum_out=ss[:, a:a + 1])
            ins.then_inc(squared.handle, 1)
            act.wait_ge(inverse.handle, inverse.at(1))
            nc.scalar.activation(ss, ss, ACT.Sqrt).then_inc(root.handle, 1)

        @block.vector
        def _(dve):
            nc.vector.memset(xt[:, :, 0:1], 0.0)
            dve.wait_ge(squared.handle, squared.at(1))
            nc.vector.tensor_scalar(ss, ss, 1.0 / D, 1e-6, ALU.mult, ALU.add).then_inc(inverse.handle, 1)
            dve.wait_ge(root.handle, root.at(1))
            nc.vector.reciprocal(ss, ss).then_inc(inverse.handle, 1)
            dve.wait_ge(inverse.handle, inverse.at(2))
            for a in range(NT):
                nc.vector.tensor_scalar(xn[:, a, :], h[:, a, :], ss[:, a:a + 1], None, ALU.mult).then_inc(scaled.handle, 1)
            for k in range(KT):
                dve.wait_ge(turned.handle, turned.at(k + 1))
                nc.vector.tensor_scalar(xt[:, k, 1:T + 1], m.bank[k][:, :], m.view(A_PT + gcol + k, 1), None,
                                        ALU.mult)

        @block.tensor
        def _(pe):
            for k in range(KT):
                for a in range(NT):
                    if k == 0:
                        pe.wait_ge(scaled.handle, scaled.at(a + 1))
                    last = nc.tensor.transpose(m.bank[k][:, a * P:(a + 1) * P], xn[:, a, k * P:(k + 1) * P],
                                               m.view(A_CONST + C_ID, P))
                last.then_inc(turned.handle, 1)
    squared.base += 1
    root.base += 1
    inverse.base += 2
    scaled.base += NT
    turned.base += KT


FIRST, SECOND = 12, 20
BC = 4
Q = 32
A_TU = A_RING
A_Z = A_DX
A_XS = A_Z + 2048
A_US = A_XS + 1024
A_S = A_T5
A_RHS = A_S + 512
A_AD = A_RHS + 512
A_ARZ = A_AD + 1024
A_BK = A_ARZ + 2048
A_EP = A_BK + 1024
A_EPI = A_EP + 8 * (C + 1)
A_A32, A_T32, A_PROD = A_ARZ, A_ARZ + 1024, A_BK
A_LORA, A_SIG, A_RESET, A_SQ, A_RT = A_ARZ, A_ARZ + 512, A_ARZ + 1536, A_BK, A_AD
A_OMKA = A_SMALL + 16
A_PC = A_SMALL + 24
GS_AT = [A_XT, A_XT + 2048, A_H, A_H + 2048, B_G, B_G + 2048, A_XT, A_XT + 2048]
LO, HI = slice(0, 64), slice(64, 128)
SIDES = ((0, LO), (1, HI))


def wide(ap, n):
    return ap.unsqueeze(1).to_broadcast([ap.shape[0], n, ap.shape[1]])


def heads(buf, par):
    return buf.rearrange("p (k h) c -> p k h c", h=2)[:, :, par, :]


def rw_mix(m, prm, w2a2, reset_src, n0, n_out, spill):
    nc = m.nc
    xt = m.view(A_XT, KT, T + 1)
    dx = m.view(A_DX, KT, T)
    R, K, BB, L, V, G, KK = (m.view(at, KT, T) for at in (B_R, B_K, B_A, B_L, B_V, B_G, B_KK))
    lora, reset, rt = m.view(A_LORA, T), m.view(A_RESET, T), m.view(A_RT, T)
    sig, sq = ([m.view(at + 512 * n, T) for n in range(2)] for at in (A_SIG, A_SQ))
    w2a2_sb = m.view(B_R, D)
    omka = m.view(A_OMKA, 8)
    ident, bones = m.view(A_CONST + C_ID, P), m.view(A_CONST + C_BONES, P)
    col = lambda at, k: m.view(prm + at + k, 1)
    gmask, xmask = m.view(A_CONST + C_GMASK, P), m.view(A_CONST + C_XMASK, C)
    arz, bk = m.view(A_ARZ, NH, P), m.view(A_BK, KT, P)
    ep, epi = m.view(A_EP, KT, C + 1), m.view(A_EPI, KT, C)
    gs = [m.view(at, 2, NH, C) for at in GS_AT]
    ad, a32, t32 = (m.view(at, Q, Q) for at in (A_AD, A_A32, A_T32))
    tt, uu = a32, ad
    tu_all = m.view(A_TU, BC * KT, P)
    tu = [m.view(A_TU + 1024 * (c % BC), KT, P) for c in range(NC)]
    z = [m.view(A_Z + 1024 * (c % 2), NH, C) for c in range(NC)]
    xs, us = m.view(A_XS, KT, P), m.view(A_US, KT, P)
    rhs, S = m.view(A_RHS, KT, C), m.view(A_S, KT, C)
    span = lambda c: slice(c * C, (c + 1) * C)
    pairs = [slice(4 * g, 4 * g + 4) for g in range(2)]
    quarter = lambda bank: bank[:, 0:256].rearrange("p (k c) -> p k c", c=C)
    blocks = lambda bank: bank[:, :].rearrange("p (k c) -> p k c", c=P)
    g_bank = lambda c, q: m.bank[q if c < BC else (q + 2) % 4]
    t_bank = lambda c, q: m.bank[4 + q if c < BC else 2 + q]

    tiles = [("lora", 0)]
    for j in range(KT):
        tiles += [("decay", j), ("a", j)]
    for j in range(KT + 1):
        tiles += [("k", j)] * (j < KT) + [("n2", j - 1)] * (j > 0)
    tiles += [(n, j) for n in ("r", "v", "g") for j in range(KT)]
    place = {t: n for n, t in enumerate(tiles)}
    tile_bank = lambda n: m.bank[6 + tiles[n][1] % 2 if tiles[n][0] in "vg" else n % 8]
    mixes = ["w", "a", "k", "r", "v", "g"]
    mix_at = {"w": G, "a": V, "k": G, "r": V, "v": G, "g": dx}
    mu_at = {"w": MU_W, "a": MU_A, "k": MU_K, "r": MU_R, "v": MU_V, "g": MU_G}
    mixed, tile_done, act_done, gated, kk_squared, chain, act_chain, aux, root_used, sig_used, keys_ready = (
        m.sem(n) for n in ("mixed", "tile_done", "act_evacuated", "g_gated", "kk_squared", "dve_chain", "act_chain",
                           "aux_loaded", "root_used", "sig_used", "keys_ready"))
    h_spilled, g_spilled, reloaded = m.sem("h_spilled"), m.sem("g_spilled"), m.sem("reloaded")
    ep_cleared, exp_ready, ar_scaled, ark_staged, b_scaled, k_scaled, b_staged = (m.sem(n) for n in (
        "ep_cleared", "exp_ready", "ar_scaled", "ark_staged", "b_scaled", "k_scaled", "b_staged"))
    g_done, g_evac, bkt_done, bkt_evac = (m.sem(n) for n in ("g_done", "g_evac", "bkt_done", "bkt_evac"))
    gathered, step, t_turned, u_turned, tu_cleared, t_placed, u_placed = (m.sem(n) for n in (
        "gathered", "inverse_step", "t_turned", "u_turned", "tu_cleared", "t_placed", "u_placed"))
    carry_cleared, z_cleared, v_done, v_evac, x_done, xs_ready, xu_done, us_ready, s_added = (m.sem(n) for n in (
        "carry_cleared", "z_cleared", "v_done", "v_evac", "x_done", "xs_ready", "xu_done", "us_ready", "s_added"))
    rhs_done, rhs_evac, sa_done, sa_evac, y_done, y_evac, s_done, s_ready = (m.sem(n) for n in (
        "rhs_done", "rhs_evac", "sa_done", "sa_evac", "y_done", "y_evac", "s_done", "s_ready"))
    m.used_by += [(tile_done.handle, tile_done.at(place[t] + 1)) for t in tiles if t[0] not in ("decay", "a", "n2")]
    links, steps = [0], [0]

    with nc.Block() as block:
        @block.sync
        def _(sp):
            sp.dma_start(w2a2_sb[0:64, :], w2a2[0]).then_inc(aux.handle, 16)
            sp.dma_start(w2a2_sb[64:128, :], w2a2[1]).then_inc(aux.handle, 16)
            sp.dma_start(reset, reset_src).then_inc(aux.handle, 16)
            sp.dma_start(spill[0], m.view(A_H, 4096)).then_inc(h_spilled.handle, 16)
            m.load_weights(sp, n0 + 33)
            sp.wait_ge(gated.handle, gated.at(KT))
            sp.dma_start(spill[1], m.view(B_G, 4096)).then_inc(g_spilled.handle, 16)
            sp.wait_ge(y_done.handle, y_done.at(2 * 4))
            sp.wait_ge(h_spilled.handle, h_spilled.at(16))
            sp.dma_start(m.view(A_H, 4096), spill[0]).then_inc(reloaded.handle, 16)
            sp.wait_ge(y_done.handle, y_done.at(2 * 6))
            sp.wait_ge(g_spilled.handle, g_spilled.at(16))
            sp.dma_start(m.view(B_G, 4096), spill[1]).then_inc(reloaded.handle, 16)
            sp.wait_ge(us_ready.handle, us_ready.at(2 * NC))
            m.load_weights(sp, n_out + SLOTS)
            sp.wait_ge(reloaded.handle, reloaded.at(32))

        @block.gpsimd
        def _(pool):
            nc.gpsimd.memset(ep[:, :, 0:1], 1.0).then_inc(ep_cleared.handle, 1)
            pool.wait_ge(keys_ready.handle, keys_ready.at(1))
            for c in range(NC):
                if c == BC:
                    pool.wait_ge(tile_done.handle, tile_done.at(len(tiles)))
                    nc.gpsimd.memset(m.view(A_Z, 4096), 0.0).then_inc(carry_cleared.handle, 1)
                t = span(c)
                pool.wait_ge(exp_ready.handle, exp_ready.at(c + 1))
                nc.gpsimd.tensor_tensor(BB[:, :, t], BB[:, :, t], epi, ALU.mult).then_inc(b_scaled.handle, 1)
                pool.wait_ge(ar_scaled.handle, ar_scaled.at(c + 1))
                nc.gpsimd.tensor_tensor(R[:, :, t], R[:, :, t], K[:, :, t], ALU.mult)
                nc.gpsimd.tensor_tensor(K[:, :, t], K[:, :, t], epi, ALU.mult).then_inc(k_scaled.handle, 1)

        @block.scalar
        def _(act):
            def read_tile(n):
                what, j = tiles[n]
                bank = tile_bank(n)
                act.wait_ge(tile_done.handle, tile_done.at(n + 1))
                if what == "lora":
                    nc.scalar.activation(lora[0:64, :], bank[0:64, :], ACT.Tanh).then_inc(act_chain.handle, 1)
                    out = nc.scalar.activation(lora[64:128, :], bank[64:128, :], ACT.Copy)
                    act.wait_ge(act_chain.handle, act_chain.at(1))
                elif what == "decay":
                    if j >= 2:
                        act.wait_ge(sig_used.handle, sig_used.at(j - 1))
                    out = nc.scalar.activation(sig[j % 2], bank[:, :], ACT.Sigmoid, bias=col(RW_W0, j))
                elif what == "a":
                    out = nc.scalar.activation(BB[:, j, :], bank[:, :], ACT.Sigmoid, bias=col(RW_A0, j))
                elif what == "n2":
                    if j >= 1:
                        act.wait_ge(root_used.handle, root_used.at(j))
                    out = nc.scalar.activation(rt, bank[:, :], ACT.Sqrt)
                elif what == "g":
                    out = nc.scalar.activation(G[:, j, :], bank[:, :], ACT.Sigmoid)
                else:
                    out = nc.scalar.activation({"k": K, "r": R, "v": V}[what][:, j, :], bank[:, :], ACT.Copy)
                out.then_inc(act_done.handle, 1)

            def exps(c):
                if c >= 1:
                    act.wait_ge(ar_scaled.handle, ar_scaled.at(c))
                    act.wait_ge(k_scaled.handle, k_scaled.at(c))
                nc.scalar.activation(ep[:, :, 1:C + 1], L[:, :, span(c)], ACT.Exp, scale=-DECAY)
                nc.scalar.activation(epi, L[:, :, span(c)], ACT.Exp, scale=DECAY).then_inc(exp_ready.handle, 1)

            def stage_b(c):
                act.wait_ge(b_scaled.handle, b_scaled.at(c + 1))
                if c >= 1:
                    act.wait_ge(bkt_done.handle, bkt_done.at(2 * c))
                if c == BC:
                    act.wait_ge(u_turned.handle, u_turned.at(1))
                nc.scalar.activation(bk[LO, :, 0:C], BB[LO, :, span(c)], ACT.Copy)
                nc.scalar.activation(bk[HI, :, C:P], BB[HI, :, span(c)], ACT.Copy).then_inc(b_staged.handle, 1)

            def keep_bkt(c):
                for q in range(2):
                    act.wait_ge(bkt_done.handle, bkt_done.at(2 * c + q + 1))
                    nc.scalar.activation(BB[:, pairs[q], span(c)], blocks(t_bank(c, q))[:, :, 0:C], ACT.Copy)
                    nc.scalar.activation(K[:, pairs[q], span(c)], blocks(t_bank(c, q))[:, :, C:P], ACT.Copy)\
                        .then_inc(bkt_evac.handle, 1)

            def gather(c):
                if c == BC:
                    act.wait_ge(u_placed.handle, u_placed.at(1))
                act.wait_ge(g_evac.handle, g_evac.at(4 * c + 4))
                i = c % BC
                for g in range(4):
                    rows, half = slice(Q * g, Q * g + Q), g % 2
                    last = nc.scalar.activation(ad[rows, :, KT * i:KT * i + KT],
                                                heads(gs[c][:, 0], g // 2)[rows, :, Q * half:Q * half + Q]
                                                .rearrange("p k c -> p c k"), ACT.Copy)
                if i == BC - 1:
                    last.then_inc(gathered.handle, 1)

            def place_inverse(b):
                act.wait_ge(t_turned.handle, t_turned.at(b + 1))
                if b == 0:
                    act.wait_ge(tu_cleared.handle, tu_cleared.at(1))
                else:
                    act.wait_ge(us_ready.handle, us_ready.at(2 * BC * b))
                for g in range(4):
                    rows, at = slice(Q * g, Q * g + Q), Q * (g % 2)
                    last = nc.scalar.activation(tu_all[rows, :, at:at + Q], tt[rows].rearrange("p c n -> p n c"), ACT.Copy)
                last.then_inc(t_placed.handle, 1)

            def values(c):
                if c >= 2:
                    act.wait_ge(s_done.handle, s_done.at(2 * (c - 1)))
                for q in range(2):
                    act.wait_ge(v_done.handle, v_done.at(2 * c + q + 1))
                    nc.scalar.activation(heads(z[c], 0)[HI, pairs[q], :], blocks(m.bank[q])[LO, :, 0:C], ACT.Copy)
                    nc.scalar.activation(heads(z[c], 1)[LO, pairs[q], :], blocks(m.bank[q])[LO, :, C:P], ACT.Copy)\
                        .then_inc(v_evac.handle, 1)

            def read_rhs(c):
                for g in range(2):
                    act.wait_ge(rhs_done.handle, rhs_done.at(2 * c + g + 1))
                    for par, rows in SIDES:
                        last = nc.scalar.activation(rhs[rows, pairs[g], :], blocks(m.bank[4 + g])[rows, :, C * par:C * par + C],
                                                    ACT.Copy, scale=-1.0)
                    last.then_inc(rhs_evac.handle, 1)

            def read_sa(c):
                for g in range(2):
                    act.wait_ge(sa_done.handle, sa_done.at(2 * c + g + 1))
                    for par, rows in SIDES:
                        last = nc.scalar.activation(heads(z[c], par)[rows, pairs[g], :], quarter(m.bank[6 + g])[rows], ACT.Copy)
                    last.then_inc(sa_evac.handle, 1)

            def read_y(c):
                for g in range(2):
                    act.wait_ge(y_done.handle, y_done.at(2 * c + g + 1))
                    for par, rows in SIDES:
                        last = nc.scalar.activation(KK[rows, pairs[g], span(c)],
                                                    blocks(m.bank[4 + g])[rows, :, C * par:C * par + C], ACT.Copy)
                    last.then_inc(y_evac.handle, 1)

            for n in range(place["v", 0]):
                read_tile(n)
            act.wait_ge(ep_cleared.handle, ep_cleared.at(1))
            act.wait_ge(keys_ready.handle, keys_ready.at(1))
            exps(0)
            stage_b(0)
            for c in range(BC):
                if c + 1 < BC:
                    exps(c + 1)
                    stage_b(c + 1)
                keep_bkt(c)
                gather(c)
                read_tile(place["v", c])
            for n in range(place["v", BC], len(tiles)):
                read_tile(n)
            place_inverse(0)
            act.wait_ge(carry_cleared.handle, carry_cleared.at(1))
            values(0)
            exps(BC)
            stage_b(BC)
            for c in range(NC):
                read_rhs(c)
                if c + 1 < NC:
                    values(c + 1)
                read_sa(c)
                if c == 0:
                    exps(5)
                if c == 1:
                    exps(7)
                read_y(c)
                if c == 0:
                    keep_bkt(4)
                    stage_b(5)
                    gather(4)
                    exps(6)
                    keep_bkt(5)
                    stage_b(6)
                    gather(5)
                if c == 1:
                    keep_bkt(6)
                    stage_b(7)
                    gather(6)
                if c == 2:
                    keep_bkt(7)
                    gather(7)
                if c == BC - 1:
                    place_inverse(1)

        @block.vector
        def _(dve):
            def link(ins):
                links[0] += 1
                ins.then_inc(chain.handle, 1)
                dve.wait_ge(chain.handle, chain.at(links[0]))

            def mix(g):
                for k in range(KT):
                    nc.vector.scalar_tensor_tensor(out=mix_at[g][:, k, :], in0=dx[:, k, :], scalar=col(mu_at[g], k),
                                                   in1=xt[:, k, 1:T + 1], op0=ALU.mult, op1=ALU.add)\
                        .then_inc(mixed.handle, 1)

            def scale(c):
                dve.wait_ge(exp_ready.handle, exp_ready.at(c + 1))
                t = span(c)
                nc.vector.tensor_copy(m.view(A_PC + KT * c, KT).unsqueeze(2), ep[:, :, C:C + 1])
                nc.vector.tensor_tensor(KK[:, :, t], KK[:, :, t], ep[:, :, 0:C], ALU.mult)
                nc.vector.tensor_tensor(L[:, :, t], R[:, :, t], ep[:, :, 1:C + 1], ALU.mult).then_inc(ar_scaled.handle, 1)

            def stage_ar(c):
                dve.wait_ge(ar_scaled.handle, ar_scaled.at(c + 1))
                if c % BC == 0:
                    if c == BC:
                        dve.wait_ge(t_placed.handle, t_placed.at(1))
                    for par, rows in ((0, HI), (1, LO)):
                        nc.vector.memset(heads(arz, par)[rows], 0.0)
                for par, rows in SIDES:
                    nc.vector.tensor_copy(heads(arz, par)[rows, :, 0:C], KK[rows, :, span(c)])
                    nc.vector.tensor_copy(heads(arz, par)[rows, :, C:P], L[rows, :, span(c)])

            def stage_k(c):
                dve.wait_ge(k_scaled.handle, k_scaled.at(c + 1))
                if c >= 1:
                    dve.wait_ge(bkt_done.handle, bkt_done.at(2 * c))
                nc.vector.tensor_copy(bk[LO, :, C:P], K[LO, :, span(c)])
                nc.vector.tensor_copy(bk[HI, :, 0:C], K[HI, :, span(c)]).then_inc(ark_staged.handle, 1)

            def mask_g(c, upto):
                if c == 2:
                    dve.wait_ge(h_spilled.handle, h_spilled.at(16))
                if c == 4:
                    dve.wait_ge(g_spilled.handle, g_spilled.at(16))
                if c >= 6:
                    dve.wait_ge(y_done.handle, y_done.at(2 * (c - 5)))
                if c + 1 < upto:
                    scale(c + 1)
                for q in range(4):
                    dve.wait_ge(g_done.handle, g_done.at(4 * c + q + 1))
                    if q == 3 and c + 1 < upto:
                        stage_ar(c + 1)
                    nc.vector.tensor_tensor(gs[c][:, :, 4 * q:4 * q + 4, :].rearrange("p a h c -> p h a c"),
                                            g_bank(c, q)[:, :].rearrange("p (h a c) -> p h a c", a=2, c=C),
                                            gmask.rearrange("p (a c) -> p a c", c=C).unsqueeze(1).to_broadcast([P, 4, 2, C]),
                                            ALU.mult).then_inc(g_evac.handle, 1)

            def invert_begin(b):
                dve.wait_ge(gathered.handle, gathered.at(b + 1))
                dve.wait_ge(bkt_done.handle, bkt_done.at(2 * BC * (b + 1)))
                nc.vector.transpose(a32, ad).then_inc(step.handle, 1)
                nc.vector.memset(t32, 0.0).then_inc(step.handle, 1)
                steps[0] += 2
                dve.wait_ge(step.handle, step.at(steps[0]))
                nc.vector.memset(m.view(A_T32, Q * Q)[:, 0:Q * Q:Q + 1], 1.0).then_inc(step.handle, 1)
                steps[0] += 1

            def invert(lo, hi):
                for s in range(lo, hi):
                    n = Q - 1 - s
                    halves = [slice(par, s + 1, 2) for par in range(min(2, s + 1))]
                    width = [len(range(s + 1)[h]) for h in halves]
                    prod = [m.view(A_PROD + 512 * par, n, w) for par, w in enumerate(width)]
                    before = steps[0]
                    for par, h in enumerate(halves):
                        dve.wait_ge(step.handle, step.at(before if s < 2 else before - 1 + par))
                        nc.vector.tensor_tensor(prod[par], a32[:, s + 1:Q, s:s + 1].to_broadcast([P, n, width[par]]),
                                                wide(t32[:, s, h], n), ALU.mult).then_inc(step.handle, 1)
                    for par, h in enumerate(halves):
                        dve.wait_ge(step.handle, step.at(before + par + 1))
                        nc.vector.tensor_tensor(t32[:, s + 1:Q, h], t32[:, s + 1:Q, h], prod[par], ALU.subtract)\
                            .then_inc(step.handle, 1)
                    steps[0] += 2 * len(halves)

            def invert_end():
                dve.wait_ge(step.handle, step.at(steps[0]))
                nc.vector.transpose(tt, t32.rearrange("p t s -> p s t")).then_inc(t_turned.handle, 1)
                nc.vector.transpose(uu, t32).then_inc(u_turned.handle, 1)

            def place_transpose(b):
                dve.wait_ge(u_turned.handle, u_turned.at(b + 1))
                if b == 0:
                    dve.wait_ge(tu_cleared.handle, tu_cleared.at(1))
                else:
                    dve.wait_ge(us_ready.handle, us_ready.at(2 * BC * b))
                for g in range(4):
                    rows, at = slice(Q * g, Q * g + Q), C + Q * (g % 2)
                    last = nc.vector.tensor_copy(tu_all[rows, :, at:at + Q], uu[rows].rearrange("p c n -> p n c"))
                last.then_inc(u_placed.handle, 1)

            def mask_x(c):
                for g in range(2):
                    dve.wait_ge(x_done.handle, x_done.at(2 * c + g + 1))
                    for par, rows in SIDES:
                        last = nc.vector.tensor_tensor(xs[rows, pairs[g], C * par:C * par + C], quarter(m.bank[g])[rows],
                                                       wide(xmask[rows], 4), ALU.mult)
                    last.then_inc(xs_ready.handle, 1)

            def complete_u(c):
                for g in range(2):
                    dve.wait_ge(xu_done.handle, xu_done.at(2 * c + g + 1))
                    for par, rows in SIDES:
                        last = nc.vector.tensor_tensor(us[rows, pairs[g], C * par:C * par + C], tu[c][rows, pairs[g], C:P],
                                                       quarter(m.bank[2 + g])[rows], ALU.subtract)
                    last.then_inc(us_ready.handle, 1)

            def advance(c):
                for g in range(2):
                    dve.wait_ge(s_done.handle, s_done.at(2 * c + g + 1))
                    nc.vector.tensor_tensor(S[:, pairs[g], :], S[:, pairs[g], :], quarter(m.bank[6 + g]), ALU.add)\
                        .then_inc(s_added.handle, 1)
                    dve.wait_ge(s_added.handle, s_added.at(2 * c + g + 1))
                    pc = m.view(A_PC + KT * c, KT)[:, pairs[g]].unsqueeze(2).to_broadcast([P, 4, C])
                    nc.vector.tensor_tensor(S[:, pairs[g], :], S[:, pairs[g], :], pc, ALU.mult).then_inc(s_ready.handle, 1)
                if c + 2 < NC:
                    nc.vector.memset(heads(z[c], 0)[LO], 0.0)
                    nc.vector.memset(heads(z[c], 1)[HI], 0.0).then_inc(z_cleared.handle, 1)

            link(nc.vector.tensor_tensor(dx, xt[:, :, 0:T], xt[:, :, 1:T + 1], ALU.subtract))
            link(nc.vector.tensor_scalar(omka, m.view(prm + RW_KA, 8), -1.0, 1.0, ALU.mult, ALU.add))
            mix("w")
            mix("a")
            dve.wait_ge(tile_done.handle, tile_done.at(1))
            mix("k")
            dve.wait_ge(aux.handle, aux.at(48))
            for j in range(KT):
                dve.wait_ge(act_done.handle, act_done.at(place["decay", j] + 1))
                nc.vector.tensor_tensor_scan(out=L[:, j, :], data0=reset, data1=sig[j % 2], initial=0.0,
                                             op0=ALU.mult, op1=ALU.add).then_inc(sig_used.handle, 1)
            mix("r")
            nc.vector.memset(S, 0.0)
            for j in range(KT + 1):
                if j < KT:
                    dve.wait_ge(act_done.handle, act_done.at(place["k", j] + 1))
                    link(nc.vector.tensor_scalar(KK[:, j, :], K[:, j, :], col(RW_KK, j), None, ALU.mult))
                    if j >= 2:
                        dve.wait_ge(tile_done.handle, tile_done.at(place["n2", j - 2] + 1))
                    nc.vector.tensor_tensor(sq[j % 2], KK[:, j, :], KK[:, j, :], ALU.mult).then_inc(kk_squared.handle, 1)
                if j > 0:
                    i = j - 1
                    dve.wait_ge(act_done.handle, act_done.at(place["n2", i] + 1))
                    link(nc.vector.tensor_scalar(rt, rt, 1e-12, None, ALU.max))
                    link(nc.vector.reciprocal(rt, rt))
                    nc.vector.tensor_tensor(KK[:, i, :], KK[:, i, :], rt, ALU.mult).then_inc(root_used.handle, 1)
            mix("v")
            dve.wait_ge(root_used.handle, root_used.at(KT))
            for j in range(KT):
                link(nc.vector.tensor_scalar(sq[j % 2], BB[:, j, :], col(RW_KA, j), omka[:, j:j + 1], ALU.mult, ALU.add))
                nc.vector.tensor_tensor(K[:, j, :], K[:, j, :], sq[j % 2], ALU.mult)
                last = nc.vector.tensor_tensor(BB[:, j, :], BB[:, j, :], KK[:, j, :], ALU.mult)
            last.then_inc(keys_ready.handle, 1)
            mix("g")
            scale(0)
            stage_ar(0)
            stage_k(0)
            for c in range(BC):
                mask_g(c, BC)
                if c + 1 < BC:
                    stage_k(c + 1)
            invert_begin(0)
            invert(0, Q - 1)
            invert_end()
            for j in range(KT):
                dve.wait_ge(act_done.handle, act_done.at(place["g", j] + 1))
                nc.vector.tensor_tensor(G[:, j, :], tile_bank(place["g", j])[:, :], G[:, j, :], ALU.mult)\
                    .then_inc(gated.handle, 1)
            nc.vector.memset(m.view(A_TU, BC * 1024), 0.0).then_inc(tu_cleared.handle, 1)
            place_transpose(0)
            dve.wait_ge(carry_cleared.handle, carry_cleared.at(1))
            mask_x(0)
            scale(BC)
            stage_ar(BC)
            complete_u(0)
            stage_k(BC)
            for c in range(NC):
                if c == 0:
                    mask_g(4, NC)
                if c == 1:
                    mask_g(6, NC)
                if c == 2:
                    mask_g(7, NC)
                if c == 3:
                    invert(FIRST, SECOND)
                advance(c)
                if c < 2:
                    stage_k((5, 7)[c])
                if c == 3:
                    invert(SECOND, Q - 1)
                    invert_end()
                    place_transpose(1)
                if c + 1 < NC:
                    mask_x(c + 1)
                    complete_u(c + 1)
                if c == 0:
                    mask_g(5, NC)
                    stage_k(6)
                if c == 2:
                    invert_begin(1)
                    invert(0, FIRST)

        @block.tensor
        def _(pe):
            mm = lambda out, a, b, start=True, stop=True: nc.tensor.matmul(out, a, b, start=start, stop=stop,
                                                                          skip_group_check=True)
            slot_used = [n0]

            def project(n):
                what, j = tiles[n]
                bank = tile_bank(n)
                if what == "g" and j >= 2:
                    pe.wait_ge(gated.handle, gated.at(j - 1))
                elif what in "vg":
                    pe.wait_ge(act_done.handle, act_done.at(n - 1 if j >= 2 or what == "g" else place["r", KT - 1] + 1))
                elif n >= 8:
                    pe.wait_ge(act_done.handle, act_done.at(n - 8 + 1))
                if what in ("decay", "a"):
                    if n == 1:
                        pe.wait_ge(act_done.handle, act_done.at(1))
                        pe.wait_ge(aux.handle, aux.at(48))
                    h = slice(0, 64) if what == "decay" else slice(64, 128)
                    last = nc.tensor.matmul(bank[:, :], w2a2_sb[h, j * P:(j + 1) * P], lora[h, :], start=True, stop=True)
                elif what == "n2":
                    pe.wait_ge(kk_squared.handle, kk_squared.at(j + 1))
                    last = nc.tensor.matmul(bank[:, :], bones, sq[j % 2], start=True, stop=True)
                else:
                    m.weights_arrived(pe, slot_used[0])
                    slot = m.view(m.slot(slot_used[0]), KT, P)
                    slot_used[0] += 1
                    if what == "lora":
                        pe.wait_ge(mixed.handle, mixed.at(2 * KT))
                    for k in range(KT):
                        if what == "lora":
                            mm(bank[0:64, :], slot[:, k, 0:64], mix_at["w"][:, k, :], k == 0, k == KT - 1)
                            last = mm(bank[64:128, :], slot[:, k, 64:128], mix_at["a"][:, k, :], k == 0, k == KT - 1)
                            continue
                        if j == 0:
                            pe.wait_ge(mixed.handle, mixed.at(KT * mixes.index(what) + k + 1))
                        last = nc.tensor.matmul(bank[:, :], slot[:, k, :], mix_at[what][:, k, :], start=k == 0,
                                                stop=k == KT - 1)
                last.then_inc(tile_done.handle, 1)

            given = {"values": 0, "x": 0, "xu": 0, "pairs": 0, "turned": 0}

            def banks_01_read():
                pe.wait_ge(v_evac.handle, v_evac.at(2 * given["values"]))
                pe.wait_ge(xs_ready.handle, xs_ready.at(2 * given["x"]))
                pe.wait_ge(g_evac.handle, g_evac.at(4 * given["pairs"]))

            def banks_23_read():
                pe.wait_ge(us_ready.handle, us_ready.at(2 * given["xu"]))
                pe.wait_ge(g_evac.handle, g_evac.at(4 * given["pairs"]))
                pe.wait_ge(bkt_evac.handle, bkt_evac.at(2 * given["turned"]))

            def multiply_pairs(c, qs):
                for q in qs:
                    if c < BC and c > 0:
                        pe.wait_ge(g_evac.handle, g_evac.at(4 * (c - 1) + q + 1))
                    for k in range(2):
                        last = mm(g_bank(c, q)[:, 256 * k:256 * k + 256], bk[:, 2 * q + k, :],
                                  arz[:, 4 * q + 2 * k:4 * q + 2 * k + 2, :])
                    last.then_inc(g_done.handle, 1)

            def turn_bk(c):
                for q in range(2):
                    if c < BC and c > 0:
                        pe.wait_ge(bkt_evac.handle, bkt_evac.at(2 * (c - 1) + q + 1))
                    for k in range(4):
                        last = nc.tensor.transpose(t_bank(c, q)[:, P * k:P * k + P], bk[:, 4 * q + k, :], ident)
                    last.then_inc(bkt_done.handle, 1)

            def staged(c):
                pe.wait_ge(ark_staged.handle, ark_staged.at(c + 1))
                pe.wait_ge(b_staged.handle, b_staged.at(c + 1))

            def pairs_first(c):
                staged(c)
                banks_23_read()
                multiply_pairs(c, (0, 1))

            def pairs_second(c):
                banks_01_read()
                multiply_pairs(c, (2, 3))
                given["pairs"] = c + 1

            def pairs_turned(c):
                banks_23_read()
                turn_bk(c)
                given["turned"] = c + 1

            def turn_values(c):
                banks_01_read()
                for q in range(2):
                    for k in range(4):
                        last = nc.tensor.transpose(m.bank[q][LO, P * k:P * k + P], V[:, 4 * q + k, span(c)], ident)
                    last.then_inc(v_done.handle, 1)
                given["values"] = c + 1

            def x(c):
                banks_01_read()
                if c % BC == 0:
                    pe.wait_ge(t_placed.handle, t_placed.at(c // BC + 1))
                for g in range(2):
                    for k in range(4):
                        p = 4 * g + k
                        for par, rows in SIDES:
                            last = mm(m.bank[g][rows, C * k:C * k + C], gs[c][rows, 0, 2 * p + par, :], tu[c][rows, p, 0:C])
                    last.then_inc(x_done.handle, 1)
                given["x"] = c + 1

            def xu(c):
                banks_23_read()
                if c % BC == 0:
                    pe.wait_ge(u_placed.handle, u_placed.at(c // BC + 1))
                for g in range(2):
                    pe.wait_ge(xs_ready.handle, xs_ready.at(2 * c + g + 1))
                    for k in range(4):
                        p = 4 * g + k
                        last = mm(m.bank[2 + g][:, C * k:C * k + C], xs[:, p, :], tu[c][:, p, C:P])
                    last.then_inc(xu_done.handle, 1)
                given["xu"] = c + 1

            def right_side(c):
                for g in range(2):
                    pe.wait_ge(v_evac.handle, v_evac.at(2 * c + g + 1))
                    if c >= 2:
                        pe.wait_ge(z_cleared.handle, z_cleared.at(c - 1))
                    if c >= 1:
                        pe.wait_ge(y_evac.handle, y_evac.at(2 * (c - 1) + g + 1))
                    bank = m.bank[4 + g]
                    for p in range(4 * g, 4 * g + 4):
                        at = P * (p % 4)
                        mm(bank[:, at:at + P], gs[c][:, 0, 2 * p:2 * p + 2, :], z[c][:, 2 * p:2 * p + 2, :], p % 4 == 0, False)
                    if c >= 1:
                        pe.wait_ge(s_ready.handle, s_ready.at(2 * (c - 1) + g + 1))
                    for p in range(4 * g, 4 * g + 4):
                        for par, rows in SIDES:
                            at = P * (p % 4) + C * par
                            last = mm(bank[rows, at:at + C], KK[rows, p, span(c)], S[rows, p, :], False, p % 4 == 3)
                    last.then_inc(rhs_done.handle, 1)

            def solve(c):
                for g in range(2):
                    pe.wait_ge(rhs_evac.handle, rhs_evac.at(2 * c + g + 1))
                    pe.wait_ge(us_ready.handle, us_ready.at(2 * c + g + 1))
                    for k in range(4):
                        p = 4 * g + k
                        last = mm(m.bank[6 + g][:, C * k:C * k + C], us[:, p, :], rhs[:, p, :])
                    last.then_inc(sa_done.handle, 1)

            def outputs(c):
                for g in range(2):
                    bank = m.bank[4 + g]
                    for p in range(4 * g, 4 * g + 4):
                        for par, rows in SIDES:
                            at = P * (p % 4) + C * par
                            mm(bank[rows, at:at + C], S[rows, p, :], L[rows, p, span(c)], p % 4 == 0, False)
                    pe.wait_ge(sa_evac.handle, sa_evac.at(2 * c + g + 1))
                    for p in range(4 * g, 4 * g + 4):
                        at = P * (p % 4)
                        last = mm(bank[:, at:at + P], z[c][:, 2 * p:2 * p + 2, :], gs[c][:, 1, 2 * p:2 * p + 2, :], False, p % 4 == 3)
                    last.then_inc(y_done.handle, 1)
                    for k in range(4):
                        p = 4 * g + k
                        for par, rows in SIDES:
                            last = mm(m.bank[6 + g][rows, C * k:C * k + C], (BB, K)[par][:, p, span(c)], z[c][:, 2 * p + par, :])
                    last.then_inc(s_done.handle, 1)

            for n in range(place["v", 0]):
                project(n)
            pe.wait_ge(act_done.handle, act_done.at(place["v", 0]))
            for c in range(BC):
                staged(c)
                multiply_pairs(c, range(4))
                turn_bk(c)
                project(place["v", c])
            given.update(pairs=BC, turned=BC)
            for n in range(place["v", BC], len(tiles)):
                project(n)
            turn_values(0)
            x(0)
            xu(0)
            pe.wait_ge(gated.handle, gated.at(KT))
            for c in range(NC):
                right_side(c)
                if c + 1 < NC:
                    turn_values(c + 1)
                extra = {0: 4, 1: 6, 2: 7}.get(c)
                if extra:
                    pairs_first(extra)
                solve(c)
                if extra:
                    pairs_second(extra)
                outputs(c)
                if extra:
                    pairs_turned(extra)
                if c + 1 < NC:
                    x(c + 1)
                    xu(c + 1)
                if c == 0:
                    pairs_first(5)
                    pairs_second(5)
                    pairs_turned(5)
    for s, n in ((mixed, 6 * KT), (tile_done, len(tiles)), (act_done, len(tiles)), (gated, KT), (kk_squared, KT),
                 (chain, links[0]), (act_chain, 1), (aux, 48), (root_used, KT), (sig_used, KT), (keys_ready, 1),
                 (h_spilled, 16), (g_spilled, 16), (reloaded, 32), (ep_cleared, 1), (exp_ready, NC), (ar_scaled, NC),
                 (ark_staged, NC), (b_scaled, NC), (k_scaled, NC), (b_staged, NC), (g_done, 4 * NC), (g_evac, 4 * NC),
                 (bkt_done, 2 * NC), (bkt_evac, 2 * NC), (gathered, 2), (step, steps[0]), (t_turned, 2), (u_turned, 2),
                 (tu_cleared, 1), (t_placed, 2), (u_placed, 2), (carry_cleared, 1), (z_cleared, NC - 2)):
        s.base += n
    for s in (v_done, v_evac, x_done, xs_ready, xu_done, us_ready, s_added, rhs_done, rhs_evac, sa_done, sa_evac, y_done,
              y_evac, s_done, s_ready):
        s.base += 2 * NC


def rw_gate(m, prm):
    nc = m.nc
    R, V, G, Y = (m.view(b, KT, T) for b in (B_R, B_V, B_G, B_KK))
    sq = m.view(B_A, KT, T)
    sd = m.view(B_L, KT, T)
    bones_rk = m.view(A_XT, KT, P)
    bones = m.view(A_CONST + C_BONES, P)
    eps = m.view(A_SMALL + 40, 1)
    col = lambda at, k: m.view(prm + at + k, 1)
    tiles = [("mean", j) for j in range(KT)] + [(w, j) for j in range(KT) for w in ("var", "bonus")]
    place = {t: n for n, t in enumerate(tiles)}
    done, rr, centred, squared, root, gated, chain = (m.sem(n) for n in (
        "sums_done", "rr_ready", "centred", "squared", "root_ready", "bonus_used", "dve_chain"))
    count = [0]
    with nc.Block() as block:
        @block.scalar
        def _(act):
            act.wait_ge(rr.handle, rr.at(1))
            for j in range(KT):
                act.wait_ge(centred.handle, centred.at(j + 1))
                nc.scalar.activation(sq[:, j, :], Y[:, j, :], ACT.Square).then_inc(squared.handle, 1)
            for j in range(KT):
                n = place["var", j]
                act.wait_ge(done.handle, done.at(n + 1))
                nc.scalar.activation(sd[:, j, :], m.bank[n % 8][:, :], ACT.Sqrt, bias=eps, scale=1.0 / C)\
                    .then_inc(root.handle, 1)

        @block.vector
        def _(dve):
            def link(ins):
                count[0] += 1
                ins.then_inc(chain.handle, 1)
                dve.wait_ge(chain.handle, chain.at(count[0]))

            nc.vector.memset(eps, 64e-5).then_inc(rr.handle, 1)
            for j in range(KT):
                dve.wait_ge(done.handle, done.at(j + 1))
                nc.vector.scalar_tensor_tensor(out=Y[:, j, :], in0=m.bank[j][:, :], scalar=-1.0 / C, in1=Y[:, j, :],
                                               op0=ALU.mult, op1=ALU.add).then_inc(centred.handle, 1)
            for j in range(KT):
                nc.vector.tensor_scalar(bones_rk[:, j, :], bones, col(RW_RK, j), None, ALU.mult).then_inc(rr.handle, 1)
            for j in range(KT):
                dve.wait_ge(root.handle, root.at(j + 1))
                link(nc.vector.reciprocal(sd[:, j, :], sd[:, j, :]))
                nc.vector.scalar_tensor_tensor(out=Y[:, j, :], in0=Y[:, j, :], scalar=col(RW_LNG, j), in1=sd[:, j, :],
                                               op0=ALU.mult, op1=ALU.mult)
                n = place["bonus", j]
                dve.wait_ge(done.handle, done.at(n + 1))
                ins = nc.vector.tensor_tensor(V[:, j, :], m.bank[n % 8][:, :], V[:, j, :], ALU.mult)
                ins.then_inc(gated.handle, 1)
                dve.wait_ge(gated.handle, gated.at(j + 1))
                link(nc.vector.scalar_tensor_tensor(out=Y[:, j, :], in0=Y[:, j, :], scalar=col(RW_LNB, j), in1=V[:, j, :],
                                                    op0=ALU.add, op1=ALU.add))
                nc.vector.tensor_tensor(Y[:, j, :], Y[:, j, :], G[:, j, :], ALU.mult)

        @block.tensor
        def _(pe):
            for n, (what, j) in enumerate(tiles):
                if what == "var":
                    pe.wait_ge(squared.handle, squared.at(j + 1))
                    if j >= 4:
                        pe.wait_ge(root.handle, root.at(j - 3))
                if what == "bonus":
                    pe.wait_ge(rr.handle, rr.at(j + 2))
                    if j >= 4:
                        pe.wait_ge(gated.handle, gated.at(j - 3))
                    else:
                        pe.wait_ge(centred.handle, centred.at(2 * j + 2))
                src = {"mean": Y, "var": sq, "bonus": R}[what][:, j, :]
                nc.tensor.matmul(m.bank[n % 8][:, :], bones_rk[:, j, :] if what == "bonus" else bones, src, start=True,
                                 stop=True).then_inc(done.handle, 1)
    for s, n in ((done, len(tiles)), (rr, KT + 1), (centred, KT), (squared, KT), (root, KT), (gated, KT), (chain, count[0])):
        s.base += n


def stage_out(m, y_at, n0):
    nc = m.nc
    Y = m.view(y_at, KT, T)
    h = m.view(A_H, NT, D)
    done, rows_used = m.sem("out_done"), m.sem("out_rows_used")
    m.used_by += [(rows_used.handle, rows_used.at(k + 1)) for k in range(KT - 1)] + [(done.handle, done.at(8))]
    with nc.Block() as block:
        @block.sync
        def _(sp):
            m.load_weights(sp, n0 + KT + SLOTS)

        @block.tensor
        def _(pe):
            for k in range(KT):
                m.weights_arrived(pe, n0 + k)
                slot = m.view(m.slot(n0 + k), D)
                for a in range(NT):
                    for half in range(2):
                        last = nc.tensor.matmul(m.bank[2 * a + half][:, :], Y[:, k, a * P:(a + 1) * P],
                                                slot[:, half * 512:half * 512 + 512], start=k == 0, stop=k == KT - 1)
                        if k == KT - 1:
                            last.then_inc(done.handle, 1)
                if k < KT - 1:
                    last.then_inc(rows_used.handle, 1)

        @block.vector
        def _(dve):
            for n in range(8):
                dve.wait_ge(done.handle, done.at(n + 1))
                part = h[:, n // 2, 512 * (n % 2):512 * (n % 2) + 512]
                nc.vector.tensor_tensor(part, part, m.bank[n][:, :], ALU.add)
    done.base += 8
    rows_used.base += KT - 1


def stage_store(m, final_g, out):
    nc = m.nc
    h = m.view(A_H, NT, D)
    tmp = m.view(B_R, NT, D)
    fg = m.view(B_K, D)
    ss = m.view(A_SMALL, NT)
    loaded, squared, root, inverse, ready, stored = (m.sem(n) for n in (
        "final_g_loaded", "norm_squared", "norm_root", "norm_inverse", "result_ready", "stored"))
    with nc.Block() as block:
        @block.scalar
        def _(act):
            for a in range(NT):
                ins = nc.scalar.activation(tmp[:, a, :], h[:, a, :], ACT.Square, accum_out=ss[:, a:a + 1])
            ins.then_inc(squared.handle, 1)
            act.wait_ge(inverse.handle, inverse.at(1))
            nc.scalar.activation(ss, ss, ACT.Sqrt).then_inc(root.handle, 1)

        @block.vector
        def _(dve):
            dve.wait_ge(squared.handle, squared.at(1))
            nc.vector.tensor_scalar(ss, ss, 1.0 / D, 1e-6, ALU.mult, ALU.add).then_inc(inverse.handle, 1)
            dve.wait_ge(root.handle, root.at(1))
            nc.vector.reciprocal(ss, ss).then_inc(inverse.handle, 1)
            dve.wait_ge(inverse.handle, inverse.at(2))
            dve.wait_ge(loaded.handle, loaded.at(16))
            for a in range(NT):
                nc.vector.scalar_tensor_tensor(out=h[:, a, :], in0=h[:, a, :], scalar=ss[:, a:a + 1], in1=fg,
                                               op0=ALU.mult, op1=ALU.mult).then_inc(ready.handle, 1)

        @block.sync
        def _(sp):
            sp.dma_start(fg, final_g.unsqueeze(0).to_broadcast([P, D])).then_inc(loaded.handle, 16)
            for a in range(NT):
                sp.wait_ge(ready.handle, ready.at(a + 1))
                sp.dma_start(out[0, a * P:(a + 1) * P, :], h[:, a, :]).then_inc(stored.handle, 16)
            sp.wait_ge(stored.handle, 16 * NT)


S_QKV = B_R
S_VS = S_QKV + 6144
S_QT = S_VS + 768
S_KT = S_QT + 4096
S_G = S_KT + 1024
S_Y = S_G + 4096
S_P = S_Y + 4096
S_PT = S_P + 2048
S_SK = S_PT + 1024
S_ROPE = S_SK + 64
SW_KV = 4


def sw_project(m, sinks, n0):
    nc = m.nc
    xt = m.view(A_XT, KT, T + 1)
    qkv = m.view(S_QKV, NT, 1536)
    vs = m.view(S_VS, 3, 256)
    qt, kt, G = m.view(S_QT, 8, T), m.view(S_KT, 2, T), m.view(S_G, KT, T)
    sk = m.view(S_SK, 8)
    rope = [m.view(S_ROPE + 160 * n, 20, 8) for n in range(4)]
    rtab = m.view(A_CONST + C_ROPE, 2, NT, 8)
    ident = m.view(A_CONST + C_ID, P)
    rows_used, q_done, qkv_evac, g_done, sig_done, g_used, turned, turn_evac, chain, sink, rotated = (m.sem(n) for n in (
        "sw_rows_used", "qkv_done", "qkv_evac", "tile_done", "act_evacuated", "g_gated", "qk_turned", "qk_evac",
        "dve_chain", "sinks_loaded", "rotated"))
    m.used_by += [(rows_used.handle, rows_used.at(k + 1)) for k in range(7)] + [(q_done.handle, q_done.at(8))]
    m.used_by += [(rows_used.handle, rows_used.at(7 + k + 1)) for k in range(3)] + [(q_done.handle, q_done.at(12))]
    m.used_by += [(g_done.handle, g_done.at(k + 1)) for k in range(KT)]
    count = [0]
    with nc.Block() as block:
        @block.sync
        def _(sp):
            sp.dma_start(sk[0:64, :], sinks[0:8].unsqueeze(0).to_broadcast([64, 8])).then_inc(sink.handle, 16)
            sp.dma_start(sk[64:128, :], sinks[8:16].unsqueeze(0).to_broadcast([64, 8])).then_inc(sink.handle, 16)
            m.load_weights(sp, n0 + 20 + SLOTS)

        @block.tensor
        def _(pe):
            w = n0
            for k in range(KT):
                m.weights_arrived(pe, w)
                slot = m.view(m.slot(w), D)
                for n in range(8):
                    last = nc.tensor.matmul(m.bank[n][:, :], xt[:, k, 1 + (n // 2) * P:1 + (n // 2 + 1) * P],
                                            slot[:, 512 * (n % 2):512 * (n % 2) + 512], start=k == 0, stop=k == KT - 1)
                    if k == KT - 1:
                        last.then_inc(q_done.handle, 1)
                if k < KT - 1:
                    last.then_inc(rows_used.handle, 1)
                w += 1
            for k2 in range(KT // 2):
                m.weights_arrived(pe, w)
                slot = m.view(m.slot(w), 2, 512)
                for n in range(NT):
                    if k2 == 0:
                        pe.wait_ge(qkv_evac.handle, qkv_evac.at(n + 1))
                    for k in range(2):
                        last = nc.tensor.matmul(m.bank[n][:, :], xt[:, 2 * k2 + k, 1 + n * P:1 + (n + 1) * P], slot[:, k, :],
                                                start=(k2, k) == (0, 0), stop=(k2, k) == (KT // 2 - 1, 1))
                    if k2 == KT // 2 - 1:
                        last.then_inc(q_done.handle, 1)
                if k2 < KT // 2 - 1:
                    last.then_inc(rows_used.handle, 1)
                w += 1
            for j in range(KT):
                m.weights_arrived(pe, w)
                slot = m.view(m.slot(w), KT, P)
                if j < 4:
                    pe.wait_ge(qkv_evac.handle, qkv_evac.at(4 + j + 1))
                else:
                    pe.wait_ge(g_used.handle, g_used.at(j - 3))
                for k in range(KT):
                    last = nc.tensor.matmul(m.bank[4 + j % 4][:, :], slot[:, k, :], xt[:, k, 1:T + 1], start=k == 0,
                                            stop=k == KT - 1)
                last.then_inc(g_done.handle, 1)
                w += 1
            for n in range(10):
                if n < 4:
                    pe.wait_ge(qkv_evac.handle, qkv_evac.at(12))
                    pe.wait_ge(rotated.handle, rotated.at(NT))
                else:
                    pe.wait_ge(turn_evac.handle, turn_evac.at(n - 3))
                for a in range(NT):
                    last = nc.tensor.transpose(m.bank[n % 4][:, a * P:(a + 1) * P], qkv[:, a, n * P:(n + 1) * P], ident)
                last.then_inc(turned.handle, 1)

        @block.scalar
        def _(act):
            for n in range(8):
                act.wait_ge(q_done.handle, q_done.at(n + 1))
                nc.scalar.activation(qkv[:, n // 2, 0:D].rearrange("p (h f c) -> p h f c", f=2, c=C)[:, :, n % 2, :],
                                     m.bank[n][:, :].rearrange("p (h c) -> p h c", c=C), ACT.Copy).then_inc(qkv_evac.handle, 1)
            for n in range(4):
                act.wait_ge(q_done.handle, q_done.at(8 + n + 1))
                for f in range(2):
                    nc.scalar.activation(qkv[:, n, D:D + 256].rearrange("p (h f c) -> p h f c", f=2, c=C)[:, :, f, :],
                                         m.bank[n][:, P * f:P * f + P].rearrange("p (h c) -> p h c", c=C), ACT.Copy)
                nc.scalar.activation(qkv[:, n, D + 256:D + 512], m.bank[n][:, 256:512], ACT.Copy).then_inc(qkv_evac.handle, 1)
            for j in range(KT):
                act.wait_ge(g_done.handle, g_done.at(j + 1))
                nc.scalar.activation(G[:, j, :], m.bank[4 + j % 4][:, :], ACT.Sigmoid).then_inc(sig_done.handle, 1)
            for n in range(10):
                act.wait_ge(turned.handle, turned.at(n + 1))
                nc.scalar.activation(qt[:, n, :] if n < 8 else kt[:, n - 8, :], m.bank[n % 4][:, :], ACT.Copy)\
                    .then_inc(turn_evac.handle, 1)

        @block.vector
        def _(dve):
            def link(ins):
                count[0] += 1
                ins.then_inc(chain.handle, 1)
                dve.wait_ge(chain.handle, chain.at(count[0]))

            for a in range(NT):
                dve.wait_ge(qkv_evac.handle, qkv_evac.at(8 + a + 1))
                qk = qkv[:, a, 0:1280].rearrange("p (h c) -> p h c", c=C)
                x1, x2 = qk[:, :, 0:8], qk[:, :, 8:16]
                cos, sin = (rtab[:, n, a, :].unsqueeze(1).to_broadcast([P, 20, 8]) for n in range(2))
                for n, (u, v) in enumerate(((x1, cos), (x2, sin), (x2, cos), (x1, sin))):
                    ins = nc.vector.tensor_tensor(rope[n], u, v, ALU.mult)
                link(ins)
                nc.vector.tensor_tensor(x1, rope[0], rope[1], ALU.subtract)
                nc.vector.tensor_tensor(x2, rope[2], rope[3], ALU.add).then_inc(rotated.handle, 1)
                dve.wait_ge(rotated.handle, rotated.at(a + 1))
            for i in range(3):
                nc.vector.tensor_copy(vs[0:64, i, :], qkv[64:128, i, 1280:1536])
                nc.vector.tensor_copy(vs[64:128, i, :], qkv[0:64, i + 1, 1280:1536])
            for j in range(KT):
                dve.wait_ge(sig_done.handle, sig_done.at(j + 1))
                nc.vector.tensor_tensor(G[:, j, :], m.bank[4 + j % 4][:, :], G[:, j, :], ALU.mult).then_inc(g_used.handle, 1)
    for s, n in ((rows_used, 10), (q_done, 12), (qkv_evac, 12), (g_done, KT), (sig_done, KT), (g_used, KT), (turned, 10),
                 (turn_evac, 10), (chain, count[0]), (sink, 32), (rotated, NT)):
        s.base += n


def sw_attend(m):
    nc = m.nc
    qkv = m.view(S_QKV, NT, 1536)
    vs = m.view(S_VS, 3, 256)
    qt, kt, G, Y = m.view(S_QT, 8, T), m.view(S_KT, 2, T), m.view(S_G, KT, T), m.view(S_Y, KT, T)
    prob = [m.view(S_P + 1024 * n, 8, P) for n in range(2)]
    pt = m.view(S_PT, 8, P)
    sk = m.view(S_SK, 8)
    small = [m.view(S_ROPE + 64 * n, 8, 8) for n in range(2)]
    ident = m.view(A_CONST + C_ID, P)
    s_done, s_max, s_exp, es_done, normed, p_turned, p_evac, o_done, o_evac, chain, sink = (m.sem(n) for n in (
        "scores_done", "score_max", "scores_exp", "sink_exp", "probs_normed", "probs_turned", "probs_evac", "o_done",
        "o_evac", "dve_chain", "sinks_loaded"))
    count = [0]
    keys = lambda c: C if c == 0 else P
    with nc.Block() as block:
        def gate(dve, c):
            dve.wait_ge(o_done.handle, o_done.at(c + 1))
            nc.vector.tensor_tensor(Y[:, :, c * C:(c + 1) * C], m.bank[6 + c % 2][:, :].rearrange("p (k t) -> p k t", t=C),
                                    G[:, :, c * C:(c + 1) * C], ALU.mult).then_inc(o_evac.handle, 1)

        def evac(act, c):
            for q in range(2):
                act.wait_ge(p_turned.handle, p_turned.at(2 * c + q + 1))
                if q == 0 and c >= 1:
                    act.wait_ge(o_done.handle, o_done.at(c))
                nc.scalar.activation(pt[0:keys(c), 4 * q:4 * q + 4, :], m.bank[4 + q][0:keys(c), :], ACT.Copy)\
                    .then_inc(p_evac.handle, 1)

        @block.tensor
        def _(pe):
            def scores(c):
                if c >= 2:
                    pe.wait_ge(s_exp.handle, s_exp.at(c - 1))
                for h in range(8):
                    bank = m.bank[2 * (c % 2) + h // 4]
                    for f, rows in ((0, slice(0, 64)), (1, slice(64, 128))):
                        last = nc.tensor.matmul(bank[rows, P * (h % 4):P * (h % 4) + keys(c)], qt[rows, h, c * C:(c + 1) * C],
                                                kt[rows, h // 4, (c + 1) * C - keys(c):(c + 1) * C], start=True, stop=True,
                                                skip_group_check=True)
                last.then_inc(s_done.handle, 1)

            scores(0)
            for c in range(NC):
                if c + 1 < NC:
                    scores(c + 1)
                pe.wait_ge(normed.handle, normed.at(c + 1))
                for q in range(2):
                    if c >= 1:
                        pe.wait_ge(p_evac.handle, p_evac.at(2 * c - 1 + q))
                    for k in range(4):
                        last = nc.tensor.transpose(m.bank[4 + q][0:keys(c), P * k:P * k + P], prob[c % 2][:, 4 * q + k, 0:keys(c)],
                                                   ident)
                    last.then_inc(p_turned.handle, 1)
                if c >= 2:
                    pe.wait_ge(o_evac.handle, o_evac.at(c - 1))
                v = qkv[:, c // 2, 1280:1536] if c % 2 or c == 0 else vs[:, c // 2 - 1, :]
                pe.wait_ge(p_evac.handle, p_evac.at(2 * c + 2))
                for h in range(8):
                    for f in range(2):
                        out = slice(64 * (h % 2), 64 * (h % 2) + 64)
                        kv = h // 4 + 2 * f
                        at = C * (h // 2 + 4 * f)
                        last = nc.tensor.matmul(m.bank[6 + c % 2][out, at:at + C], v[0:keys(c), C * kv:C * kv + C],
                                                pt[0:keys(c), h, C * f:C * f + C], start=True, stop=True, skip_group_check=True)
                last.then_inc(o_done.handle, 1)

        @block.scalar
        def _(act):
            for c in range(NC):
                p, st = prob[c % 2], small[c % 2]
                act.wait_ge(s_max.handle, s_max.at(c + 1))
                if c >= 2:
                    act.wait_ge(p_turned.handle, p_turned.at(2 * (c - 1)))
                nc.scalar.activation(st[:, 2, :], st[:, 1, :], ACT.Exp)
                for h in range(8):
                    bank = m.bank[2 * (c % 2) + h // 4]
                    last = nc.scalar.activation(p[:, h, 0:keys(c)], bank[:, P * (h % 4):P * (h % 4) + keys(c)], ACT.Exp,
                                                bias=st[:, 0, h:h + 1], scale=C ** -0.5, accum_out=st[:, 3, h:h + 1])
                last.then_inc(s_exp.handle, 1)
                if c >= 1:
                    evac(act, c - 1)
            evac(act, NC - 1)


        @block.vector
        def _(dve):
            def link(ins):
                count[0] += 1
                ins.then_inc(chain.handle, 1)
                dve.wait_ge(chain.handle, chain.at(count[0]))

            def maxima(c):
                st = small[c % 2]
                dve.wait_ge(s_done.handle, s_done.at(c + 1))
                for q in range(2):
                    bank = m.bank[2 * (c % 2) + q][:, :].rearrange("p (h k) -> p h k", k=P)[:, :, 0:keys(c)]
                    ins = nc.vector.tensor_reduce(st[:, 0, 4 * q:4 * q + 4], bank, AX.X, ALU.max)
                link(ins)
                link(nc.vector.tensor_scalar(st[:, 0, :], st[:, 0, :], C ** -0.5, None, ALU.mult))
                link(nc.vector.tensor_tensor(st[:, 0, :], st[:, 0, :], sk, ALU.max))
                link(nc.vector.tensor_tensor(st[:, 1, :], sk, st[:, 0, :], ALU.subtract))
                nc.vector.tensor_scalar(st[:, 0, :], st[:, 0, :], -1.0, None, ALU.mult).then_inc(s_max.handle, 1)

            dve.wait_ge(sink.handle, sink.at(0))
            maxima(0)
            for c in range(NC):
                st, p = small[c % 2], prob[c % 2]
                if c + 1 < NC:
                    maxima(c + 1)
                dve.wait_ge(s_exp.handle, s_exp.at(c + 1))
                link(nc.vector.tensor_tensor(st[:, 3, :], st[:, 3, :], st[:, 2, :], ALU.add))
                link(nc.vector.reciprocal(st[:, 3, :], st[:, 3, :]))
                nc.vector.tensor_tensor(p[:, :, 0:keys(c)], p[:, :, 0:keys(c)], st[:, 3, :].unsqueeze(2).to_broadcast([P, 8, keys(c)]),
                                        ALU.mult).then_inc(normed.handle, 1)
                if c >= 1:
                    gate(dve, c - 1)
            gate(dve, NC - 1)

    for s, n in ((s_done, NC), (s_max, NC), (s_exp, NC), (normed, NC), (p_turned, 2 * NC), (p_evac, 2 * NC), (o_done, NC),
                 (o_evac, NC), (chain, count[0])):
        s.base += n


ML_H, ML_V = 4, 256
M_U = B_R
M_C = M_U + KT * (T + 3)
M_Z = M_C + 4096
M_V = M_Z + 4096
M_HM = M_V + NT * ML_H * (ML_V + 1)
M_Q = M_HM + 4096
M_K = M_Q + 2048
M_QS = M_K + 2048
M_E = M_QS + 2048
M_SI = M_E + 2048
M_KTOK = M_SI + 2048
M_STATE = M_KTOK + 2048
M_SM = M_STATE + ML_H * (ML_V + 1)
M_XT = A_END - KT * (T + 1)
M_ROWS = M_HM
M_Y = M_U


def ml_project(m, w_if, i_bias, f_bias, rows_src, n0):
    nc = m.nc
    xt = m.view(M_XT, KT, T + 1)
    U = m.view(M_U, KT, T + 3)
    cc, Z = m.view(M_C, KT, T), m.view(M_Z, KT, T)
    V = m.view(M_V, NT * ML_H, ML_V + 1)
    q, k = m.view(M_Q, ML_H, T), m.view(M_K, ML_H, T)
    tmp = m.view(M_E, T)
    sig = [m.view(M_SI + 512 * n, T) for n in range(2)]
    gw = m.view(M_ROWS, KT, 8)
    gates = m.view(M_SM, NT, 8)
    bias = m.view(M_SM + 32, 2, rows=slice(0, 4))
    consts = m.view(M_ROWS + 64, 3, T, rows=slice(0, 4))
    gi = m.view(M_ROWS + 64 + 3 * T, 2, T, rows=slice(0, 4))
    ident = m.view(A_CONST + C_ID, P)
    prm = A_PT + 128
    col = lambda at, j: m.view(prm + at + j, 1)
    done, act_done, z_used, conv_done, sig_ready, rows_used, aux, v_done, chain, c_ready, sig_free = (m.sem(n) for n in (
        "tile_done", "act_evacuated", "g_gated", "conv_done", "sig_ready", "out_rows_used", "aux_loaded", "v_rows_done",
        "dve_chain", "c_ready", "sig_used"))
    v_evac = m.sem("v_rows_evac")
    tiles = [("gates", 0), ("gates_t", 0)] + [("u", j) for j in range(KT)] + [("z", j) for j in range(KT)]
    tiles += [(w, h) for w in "qk" for h in range(ML_H)]
    place = {t: n for n, t in enumerate(tiles)}
    m.used_by += [(done.handle, done.at(place["u", j] + 1)) for j in range(KT)]
    m.used_by += [(done.handle, done.at(place["z", j] + 1)) for j in range(KT)]
    m.used_by += [(done.handle, done.at(place[w, 3] + 1)) for w in "qk"]
    m.used_by += [(rows_used.handle, rows_used.at(n + 1)) for n in range(7)] + [(v_done.handle, v_done.at(8))]
    count = [0]
    with nc.Block() as block:
        def conv_sig(act, j):
            act.wait_ge(conv_done.handle, conv_done.at(j + 1))
            if j >= 2:
                act.wait_ge(c_ready.handle, c_ready.at(j - 1))
            nc.scalar.activation(sig[j % 2], cc[:, j, :], ACT.Sigmoid, bias=col(ML_CB, j)).then_inc(sig_ready.handle, 1)

        @block.sync
        def _(sp):
            with nc.allow_non_contiguous_dma(reason="eight columns of gate weights, four biases"):
                sp.dma_start(gw, w_if.rearrange("(k p) n -> p k n", p=P)).then_inc(aux.handle, 16)
                sp.dma_start(bias[:, 0:1], i_bias.unsqueeze(1)).then_inc(aux.handle, 16)
                sp.dma_start(bias[:, 1:2], f_bias.unsqueeze(1)).then_inc(aux.handle, 16)
            sp.dma_start(consts, rows_src).then_inc(aux.handle, 16)
            m.load_weights(sp, n0 + 26 + SLOTS)

        @block.tensor
        def _(pe):
            w = n0
            pe.wait_ge(aux.handle, aux.at(64))
            for n, (what, j) in enumerate(tiles):
                bank = m.bank[n % 8]
                if n >= 8:
                    before = tiles[n - 8]
                    if before[0] == "z":
                        pe.wait_ge(z_used.handle, z_used.at(before[1] + 1))
                    else:
                        pe.wait_ge(act_done.handle, act_done.at(n - 7))
                if what == "gates":
                    for a in range(NT):
                        for c in range(KT):
                            last = nc.tensor.matmul(bank[:, 8 * a:8 * a + 8], xt[:, c, 1 + a * P:1 + (a + 1) * P], gw[:, c, :],
                                                    start=c == 0, stop=c == KT - 1)
                elif what == "gates_t":
                    pe.wait_ge(act_done.handle, act_done.at(1))
                    for f in range(2):
                        for a in range(NT):
                            last = nc.tensor.transpose((bank if f == 0 else m.bank[7])[0:4, a * P:(a + 1) * P],
                                                       gates[:, a, 4 * f:4 * f + 4], ident)
                elif what in "uz":
                    if (what, j) == ("u", 5):
                        pe.wait_ge(act_done.handle, act_done.at(2))
                    m.weights_arrived(pe, w)
                    slot = m.view(m.slot(w), KT, P)
                    for c in range(KT):
                        last = nc.tensor.matmul(bank[:, :], slot[:, c, :], xt[:, c, 1:T + 1], start=c == 0, stop=c == KT - 1)
                    w += 1
                else:
                    if j == 0:
                        m.weights_arrived(pe, w)
                        slot = m.view(m.slot(w), KT, P)
                        w += 1
                    pe.wait_ge(c_ready.handle, c_ready.at(KT))
                    for e in range(2):
                        last = nc.tensor.matmul(bank[:, :], slot[:, 2 * j + e, :], cc[:, 2 * j + e, :], start=e == 0, stop=e == 1)
                last.then_inc(done.handle, 1)
            pe.wait_ge(act_done.handle, act_done.at(len(tiles)))
            pe.wait_ge(z_used.handle, z_used.at(KT))
            for c in range(KT):
                m.weights_arrived(pe, w)
                slot = m.view(m.slot(w), D)
                for n in range(8):
                    last = nc.tensor.matmul(m.bank[n][:, :], xt[:, c, 1 + (n // 2) * P:1 + (n // 2 + 1) * P],
                                            slot[:, 512 * (n % 2):512 * (n % 2) + 512], start=c == 0, stop=c == KT - 1)
                    if c == KT - 1:
                        last.then_inc(v_done.handle, 1)
                if c < KT - 1:
                    last.then_inc(rows_used.handle, 1)
                w += 1

        @block.scalar
        def _(act):
            for n, (what, j) in enumerate(tiles):
                bank = m.bank[n % 8]
                act.wait_ge(done.handle, done.at(n + 1))
                if what == "gates":
                    out = nc.scalar.activation(m.view(M_SM, 32), bank[:, 0:32], ACT.Copy)
                elif what == "gates_t":
                    act.wait_ge(aux.handle, aux.at(64))
                    nc.scalar.activation(gi[:, 0, :], bank[0:4, :], ACT.Identity, bias=bias[:, 0:1])
                    out = nc.scalar.activation(gi[:, 1, :], m.bank[7][0:4, :], ACT.Identity, bias=bias[:, 1:2])
                elif what == "u":
                    out = nc.scalar.activation(U[:, j, 3:T + 3], bank[:, :], ACT.Copy)
                elif what == "z":
                    if j >= 1:
                        conv_sig(act, j - 1)
                    out = nc.scalar.activation(Z[:, j, :], bank[:, :], ACT.Sigmoid)
                elif what == "q":
                    out = nc.scalar.activation(q[:, j, :], bank[:, :], ACT.Copy)
                else:
                    out = nc.scalar.activation(k[:, j, :], bank[:, :], ACT.Copy, scale=P ** -0.5)
                out.then_inc(act_done.handle, 1)
                if (what, j) == ("z", KT - 1):
                    conv_sig(act, KT - 1)
            for n in range(8):
                act.wait_ge(v_done.handle, v_done.at(n + 1))
                nc.scalar.activation(V[:, 2 * n:2 * n + 2, 0:ML_V], m.bank[n][:, :].rearrange("p (h c) -> p h c", h=2), ACT.Copy)


        @block.vector
        def _(dve):
            def link(ins):
                count[0] += 1
                ins.then_inc(chain.handle, 1)
                dve.wait_ge(chain.handle, chain.at(count[0]))

            nc.vector.memset(V[:, :, ML_V:ML_V + 1], 1.0)
            link(nc.vector.memset(U[:, :, 0:3], 0.0))

            def gate(j):
                dve.wait_ge(sig_ready.handle, sig_ready.at(j + 1))
                nc.vector.scalar_tensor_tensor(out=cc[:, j, :], in0=cc[:, j, :], scalar=col(ML_CB, j), in1=sig[j % 2],
                                               op0=ALU.add, op1=ALU.mult).then_inc(c_ready.handle, 1)

            def z_gate(j):
                n = place["z", j]
                dve.wait_ge(act_done.handle, act_done.at(n + 1))
                nc.vector.tensor_tensor(Z[:, j, :], m.bank[n % 8][:, :], Z[:, j, :], ALU.mult).then_inc(z_used.handle, 1)

            for j in range(KT):
                dve.wait_ge(act_done.handle, act_done.at(place["u", j] + 1))
                link(nc.vector.tensor_scalar(cc[:, j, :], U[:, j, 0:T], col(ML_CW, j), None, ALU.mult))
                for i in range(1, 4):
                    ins = nc.vector.scalar_tensor_tensor(out=cc[:, j, :], in0=U[:, j, i:i + T], scalar=col(ML_CW + 8 * i, j),
                                                         in1=cc[:, j, :], op0=ALU.mult, op1=ALU.add)
                    if i < 3:
                        link(ins)
                ins.then_inc(conv_done.handle, 1)
            for j in range(KT):
                z_gate(j)
                gate(j)
    for s, n in ((done, len(tiles)), (act_done, len(tiles)), (z_used, KT), (conv_done, KT), (sig_ready, KT), (rows_used, 7),
                 (aux, 64), (v_done, 8), (chain, count[0]), (c_ready, KT)):
        s.base += n


def ml_gates(m):
    nc = m.nc
    one = slice(0, 4)
    consts = m.view(M_ROWS + 64, 3, T, rows=one)
    at = M_ROWS + 64 + 3 * T
    li, lf, b, mx = (m.view(at + n * T, T, rows=one) for n in range(4))
    sel = consts[:, 2, :].rearrange("p (h n) -> p h n", n=P)
    small = m.view(M_SM + 40, 20, rows=one)
    m0 = small[:, 0:5]
    E, SI = m.view(M_E, ML_H, T), m.view(M_SI, ML_H, T)
    q, qs = m.view(M_Q, ML_H, T), m.view(M_QS, ML_H, T)
    cols = m.view(M_SM, NT, 8)
    tri = m.view(A_CONST + C_TRI, P)
    ident = m.view(A_CONST + C_ID, P)
    chain, ready, act_ready, turned, spread, evac, expd = (m.sem(n) for n in (
        "dve_chain", "gates_ready", "gates_act", "gates_turned", "gates_spread", "gates_evac", "gates_exp"))
    last_of = lambda x: x.rearrange("p (c t) -> p c t", t=P)[:, :, P - 1]
    count = [0]
    with nc.Block() as block:
        @block.vector
        def _(dve):
            def link(ins):
                count[0] += 1
                ins.then_inc(chain.handle, 1)
                dve.wait_ge(chain.handle, chain.at(count[0]))

            nc.vector.scalar_tensor_tensor(out=b, in0=lf, scalar=-1.0, in1=lf, op0=ALU.mult, op1=ALU.max).then_inc(ready.handle, 1)
            link(nc.vector.tensor_scalar(lf, lf, 0.0, None, ALU.min))
            dve.wait_ge(act_ready.handle, act_ready.at(2))
            link(nc.vector.tensor_tensor(lf, lf, mx, ALU.subtract))
            link(nc.vector.tensor_tensor_scan(out=b, data0=consts[:, 0, :], data1=lf, initial=0.0, op0=ALU.mult, op1=ALU.add))
            link(nc.vector.tensor_tensor(li, li, b, ALU.subtract))
            link(nc.vector.tensor_tensor_scan(out=mx, data0=consts[:, 1, :], data1=li, initial=NEG, op0=ALU.add, op1=ALU.max))
            link(nc.vector.memset(m0[:, 0:1], 0.0))
            link(nc.vector.tensor_copy(small[:, 5:9], last_of(mx)))
            link(nc.vector.tensor_copy(small[:, 9:13], last_of(b)))
            link(nc.vector.tensor_tensor_scan(out=m0[:, 1:5], data0=small[:, 5:9], data1=small[:, 9:13], initial=0.0,
                                              op0=ALU.max, op1=ALU.add))
            mxc, lfc = (x.rearrange("p (c t) -> p c t", t=P) for x in (mx, lf))
            m0w = m0[:, 0:4].unsqueeze(2).to_broadcast([4, NT, P])
            link(nc.vector.tensor_tensor(mxc, mxc, m0w, ALU.max))
            link(nc.vector.tensor_tensor(lfc, m0w, mxc, ALU.subtract))
            link(nc.vector.scalar_tensor_tensor(out=b, in0=b, scalar=-1.0, in1=mx, op0=ALU.mult, op1=ALU.subtract))
            nc.vector.tensor_scalar(mx, mx, -1.0, None, ALU.mult).then_inc(ready.handle, 1)
            for h in range(ML_H):
                dve.wait_ge(spread.handle, spread.at(h + 1))
                nc.vector.tensor_tensor(E[:, h, :].rearrange("p (c t) -> p c t", t=P),
                                        m.bank[1 + h][:, :].rearrange("p (c t) -> p c t", t=P),
                                        tri.unsqueeze(1).to_broadcast([P, NT, P]), ALU.add).then_inc(evac.handle, 1)
            for h in range(ML_H):
                dve.wait_ge(expd.handle, expd.at(h + 1))
                nc.vector.tensor_tensor(qs[:, h, :], q[:, h, :], SI[:, h, :], ALU.mult)

        @block.scalar
        def _(act):
            act.wait_ge(ready.handle, ready.at(1))
            nc.scalar.activation(mx, b, ACT.Exp, scale=-1.0).then_inc(act_ready.handle, 1)
            act.wait_ge(act_ready.handle, act_ready.at(1))
            nc.scalar.activation(mx, mx, ACT.Ln, bias=1.0).then_inc(act_ready.handle, 1)
            act.wait_ge(turned.handle, turned.at(1))
            bank = m.bank[0][:, 0:32].rearrange("p (c n) -> p c n", n=8)
            nc.scalar.activation(cols[:, :, 0:4], bank[:, :, 0:4], ACT.Copy).then_inc(act_ready.handle, 1)
            nc.scalar.activation(cols[:, :, 4:8], bank[:, :, 4:8], ACT.Exp)
            act.wait_ge(act_ready.handle, act_ready.at(3))
            for h in range(ML_H):
                act.wait_ge(spread.handle, spread.at(ML_H + h + 1))
                nc.scalar.activation(SI[:, h, :], m.bank[(5 + h) % 8][:, :], ACT.Exp).then_inc(expd.handle, 1)
            for h in range(ML_H):
                act.wait_ge(evac.handle, evac.at(h + 1))
                for c in range(NT):
                    nc.scalar.activation(E[:, h, c * P:(c + 1) * P], E[:, h, c * P:(c + 1) * P], ACT.Exp, bias=cols[:, c, h:h + 1])

        @block.tensor
        def _(pe):
            pe.wait_ge(ready.handle, ready.at(2))
            for c in range(NT):
                for n, row in enumerate((li, b)):
                    last = nc.tensor.transpose(m.bank[0][:, 8 * c + 4 * n:8 * c + 4 * n + 4], row[:, c * P:(c + 1) * P],
                                               ident[0:4, 0:4])
            last.then_inc(turned.handle, 1)
            for n in range(8):
                h = n % ML_H
                if n == 7:
                    pe.wait_ge(act_ready.handle, act_ready.at(3))
                    pe.wait_ge(expd.handle, expd.at(1))
                nc.tensor.matmul(m.bank[(1 + n) % 8][:, :], sel[:, h, :], (mx if n < ML_H else lf), start=True, stop=True)\
                    .then_inc(spread.handle, 1)

        @block.sync
        def _(sp):
            pass
    for s, n in ((chain, count[0]), (ready, 2), (act_ready, 3), (turned, 1), (spread, 8), (evac, ML_H), (expd, ML_H)):
        s.base += n


def ml_chunks(m):
    nc = m.nc
    W1 = ML_V + 1
    V = m.view(M_V, NT * ML_H, W1)
    hm = m.view(M_HM, NT, D)
    q, k, qs = m.view(M_Q, ML_H, T), m.view(M_K, ML_H, T), m.view(M_QS, ML_H, T)
    E, SI = m.view(M_E, ML_H, T), m.view(M_SI, ML_H, T)
    ktok = m.view(M_KTOK, NT * ML_H, P)
    state = m.view(M_STATE, ML_H, W1)
    cols = m.view(M_SM, NT, 8)
    stats = m.view(M_SM + 64, 16, 6)
    den = m.view(M_SM + 40, 16)
    ident = m.view(A_CONST + C_ID, P)
    kt_done, kt_evac, qk_done, p_ready, num_done, num_evac, ds_done, st_ready, chain, zero = (m.sem(n) for n in (
        "ktok_turned", "ktok_evac", "qk_done", "p_ready", "num_done", "num_evac", "ds_done", "state_ready", "dve_chain",
        "state_zeroed"))
    count = [0]
    units = [(c, h) for c in range(NT) for h in range(ML_H)]
    with nc.Block() as block:
        @block.tensor
        def _(pe):
            for h in range(ML_H):
                if h >= 2:
                    pe.wait_ge(kt_evac.handle, kt_evac.at(h - 1))
                for c in range(NT):
                    last = nc.tensor.transpose(m.bank[h % 2][:, c * P:(c + 1) * P], k[:, h, c * P:(c + 1) * P], ident)
                last.then_inc(kt_done.handle, 1)
            pe.wait_ge(kt_evac.handle, kt_evac.at(ML_H))
            pe.wait_ge(zero.handle, zero.at(1))

            def product(n):
                c, h = units[n]
                if n >= 2:
                    pe.wait_ge(p_ready.handle, p_ready.at(n - 1))
                t = slice(c * P, (c + 1) * P)
                nc.tensor.matmul(m.bank[n % 2][:, 0:P], k[:, h, t], q[:, h, t], start=True, stop=True).then_inc(qk_done.handle, 1)

            product(0)
            for n, (c, h) in enumerate(units):
                t = slice(c * P, (c + 1) * P)
                if n + 1 < len(units):
                    product(n + 1)
                if n >= 2:
                    pe.wait_ge(st_ready.handle, st_ready.at(n - 1))
                nc.tensor.matmul(m.bank[4 + n % 2][:, 0:W1], ktok[:, ML_H * c + h, :], V[:, n, :], start=True, stop=True)\
                    .then_inc(ds_done.handle, 1)
                pe.wait_ge(p_ready.handle, p_ready.at(n + 1))
                if n >= 2:
                    pe.wait_ge(num_evac.handle, num_evac.at(n - 1))
                if c >= 1:
                    pe.wait_ge(st_ready.handle, st_ready.at(n - ML_H + 1))
                nc.tensor.matmul(m.bank[2 + n % 2][:, 0:W1], E[:, h, t], V[:, n, :], start=True, stop=False)
                nc.tensor.matmul(m.bank[2 + n % 2][:, 0:W1], qs[:, h, t], state[:, h, :], start=False, stop=True)\
                    .then_inc(num_done.handle, 1)

        @block.scalar
        def _(act):
            for h in range(ML_H):
                act.wait_ge(kt_done.handle, kt_done.at(h + 1))
                for c in range(NT):
                    last = nc.scalar.activation(ktok[:, ML_H * c + h, :], m.bank[h % 2][:, c * P:(c + 1) * P], ACT.Copy,
                                                scale=E[:, h, c * P + P - 1:c * P + P])
                last.then_inc(kt_evac.handle, 1)

        @block.vector
        def _(dve):
            def link(ins):
                count[0] += 1
                ins.then_inc(chain.handle, 1)
                dve.wait_ge(chain.handle, chain.at(count[0]))

            nc.vector.memset(state[:, :, :], 0.0).then_inc(zero.handle, 1)
            dve.wait_ge(kt_evac.handle, kt_evac.at(ML_H))
            dve.wait_ge(zero.handle, zero.at(1))

            def weigh(n):
                c, h = units[n]
                dve.wait_ge(qk_done.handle, qk_done.at(n + 1))
                t = slice(c * P, (c + 1) * P)
                nc.vector.tensor_tensor(E[:, h, t], m.bank[n % 2][:, 0:P], E[:, h, t], ALU.mult).then_inc(p_ready.handle, 1)

            weigh(0)
            for n, (c, h) in enumerate(units):
                if n + 1 < len(units):
                    weigh(n + 1)
                bank = m.bank[2 + n % 2]
                dve.wait_ge(num_done.handle, num_done.at(n + 1))
                link(nc.vector.tensor_scalar(den[:, n:n + 1], bank[:, ML_V:W1], -1.0, None, ALU.mult))
                link(nc.vector.scalar_tensor_tensor(out=den[:, n:n + 1], in0=bank[:, ML_V:W1], scalar=cols[:, c, 4 + h:5 + h],
                                                    in1=den[:, n:n + 1], op0=ALU.max, op1=ALU.max))
                link(nc.vector.reciprocal(den[:, n:n + 1], den[:, n:n + 1]))
                out = hm[:, c, ML_V * h:ML_V * (h + 1)]
                nc.vector.tensor_scalar(out, bank[:, 0:ML_V], den[:, n:n + 1], None, ALU.mult).then_inc(num_evac.handle, 1)
                dve.wait_ge(num_evac.handle, num_evac.at(n + 1))
                nc.vector.bn_stats(stats[:, n, :], out)
                dve.wait_ge(ds_done.handle, ds_done.at(n + 1))
                nc.vector.scalar_tensor_tensor(out=state[:, h, :], in0=state[:, h, :], scalar=SI[:, h, c * P + P - 1:c * P + P],
                                               in1=m.bank[4 + n % 2][:, 0:W1], op0=ALU.mult, op1=ALU.add).then_inc(st_ready.handle, 1)
                dve.wait_ge(st_ready.handle, st_ready.at(n + 1))
    for s, n in ((kt_done, ML_H), (kt_evac, ML_H), (qk_done, 16), (p_ready, 16), (num_done, 16), (num_evac, 16), (ds_done, 16),
                 (st_ready, 16), (chain, count[0]), (zero, 1)):
        s.base += n


def ml_gate(m):
    nc = m.nc
    hm = m.view(M_HM, NT, D)
    cc, Z, Y = m.view(M_C, KT, T), m.view(M_Z, KT, T), m.view(M_Y, KT, T)
    stats = m.view(M_SM + 64, 16, 6)
    mv = m.view(M_SM + 160, 16, 2)
    ident = m.view(A_CONST + C_ID, P)
    prm = A_PT + 128
    col = lambda at, j: m.view(prm + at + j, 1)
    var, root, normed, turned, y_used, chain = (m.sem(n) for n in (
        "norm_inverse", "norm_root", "hm_normed", "norm_turned", "y_evac", "dve_chain"))
    count = [0]
    with nc.Block() as block:
        @block.vector
        def _(dve):
            def link(ins):
                count[0] += 1
                ins.then_inc(chain.handle, 1)
                dve.wait_ge(chain.handle, chain.at(count[0]))

            for n in range(16):
                ins = nc.vector.bn_aggr(mv[:, n, :], stats[:, n, :])
            link(ins)
            nc.vector.tensor_scalar(mv[:, :, 1], mv[:, :, 1], 1e-6, None, ALU.add).then_inc(var.handle, 1)
            for j in range(KT):
                ins = nc.vector.tensor_scalar(cc[:, j, :], cc[:, j, :], col(ML_SKIP, j), None, ALU.mult)
            dve.wait_ge(root.handle, root.at(1))
            link(nc.vector.reciprocal(mv[:, :, 1], mv[:, :, 1]))
            for n in range(16):
                part = hm[:, n // 4, ML_V * (n % 4):ML_V * (n % 4 + 1)]
                nc.vector.tensor_scalar(part, part, mv[:, n, 0:1], mv[:, n, 1:2], ALU.subtract, ALU.mult).then_inc(normed.handle, 1)
            for j in range(KT):
                dve.wait_ge(turned.handle, turned.at(j + 1))
                link(nc.vector.scalar_tensor_tensor(out=Y[:, j, :], in0=m.bank[j][:, :], scalar=col(ML_GN, j), in1=cc[:, j, :],
                                                    op0=ALU.mult, op1=ALU.add))
                nc.vector.tensor_tensor(Y[:, j, :], Y[:, j, :], Z[:, j, :], ALU.mult)

        @block.scalar
        def _(act):
            act.wait_ge(var.handle, var.at(1))
            nc.scalar.activation(mv[:, :, 1], mv[:, :, 1], ACT.Sqrt).then_inc(root.handle, 1)

        @block.tensor
        def _(pe):
            pe.wait_ge(normed.handle, normed.at(16))
            for j in range(KT):
                for a in range(NT):
                    last = nc.tensor.transpose(m.bank[j][:, a * P:(a + 1) * P], hm[:, a, j * P:(j + 1) * P], ident)
                last.then_inc(turned.handle, 1)
    for s, n in ((var, 1), (root, 1), (normed, 16), (turned, KT), (chain, count[0])):
        s.base += n


LAYERS = "rsmr"


def encoder(nc, x, norm_g, final_g, rw_w_in, rw_mu, rw_w0, rw_w2, rw_a0, rw_a2, rw_k_k, rw_k_a, rw_r_k, rw_ln_g,
            rw_ln_b, rw_w_out, sw_w_in, sw_sinks, sw_w_out, ml_w_in, ml_conv_w, ml_conv_b, ml_w_q, ml_w_k, ml_i_bias,
            ml_f_bias, ml_gn_g, ml_skip, ml_w_out, consts, consts2, out, spill):
    rows = lambda ap: ap.rearrange("(k c) -> k c", c=P)
    heads = lambda ap: ap.rearrange("h c -> (h c)").rearrange("(k c) -> k c", c=P)
    rw_rows = []
    for j, layer in ((0, 0), (1, 3)):
        rw_rows.append([(RW_NORM, rows(norm_g[layer])),
                        (RW_MU, rw_mu[j].rearrange("g d -> (g d)").rearrange("(k c) -> k c", c=P)),
                        (RW_W0, rows(rw_w0[j])), (RW_A0, rows(rw_a0[j])), (RW_KK, heads(rw_k_k[j])),
                        (RW_KA, heads(rw_k_a[j])), (RW_RK, heads(rw_r_k[j])), (RW_LNG, heads(rw_ln_g[j])),
                        (RW_LNB, heads(rw_ln_b[j]))])
    sw_ml = [(SW_NORM, rows(norm_g[1])), (ML_NORM, rows(norm_g[2])),
             (ML_CW, ml_conv_w[0].rearrange("t d -> (t d)").rearrange("(k c) -> k c", c=P)),
             (ML_CB, rows(ml_conv_b[0])), (ML_GN, heads(ml_gn_g[0])), (ML_SKIP, rows(ml_skip[0]))]
    with ExitStack() as ctx:
        m = Machine(nc, ctx)
        tile = lambda w, at, n=P: (w[:, at:at + n].rearrange("(k p) n -> p k n", p=P), (KT, n))
        row = lambda w, k: (w[k * P:(k + 1) * P, :], (D,))
        plan = []
        for n, kind in enumerate(LAYERS):
            plan.append(len(m.weights))
            if kind == "r":
                j = 1 if n == 3 else 0
                w = rw_w_in[j]
                m.weights.append(tile(w, 4 * D))
                for g in (1, 0, 2, 3):
                    m.weights += [tile(w, g * D + k * P) for k in range(KT)]
                plan.append(len(m.weights))
                m.weights += [row(rw_w_out[j], k) for k in range(KT)]
            elif kind == "s":
                w = sw_w_in[0]
                m.weights += [row(w[:, 0:D], k) for k in range(KT)]
                m.weights += [(w[2 * k * P:2 * (k + 1) * P, D:D + 512].rearrange("(k p) n -> p k n", p=P), (2, 512))
                              for k in range(KT // 2)]
                m.weights += [tile(w, D + 512 + k * P) for k in range(KT)]
                plan.append(len(m.weights))
                m.weights += [row(sw_w_out[0], k) for k in range(KT)]
            else:
                w = ml_w_in[0]
                m.weights += [tile(w, k * P) for k in range(KT)] + [tile(w, 2 * D + k * P) for k in range(KT)]
                m.weights += [(v.rearrange("h (e p) d -> p (h e) d", p=P), (KT, P)) for v in (ml_w_q[0], ml_w_k[0])]
                m.weights += [row(w[:, D:2 * D], k) for k in range(KT)]
                plan.append(len(m.weights))
                m.weights += [row(ml_w_out[0], k) for k in range(KT)]
        stage_load(m, x, consts, rw_rows, sw_ml, plan)
        for n, kind in enumerate(LAYERS):
            if kind == "r":
                j = 1 if n == 3 else 0
                prm = A_PT + 256 * j
                a, b = plan[2 * n:2 * n + 2]
                stage_norm(m, 256 * j + RW_NORM, B_R, A_XT)
                rw_mix(m, prm, (rw_w2[j], rw_a2[j]), consts2[:, 0:T], a, b, spill)
                rw_gate(m, prm)
                stage_out(m, B_KK, b)
            elif kind == "s":
                a, b = plan[2 * n:2 * n + 2]
                stage_norm(m, 128 + SW_NORM, B_R, A_XT)
                sw_project(m, sw_sinks[0], a)
                sw_attend(m)
                stage_out(m, S_Y, b)
            else:
                a, b = plan[2 * n:2 * n + 2]
                stage_norm(m, 128 + ML_NORM, B_R, M_XT)
                ml_project(m, ml_w_in[0][:, 3 * D:3 * D + 8], ml_i_bias[0], ml_f_bias[0],
                           consts2[0:4, T:4 * T].rearrange("p (a t) -> p a t", a=3), a)
                ml_gates(m)
                ml_chunks(m)
                ml_gate(m)
                stage_out(m, M_Y, b)
        stage_store(m, final_g, out)


_INS = ["x", "norm_g", "final_g", "rw_w_in", "rw_mu", "rw_w0", "rw_w2", "rw_a0", "rw_a2", "rw_k_k", "rw_k_a", "rw_r_k",
        "rw_ln_g", "rw_ln_b", "rw_w_out", "sw_w_in", "sw_sinks", "sw_w_out", "ml_w_in", "ml_conv_w", "ml_conv_b",
        "ml_w_q", "ml_w_k", "ml_i_bias", "ml_f_bias", "ml_gn_g", "ml_skip", "ml_w_out"]


def kernel(**inputs):
    import numpy as _np
    import concourse.bacc as _bacc
    from concourse import mybir as _mybir
    from concourse.bass_utils import run_bass_kernel_spmd as _run

    nc = _bacc.Bacc("TRN2", target_bir_lowering=False, num_devices=1)
    arrays, args = {}, []
    given = {name: _np.ascontiguousarray(inputs[name]) for name in _INS}
    given["masks"], given["rows"] = constants(), more_constants()
    for name, a in given.items():
        arrays[f"in_{name}"] = a
        args.append(nc.dram_tensor(f"in_{name}", a.shape, _mybir.dt.from_np(a.dtype), kind="ExternalInput").ap())
    args.append(nc.dram_tensor("out_h", (1, T, D), _mybir.dt.float32, kind="ExternalOutput").ap())
    args.append(nc.dram_tensor("spill", (2, P, 4096), _mybir.dt.float32).ap())
    encoder(nc, *args)
    r = _run(nc, [arrays], core_ids=[0])
    return r.results[0]["out_h"]
```

```python
import math
from contextlib import ExitStack

import numpy as np

import concourse.bass as bass
from concourse import mybir

F32 = mybir.dt.float32
ALU = mybir.AluOpType
ACT = mybir.ActivationFunctionType
AX = mybir.AxisListType

P = 128
T = 512
D = 1024
KT = D // P
NT = T // P
C = 64
NC = T // C
NH = 16
DECAY = math.exp(-0.5)
NEG = -1.0e30
SLOTS = 4

C_ID, C_BONES, C_GMASK, C_XMASK, C_TRI, C_ROPE, C_CENTRE, C_COMPACT = 0, 128, 256, 384, 448, 576, 640, 768
C_END = 800
RW_NORM, RW_MU, RW_W0, RW_A0, RW_KK, RW_KA, RW_RK, RW_LNG, RW_LNB = 0, 8, 56, 64, 72, 80, 88, 96, 104
SW_NORM, ML_NORM, ML_CW, ML_CB, ML_GN, ML_SKIP = 0, 8, 16, 48, 56, 64
MU_R, MU_K, MU_V, MU_G, MU_W, MU_A = (RW_MU + 8 * n for n in range(6))

A_H = 0
A_CONST = A_H + 4096
A_PT = A_CONST + C_END
A_SMALL = A_PT + 384
A_RING = A_SMALL + 96
A_BUF = A_RING + SLOTS * 1024
A_TMP = A_BUF + 7 * 4096
A_END = 53100
B_R, B_K, B_A, B_L, B_V, B_G, B_KK = (A_BUF + 4096 * n for n in range(7))
A_XT = A_TMP
A_DX = A_XT + KT * (T + 1)
A_T5 = A_DX + 4096


def constants():
    c = np.zeros((P, C_END), np.float32)
    r = np.arange(P)
    c[:, C_ID:C_ID + P] = np.eye(P)
    c[:, C_BONES:C_BONES + P] = (r[:, None] // C == r[None, :] // C)
    c[:, C_CENTRE:C_CENTRE + P] = c[:, C_ID:C_ID + P] - c[:, C_BONES:C_BONES + P] / C
    c[:C, C_COMPACT + 14] = 1.0
    c[C:, C_COMPACT + 15] = 1.0
    s, t = (r % C)[:, None], np.arange(C)[None, :]
    c[:, C_GMASK:C_GMASK + C] = t > s
    c[:, C_GMASK + C:C_GMASK + P] = t >= s
    c[:, C_XMASK:C_XMASK + C] = (s >= 32) & (t < 32)
    c[:, C_TRI:C_TRI + P] = np.where(r[None, :] >= r[:, None], 0.0, NEG)
    inv = np.power(np.float32(500000.0), -np.arange(8, dtype=np.float32) * np.float32(2.0 / 16))
    for a in range(NT):
        ang = (a * P + r).astype(np.float32)[:, None] * inv[None, :]
        c[:, C_ROPE + a * 8:C_ROPE + a * 8 + 8] = np.cos(ang)
        c[:, C_ROPE + 32 + a * 8:C_ROPE + 40 + a * 8] = np.sin(ang)
    return c


def more_constants():
    c = np.ones((P, 7 * T), np.float32)
    c[:, 0:T:C] = 0.0
    c[:, T:2 * T:P] = 0.0
    c[:, 2 * T:] = 0.0
    c[:, 2 * T:3 * T:P] = NEG
    for h in range(4):
        c[h, 3 * T + h * P:3 * T + (h + 1) * P] = 1.0
    for h in range(NH):
        c[h, 5 * T + h * C:5 * T + (h + 1) * C] = 1.0
    return c


class Count:

    def __init__(self, handle):
        self.handle, self.base = handle, 0

    def at(self, n):
        return self.base + n


class Machine:

    def __init__(self, nc, ctx):
        self.nc = nc
        self.arena = ctx.enter_context(nc.sbuf_tensor("arena", [P, A_END], F32))
        self.bank = [ctx.enter_context(nc.psum_tensor(f"bank{n}", [P, 512], F32)) for n in range(8)]
        self.ctx = ctx
        self.sems = {}
        self.slot_full = [ctx.enter_context(nc.semaphore(f"slot{n}_full")) for n in range(SLOTS)]
        self.used_by = []
        self.weights = []
        self.issued = 0

    def sem(self, name):
        if name not in self.sems:
            self.sems[name] = Count(self.ctx.enter_context(self.nc.semaphore(name)))
        return self.sems[name]

    def view(self, at, *shape, rows=slice(0, P)):
        n = int(np.prod(shape))
        flat = self.arena[rows, at:at + n]
        if len(shape) == 1:
            return flat
        names = "abc"[:len(shape)]
        return flat.rearrange(f"p ({' '.join(names)}) -> p {' '.join(names)}",
                              **{k: v for k, v in zip(names[1:], shape[1:])})

    def slot(self, n):
        return A_RING + (n % SLOTS) * 1024

    def load_weights(self, eng, upto):
        for n in range(self.issued, min(upto, len(self.weights))):
            if n >= SLOTS:
                eng.wait_ge(*self.used_by[n - SLOTS])
            src, shape = self.weights[n]
            eng.dma_start(self.view(self.slot(n), *shape), src).then_inc(self.slot_full[n % SLOTS], 16)
        self.issued = max(self.issued, min(upto, len(self.weights)))

    def weights_arrived(self, pe, n):
        pe.wait_ge(self.slot_full[n % SLOTS], 16 * (n // SLOTS + 1))


class Norm:

    def __init__(self, m, banks, xn_at, out_at=None, gcol=None):
        self.m, self.banks, self.gcol = m, banks, gcol
        self.h, self.xn, self.ss = m.view(A_H, NT, D), m.view(xn_at, NT, D), m.view(A_SMALL, NT)
        if out_at is not None:
            self.xt = m.view(out_at, KT, T + 1)
        self.squared, self.mean_ready, self.root_ready, self.inverse_ready, self.scaled, self.turned = (
            m.sem(n) for n in ("norm_squared", "norm_mean", "norm_root", "norm_inverse", "norm_scaled", "norm_turned"))

    def clear(self, dve):
        self.m.nc.vector.memset(self.xt[:, :, 0:1], 0.0)

    def square(self, act, a):
        self.m.nc.scalar.activation(self.xn[:, a, :], self.h[:, a, :], ACT.Square, accum_out=self.ss[:, a:a + 1])\
            .then_inc(self.squared.handle, 1)

    def mean(self, dve, a):
        ss = self.ss[:, a:a + 1]
        dve.wait_ge(self.squared.handle, self.squared.at(a + 1))
        self.m.nc.vector.tensor_scalar(ss, ss, 1.0 / D, 1e-6, ALU.mult, ALU.add).then_inc(self.mean_ready.handle, 1)

    def root(self, act, a):
        ss = self.ss[:, a:a + 1]
        act.wait_ge(self.mean_ready.handle, self.mean_ready.at(a + 1))
        self.m.nc.scalar.activation(ss, ss, ACT.Sqrt).then_inc(self.root_ready.handle, 1)

    def scale(self, dve, a, weights=None):
        ss = self.ss[:, a:a + 1]
        dve.wait_ge(self.root_ready.handle, self.root_ready.at(a + 1))
        self.m.nc.vector.reciprocal(ss, ss).then_inc(self.inverse_ready.handle, 1)
        dve.wait_ge(self.inverse_ready.handle, self.inverse_ready.at(a + 1))
        if weights is None:
            self.m.nc.vector.tensor_scalar(self.xn[:, a, :], self.h[:, a, :], ss, None, ALU.mult).then_inc(self.scaled.handle, 1)
        else:
            self.m.nc.vector.scalar_tensor_tensor(out=self.h[:, a, :], in0=self.h[:, a, :], scalar=ss, in1=weights,
                                                  op0=ALU.mult, op1=ALU.mult).then_inc(self.scaled.handle, 1)

    def turn(self, pe, a):
        pe.wait_ge(self.scaled.handle, self.scaled.at(a + 1))
        for k in range(KT):
            last = self.m.nc.tensor.transpose(self.banks[a][k // 4][:, (k % 4) * P:(k % 4 + 1) * P],
                                              self.xn[:, a, k * P:(k + 1) * P], self.m.view(A_CONST + C_ID, P))
        last.then_inc(self.turned.handle, 1)

    def keep(self, dve, a):
        dve.wait_ge(self.turned.handle, self.turned.at(a + 1))
        for half in range(2):
            weights = self.m.view(A_PT + self.gcol + 4 * half, 4).unsqueeze(2).to_broadcast([P, 4, P])
            self.m.nc.vector.tensor_tensor(self.xt[:, 4 * half:4 * half + 4, 1 + a * P:1 + (a + 1) * P],
                                           self.banks[a][half][:, :].rearrange("p (k t) -> p k t", t=P), weights, ALU.mult)

    def act_steps(self, act, wait):
        for s in range(NT + 1):
            if s < NT:
                wait(act, s)
                self.square(act, s)
            if s > 0:
                self.root(act, s - 1)

    def dve_steps(self, dve, before, weights=None):
        for s in range(NT + 3):
            if s < NT:
                before(dve, s)
            if 1 <= s <= NT:
                self.mean(dve, s - 1)
            if 2 <= s <= NT + 1:
                self.scale(dve, s - 2, weights)
            if s >= 3 and weights is None:
                self.keep(dve, s - 3)

    def finish(self, last=False):
        for s in (self.squared, self.mean_ready, self.root_ready, self.inverse_ready, self.scaled):
            s.base += NT
        self.turned.base += 0 if last else NT


def stage_load(m, x, consts, rw, sw_ml, norm):
    nc = m.nc
    loaded, x_loaded, zeroed, turned = m.sem("loaded"), [m.sem(f"x{a}_loaded") for a in range(NT)], m.sem("zeroed"), m.sem("turned")
    params = m.sem("params_kept")
    stage = m.view(A_T5, 3, P)
    with nc.Block() as block:
        @block.sync
        def _(sp):
            sp.dma_start(m.view(A_CONST, C_END), consts).then_inc(loaded.handle, 16)
            sp.wait_ge(zeroed.handle, 1)
            n = 1
            for s, rows in ((0, rw[0]), (2, rw[1]), (1, sw_ml)):
                for at, src in rows:
                    k = src.shape[0]
                    sp.dma_start(stage[at:at + k, s, :], src).then_inc(loaded.handle, 16)
                    n += 1
            loaded.total = 16 * n
            m.load_weights(sp, SLOTS)

        @block.scalar
        def _(act):
            for a in range(NT):
                act.dma_start(m.view(A_H, NT, D)[:, a, :], x[0, a * P:(a + 1) * P, :]).then_inc(x_loaded[a].handle, 16)
            norm.act_steps(act, lambda act, a: act.wait_ge(x_loaded[a].handle, 16))

        @block.vector
        def _(dve):
            nc.vector.memset(stage[:, :, :], 0.0).then_inc(zeroed.handle, 1)
            norm.clear(dve)

            def keep_params(dve, a):
                if a == 0:
                    dve.wait_ge(turned.handle, turned.at(1))
                    nc.vector.tensor_copy(m.view(A_PT, 384), m.bank[0][:, 0:384]).then_inc(params.handle, 1)
                    dve.wait_ge(params.handle, params.at(1))

            norm.dve_steps(dve, keep_params)

        @block.tensor
        def _(pe):
            pe.wait_ge(loaded.handle, loaded.total)
            for s in range(3):
                last = nc.tensor.transpose(m.bank[0][:, s * P:(s + 1) * P], stage[:, s, :], m.view(A_CONST + C_ID, P))
            last.then_inc(turned.handle, 1)
            for a in range(NT):
                norm.turn(pe, a)
    norm.finish()


def stage_out(m, y_at, n0, norm):
    nc = m.nc
    Y = m.view(y_at, KT, T)
    done, rows_used = m.sem("out_done"), m.sem("out_rows_used")
    m.used_by += [(rows_used.handle, rows_used.at(k + 1)) for k in range(KT - 1)] + [(done.handle, done.at(8))]
    added = m.sem("h_added")
    with nc.Block() as block:
        @block.sync
        def _(sp):
            m.load_weights(sp, n0 + KT + SLOTS)

        @block.tensor
        def _(pe):
            for k in range(KT):
                m.weights_arrived(pe, n0 + k)
                slot = m.view(m.slot(n0 + k), D)
                for a in range(NT):
                    for half in range(2):
                        last = nc.tensor.matmul(m.bank[2 * a + half][:, :], Y[:, k, a * P:(a + 1) * P],
                                                slot[:, half * 512:half * 512 + 512], start=k == 0, stop=k == KT - 1)
                        if k == KT - 1:
                            last.then_inc(done.handle, 1)
                if k < KT - 1:
                    last.then_inc(rows_used.handle, 1)
            for a in range(NT):
                norm.turn(pe, a)

        @block.scalar
        def _(act):
            norm.act_steps(act, lambda act, a: act.wait_ge(added.handle, added.at(2 * a + 2)))

        @block.vector
        def _(dve):
            norm.clear(dve)

            def add(dve, a):
                for half in range(2):
                    dve.wait_ge(done.handle, done.at(2 * a + half + 1))
                    part = norm.h[:, a, 512 * half:512 * half + 512]
                    nc.vector.tensor_tensor(part, part, m.bank[2 * a + half][:, :], ALU.add).then_inc(added.handle, 1)

            norm.dve_steps(dve, add)
    norm.finish()
    done.base += 8
    rows_used.base += KT - 1
    added.base += 8


FIRST = 8
BC = 4
Q = 32
A_TU = A_RING
A_Z = A_DX
A_XS = A_Z + 2048
A_US = A_XS + 1024
A_S = A_T5
A_RHS = A_S + 512
A_AD = A_RHS + 512
A_ARZ = A_AD + 1024
A_BK = A_ARZ + 2048
A_EP = A_BK + 1024
A_EPI = A_EP + 8 * (C + 1)
A_A32, A_T32, A_PROD = A_ARZ, A_ARZ + 1024, A_BK
A_LORA, A_SIG, A_RESET, A_SQ, A_RT = A_ARZ, A_ARZ + 512, A_ARZ + 1536, A_BK, A_AD
A_OMKA = A_SMALL + 16
A_PC = A_SMALL + 24
GS_AT = [A_XT, A_XT + 2048, A_H, A_H + 2048, B_G, B_G + 2048, A_XT, A_XT + 2048]
LO, HI = slice(0, 64), slice(64, 128)
SIDES = ((0, LO), (1, HI))


def wide(ap, n):
    return ap.unsqueeze(1).to_broadcast([ap.shape[0], n, ap.shape[1]])


def heads(buf, par):
    return buf.rearrange("p (k h) c -> p k h c", h=2)[:, :, par, :]


def rw_mix(m, prm, w2a2, reset_src, n0, spill):
    nc = m.nc
    xt = m.view(A_XT, KT, T + 1)
    dx = m.view(A_DX, KT, T)
    R, K, BB, L, V, G, KK = (m.view(at, KT, T) for at in (B_R, B_K, B_A, B_L, B_V, B_G, B_KK))
    lora, reset, rt = m.view(A_LORA, T), m.view(A_RESET, T), m.view(A_RT, T)
    sig, sq = ([m.view(at + 512 * n, T) for n in range(2)] for at in (A_SIG, A_SQ))
    w2a2_sb = m.view(B_R, D)
    omka = m.view(A_OMKA, 8)
    ident, bones = m.view(A_CONST + C_ID, P), m.view(A_CONST + C_BONES, P)
    col = lambda at, k: m.view(prm + at + k, 1)
    gmask, xmask = m.view(A_CONST + C_GMASK, P), m.view(A_CONST + C_XMASK, C)
    arz, bk = m.view(A_ARZ, NH, P), m.view(A_BK, KT, P)
    ep, epi = m.view(A_EP, KT, C + 1), m.view(A_EPI, KT, C)
    gs = [m.view(at, 2, NH, C) for at in GS_AT]
    ad, a32, t32 = (m.view(at, Q, Q) for at in (A_AD, A_A32, A_T32))
    tt, uu = a32, ad
    tu = [m.view(A_TU + 1024 * (c % BC), KT, P) for c in range(NC)]
    z = [m.view(A_Z + 1024 * (c % 2), NH, C) for c in range(NC)]
    xs, us = m.view(A_XS, KT, P), m.view(A_US, KT, P)
    rhs, S = m.view(A_RHS, KT, C), m.view(A_S, KT, C)
    span = lambda c: slice(c * C, (c + 1) * C)
    pairs = [slice(4 * g, 4 * g + 4) for g in range(2)]
    quarter = lambda bank: bank[:, 0:256].rearrange("p (k c) -> p k c", c=C)
    blocks = lambda bank: bank[:, :].rearrange("p (k c) -> p k c", c=P)
    g_bank = lambda c, q: m.bank[q if c < BC else (q + 2) % 4]
    t_bank = lambda c, q: m.bank[4 + q if c < BC else 2 + q]

    tiles = []
    for j in range(KT + 1):
        tiles += [("k", j)] * (j < KT) + [("n2", j - 1)] * (j > 0)
    tiles += [("lora", 0)]
    for j in range(KT):
        tiles += [("decay", j), ("a", j)]
    tiles += [(n, j) for n in ("r", "v", "g") for j in range(KT)]
    place = {t: n for n, t in enumerate(tiles)}
    tile_bank = lambda n: m.bank[6 + tiles[n][1] % 2 if tiles[n][0] in "vg" else n % 8]
    mixes = ["k", "w", "a", "r", "v", "g"]
    mix_at = {"k": G, "w": V, "a": L, "r": V, "v": G, "g": dx}
    mu_at = {"w": MU_W, "a": MU_A, "k": MU_K, "r": MU_R, "v": MU_V, "g": MU_G}
    dx_ready, mixed, tile_done, act_done, gated, kk_squared, chain, act_chain, aux, root_used, sig_used, keys_ready = (
        m.sem(n) for n in ("dx_ready", "mixed", "tile_done", "act_evacuated", "g_gated", "kk_squared", "dve_chain", "act_chain",
                           "aux_loaded", "root_used", "sig_used", "keys_ready"))
    h_spilled, g_spilled, reloaded = m.sem("h_spilled"), m.sem("g_spilled"), m.sem("reloaded")
    ep_cleared, exp_ready, ar_scaled, ar_staged, k_staged, b_scaled, k_scaled, b_staged = (m.sem(n) for n in (
        "ep_cleared", "exp_ready", "ar_scaled", "ar_staged", "k_staged", "b_scaled", "k_scaled", "b_staged"))
    g_done, g_evac, bkt_done, bkt_evac = (m.sem(n) for n in ("g_done", "g_evac", "bkt_done", "bkt_evac"))
    gathered, step, t_turned, u_turned, tu_cleared, t_placed, u_placed = (m.sem(n) for n in (
        "gathered", "inverse_step", "t_turned", "u_turned", "tu_cleared", "t_placed", "u_placed"))
    carry_cleared, z_cleared, v_done, v_evac, x_done, xs_ready, xu_done, us_ready, s_added = (m.sem(n) for n in (
        "carry_cleared", "z_cleared", "v_done", "v_evac", "x_done", "xs_ready", "xu_done", "us_ready", "s_added"))
    rhs_done, rhs_evac, sa_done, sa_evac, y_done, y_evac, s_done, s_ready = (m.sem(n) for n in (
        "rhs_done", "rhs_evac", "sa_done", "sa_evac", "y_done", "y_evac", "s_done", "s_ready"))
    m.used_by += [(tile_done.handle, tile_done.at(place[t] + 1)) for t in tiles if t[0] not in ("decay", "a", "n2")]
    links, steps = [0], [0]

    with nc.Block() as block:
        @block.sync
        def _(sp):
            sp.dma_start(w2a2_sb[0:64, :], w2a2[0]).then_inc(aux.handle, 16)
            sp.dma_start(w2a2_sb[64:128, :], w2a2[1]).then_inc(aux.handle, 16)
            sp.dma_start(reset, reset_src).then_inc(aux.handle, 16)
            sp.dma_start(spill[0], m.view(A_H, 4096)).then_inc(h_spilled.handle, 16)
            m.load_weights(sp, n0 + 33)
            sp.wait_ge(gated.handle, gated.at(KT))
            sp.dma_start(spill[1], m.view(B_G, 4096)).then_inc(g_spilled.handle, 16)
            sp.wait_ge(y_done.handle, y_done.at(2 * 4))
            sp.wait_ge(h_spilled.handle, h_spilled.at(16))
            sp.dma_start(m.view(A_H, 4096), spill[0]).then_inc(reloaded.handle, 16)
            sp.wait_ge(y_done.handle, y_done.at(2 * 6))
            sp.wait_ge(g_spilled.handle, g_spilled.at(16))
            sp.dma_start(m.view(B_G, 4096), spill[1]).then_inc(reloaded.handle, 16)
            sp.wait_ge(us_ready.handle, us_ready.at(2 * NC))
            m.load_weights(sp, n0 + 33 + SLOTS)
            sp.wait_ge(reloaded.handle, reloaded.at(32))

        @block.gpsimd
        def _(pool):
            nc.gpsimd.memset(ep[:, :, 0:1], 1.0).then_inc(ep_cleared.handle, 1)
            pool.wait_ge(keys_ready.handle, keys_ready.at(1))
            for c in range(NC):
                t = span(c)
                pool.wait_ge(exp_ready.handle, exp_ready.at(c + 1))
                nc.gpsimd.tensor_tensor(BB[:, :, t], BB[:, :, t], epi, ALU.mult).then_inc(b_scaled.handle, 1)
                pool.wait_ge(ar_scaled.handle, ar_scaled.at(c + 1))
                nc.gpsimd.tensor_tensor(R[:, :, t], R[:, :, t], K[:, :, t], ALU.mult)
                nc.gpsimd.tensor_tensor(K[:, :, t], K[:, :, t], epi, ALU.mult).then_inc(k_scaled.handle, 1)
                if c == BC:
                    pool.wait_ge(tile_done.handle, tile_done.at(len(tiles)))
                    nc.gpsimd.memset(m.view(A_Z, 2048), 0.0).then_inc(carry_cleared.handle, 1)
                    nc.gpsimd.memset(m.view(A_XS, 2048), 0.0).then_inc(carry_cleared.handle, 1)

        @block.scalar
        def _(act):
            def read_tile(n):
                what, j = tiles[n]
                bank = tile_bank(n)
                act.wait_ge(tile_done.handle, tile_done.at(n + 1))
                if what == "lora":
                    nc.scalar.activation(lora[0:64, :], bank[0:64, :], ACT.Tanh).then_inc(act_chain.handle, 1)
                    out = nc.scalar.activation(lora[64:128, :], bank[64:128, :], ACT.Copy)
                    act.wait_ge(act_chain.handle, act_chain.at(1))
                elif what == "decay":
                    if j >= 2:
                        act.wait_ge(sig_used.handle, sig_used.at(j - 1))
                    out = nc.scalar.activation(sig[j % 2], bank[:, :], ACT.Sigmoid, bias=col(RW_W0, j))
                elif what == "a":
                    out = nc.scalar.activation(BB[:, j, :], bank[:, :], ACT.Sigmoid, bias=col(RW_A0, j))
                elif what == "n2":
                    if j >= 1:
                        act.wait_ge(root_used.handle, root_used.at(j))
                    out = nc.scalar.activation(rt, bank[:, :], ACT.Sqrt)
                elif what == "g":
                    out = nc.scalar.activation(G[:, j, :], bank[:, :], ACT.Sigmoid)
                else:
                    out = nc.scalar.activation({"k": K, "r": R, "v": V}[what][:, j, :], bank[:, :], ACT.Copy)
                out.then_inc(act_done.handle, 1)

            def exps(c):
                if c >= 1:
                    act.wait_ge(ar_scaled.handle, ar_scaled.at(c))
                    act.wait_ge(k_scaled.handle, k_scaled.at(c))
                nc.scalar.activation(ep[:, :, 1:C + 1], L[:, :, span(c)], ACT.Exp, scale=-DECAY)
                nc.scalar.activation(epi, L[:, :, span(c)], ACT.Exp, scale=DECAY).then_inc(exp_ready.handle, 1)

            def stage_b(c):
                act.wait_ge(b_scaled.handle, b_scaled.at(c + 1))
                if c >= 1:
                    act.wait_ge(bkt_done.handle, bkt_done.at(2 * c))
                if c == BC:
                    act.wait_ge(u_turned.handle, u_turned.at(1))
                nc.scalar.activation(bk[LO, :, 0:C], BB[LO, :, span(c)], ACT.Copy)
                nc.scalar.activation(bk[HI, :, C:P], BB[HI, :, span(c)], ACT.Copy).then_inc(b_staged.handle, 1)

            def keep_bkt(c):
                for q in range(2):
                    act.wait_ge(bkt_done.handle, bkt_done.at(2 * c + q + 1))
                    nc.scalar.activation(BB[:, pairs[q], span(c)], blocks(t_bank(c, q))[:, :, 0:C], ACT.Copy)
                    nc.scalar.activation(K[:, pairs[q], span(c)], blocks(t_bank(c, q))[:, :, C:P], ACT.Copy)\
                        .then_inc(bkt_evac.handle, 1)

            def gather(c):
                if c == BC:
                    act.wait_ge(u_placed.handle, u_placed.at(BC))
                act.wait_ge(g_evac.handle, g_evac.at(4 * c + 4))
                i = c % BC
                for g in range(4):
                    rows, half = slice(Q * g, Q * g + Q), g % 2
                    last = nc.scalar.activation(ad[rows, :, KT * i:KT * i + KT],
                                                heads(gs[c][:, 0], g // 2)[rows, :, Q * half:Q * half + Q]
                                                .rearrange("p k c -> p c k"), ACT.Copy)
                if i == BC - 1:
                    last.then_inc(gathered.handle, 1)

            def place_inverse(b):
                act.wait_ge(t_turned.handle, t_turned.at(b + 1))
                act.wait_ge(tu_cleared.handle, tu_cleared.at(1))
                for i in range(BC):
                    if b > 0:
                        act.wait_ge(us_ready.handle, us_ready.at(2 * (BC * (b - 1) + i + 1)))
                    for g in range(4):
                        rows, at = slice(Q * g, Q * g + Q), Q * (g % 2)
                        last = nc.scalar.activation(tu[i][rows, :, at:at + Q],
                                                    tt[rows, :, KT * i:KT * i + KT].rearrange("p c n -> p n c"), ACT.Copy)
                    last.then_inc(t_placed.handle, 1)

            def values(c):
                if c >= 2:
                    act.wait_ge(s_done.handle, s_done.at(2 * (c - 1)))
                for q in range(2):
                    act.wait_ge(v_done.handle, v_done.at(2 * c + q + 1))
                    nc.scalar.activation(heads(z[c], 0)[HI, pairs[q], :], blocks(m.bank[q])[LO, :, 0:C], ACT.Copy)
                    nc.scalar.activation(heads(z[c], 1)[LO, pairs[q], :], blocks(m.bank[q])[LO, :, C:P], ACT.Copy)\
                        .then_inc(v_evac.handle, 1)

            def read_rhs(c):
                for g in range(2):
                    act.wait_ge(rhs_done.handle, rhs_done.at(2 * c + g + 1))
                    for par, rows in SIDES:
                        last = nc.scalar.activation(rhs[rows, pairs[g], :], blocks(m.bank[4 + g])[rows, :, C * par:C * par + C],
                                                    ACT.Copy, scale=-1.0)
                    last.then_inc(rhs_evac.handle, 1)

            def read_sa(c):
                for g in range(2):
                    act.wait_ge(sa_done.handle, sa_done.at(2 * c + g + 1))
                    for par, rows in SIDES:
                        last = nc.scalar.activation(heads(z[c], par)[rows, pairs[g], :], quarter(m.bank[6 + g])[rows], ACT.Copy)
                    last.then_inc(sa_evac.handle, 1)

            def read_y(c):
                for g in range(2):
                    act.wait_ge(y_done.handle, y_done.at(2 * c + g + 1))
                    for par, rows in SIDES:
                        last = nc.scalar.activation(KK[rows, pairs[g], span(c)],
                                                    blocks(m.bank[4 + g])[rows, :, C * par:C * par + C], ACT.Copy)
                    last.then_inc(y_evac.handle, 1)

            for n in range(place["v", 0]):
                read_tile(n)
            act.wait_ge(ep_cleared.handle, ep_cleared.at(1))
            act.wait_ge(keys_ready.handle, keys_ready.at(1))
            exps(0)
            stage_b(0)
            for c in range(BC):
                read_tile(place["v", c])
                if c + 1 < BC:
                    exps(c + 1)
                    stage_b(c + 1)
                keep_bkt(c)
                gather(c)
            for n in range(place["v", BC], place["g", 0]):
                read_tile(n)
            exps(BC)
            for j in range(KT):
                read_tile(place["g", j])
                if j == KT // 2:
                    stage_b(BC)
            act.wait_ge(carry_cleared.handle, carry_cleared.at(1))
            values(0)
            place_inverse(0)
            for c in range(NC):
                read_rhs(c)
                if c + 1 < NC:
                    values(c + 1)
                read_sa(c)
                if c == 0:
                    exps(5)
                if c == 1:
                    exps(7)
                read_y(c)
                if c == BC - 1:
                    place_inverse(1)
                if c == 0:
                    keep_bkt(4)
                    stage_b(5)
                    gather(4)
                    exps(6)
                    keep_bkt(5)
                    stage_b(6)
                    gather(5)
                if c == 1:
                    keep_bkt(6)
                    stage_b(7)
                    gather(6)
                    keep_bkt(7)
                    gather(7)

        @block.vector
        def _(dve):
            def link(ins):
                links[0] += 1
                ins.then_inc(chain.handle, 1)
                dve.wait_ge(chain.handle, chain.at(links[0]))

            def mix(g, tiles=range(KT)):
                for k in tiles:
                    nc.vector.scalar_tensor_tensor(out=mix_at[g][:, k, :], in0=dx[:, k, :], scalar=col(mu_at[g], k),
                                                   in1=xt[:, k, 1:T + 1], op0=ALU.mult, op1=ALU.add)\
                        .then_inc(mixed.handle, 1)

            def scale(c):
                dve.wait_ge(exp_ready.handle, exp_ready.at(c + 1))
                t = span(c)
                nc.vector.tensor_copy(m.view(A_PC + KT * c, KT).unsqueeze(2), ep[:, :, C:C + 1])
                nc.vector.tensor_tensor(KK[:, :, t], KK[:, :, t], ep[:, :, 0:C], ALU.mult)
                nc.vector.tensor_tensor(L[:, :, t], R[:, :, t], ep[:, :, 1:C + 1], ALU.mult).then_inc(ar_scaled.handle, 1)

            def stage_ar(c):
                dve.wait_ge(ar_scaled.handle, ar_scaled.at(c + 1))
                if c % BC == 0:
                    if c == BC:
                        dve.wait_ge(t_placed.handle, t_placed.at(BC))
                    for par, rows in ((0, HI), (1, LO)):
                        nc.vector.memset(heads(arz, par)[rows], 0.0)
                for par, rows in SIDES:
                    nc.vector.tensor_copy(heads(arz, par)[rows, :, 0:C], KK[rows, :, span(c)])
                    last = nc.vector.tensor_copy(heads(arz, par)[rows, :, C:P], L[rows, :, span(c)])
                last.then_inc(ar_staged.handle, 1)

            def stage_k(c):
                dve.wait_ge(k_scaled.handle, k_scaled.at(c + 1))
                if c >= 1:
                    dve.wait_ge(bkt_done.handle, bkt_done.at(2 * c))
                nc.vector.tensor_copy(bk[LO, :, C:P], K[LO, :, span(c)])
                nc.vector.tensor_copy(bk[HI, :, 0:C], K[HI, :, span(c)]).then_inc(k_staged.handle, 1)

            def mask_g(c, upto):
                if c == 2:
                    dve.wait_ge(h_spilled.handle, h_spilled.at(16))
                if c == 4:
                    dve.wait_ge(g_spilled.handle, g_spilled.at(16))
                if c >= 6:
                    dve.wait_ge(y_done.handle, y_done.at(2 * (c - 5)))
                if c + 1 < upto:
                    scale(c + 1)
                for q in range(4):
                    dve.wait_ge(g_done.handle, g_done.at(4 * c + q + 1))
                    if q == 3 and c + 1 < upto:
                        stage_ar(c + 1)
                    nc.vector.tensor_tensor(gs[c][:, :, 4 * q:4 * q + 4, :].rearrange("p a h c -> p h a c"),
                                            g_bank(c, q)[:, :].rearrange("p (h a c) -> p h a c", a=2, c=C),
                                            gmask.rearrange("p (a c) -> p a c", c=C).unsqueeze(1).to_broadcast([P, 4, 2, C]),
                                            ALU.mult).then_inc(g_evac.handle, 1)

            def invert_begin(b):
                dve.wait_ge(gathered.handle, gathered.at(b + 1))
                dve.wait_ge(bkt_done.handle, bkt_done.at(2 * BC * (b + 1)))
                nc.vector.transpose(a32, ad).then_inc(step.handle, 1)
                nc.vector.memset(t32, 0.0).then_inc(step.handle, 1)
                steps[0] += 2
                dve.wait_ge(step.handle, step.at(steps[0]))
                nc.vector.memset(m.view(A_T32, Q * Q)[:, 0:Q * Q:Q + 1], 1.0).then_inc(step.handle, 1)
                steps[0] += 1

            def invert(lo, hi):
                for s in range(lo, hi):
                    n = Q - 1 - s
                    halves = [slice(par, s + 1, 2) for par in range(min(2, s + 1))]
                    width = [len(range(s + 1)[h]) for h in halves]
                    prod = [m.view(A_PROD + 512 * par, n, w) for par, w in enumerate(width)]
                    before = steps[0]
                    for par, h in enumerate(halves):
                        dve.wait_ge(step.handle, step.at(before if s < 2 else before - 1 + par))
                        nc.vector.tensor_tensor(prod[par], a32[:, s + 1:Q, s:s + 1].to_broadcast([P, n, width[par]]),
                                                wide(t32[:, s, h], n), ALU.mult).then_inc(step.handle, 1)
                    for par, h in enumerate(halves):
                        dve.wait_ge(step.handle, step.at(before + par + 1))
                        nc.vector.tensor_tensor(t32[:, s + 1:Q, h], t32[:, s + 1:Q, h], prod[par], ALU.subtract)\
                            .then_inc(step.handle, 1)
                    steps[0] += 2 * len(halves)

            def invert_end():
                dve.wait_ge(step.handle, step.at(steps[0]))
                nc.vector.transpose(tt, t32.rearrange("p t s -> p s t")).then_inc(t_turned.handle, 1)
                nc.vector.transpose(uu, t32).then_inc(u_turned.handle, 1)

            def place_transpose(b):
                dve.wait_ge(u_turned.handle, u_turned.at(b + 1))
                if b == 0:
                    dve.wait_ge(tu_cleared.handle, tu_cleared.at(1))
                for i in range(BC):
                    if b > 0:
                        dve.wait_ge(us_ready.handle, us_ready.at(2 * (BC * (b - 1) + i + 1)))
                    for g in range(4):
                        rows, at = slice(Q * g, Q * g + Q), C + Q * (g % 2)
                        last = nc.vector.tensor_copy(tu[i][rows, :, at:at + Q],
                                                     uu[rows, :, KT * i:KT * i + KT].rearrange("p c n -> p n c"))
                    last.then_inc(u_placed.handle, 1)

            def mask_x(c):
                for g in range(2):
                    dve.wait_ge(x_done.handle, x_done.at(2 * c + g + 1))
                    for par, rows in SIDES:
                        last = nc.vector.tensor_tensor(xs[rows, pairs[g], C * par:C * par + C], quarter(m.bank[g])[rows],
                                                       wide(xmask[rows], 4), ALU.mult)
                    last.then_inc(xs_ready.handle, 1)

            def complete_u(c):
                for g in range(2):
                    dve.wait_ge(xu_done.handle, xu_done.at(2 * c + g + 1))
                    for par, rows in SIDES:
                        last = nc.vector.tensor_tensor(us[rows, pairs[g], C * par:C * par + C], tu[c][rows, pairs[g], C:P],
                                                       quarter(m.bank[2 + g])[rows], ALU.subtract)
                    last.then_inc(us_ready.handle, 1)

            def advance(c):
                for g in range(2):
                    dve.wait_ge(s_done.handle, s_done.at(2 * c + g + 1))
                    nc.vector.tensor_tensor(S[:, pairs[g], :], S[:, pairs[g], :], quarter(m.bank[6 + g]), ALU.add)\
                        .then_inc(s_added.handle, 1)
                    dve.wait_ge(s_added.handle, s_added.at(2 * c + g + 1))
                    pc = m.view(A_PC + KT * c, KT)[:, pairs[g]].unsqueeze(2).to_broadcast([P, 4, C])
                    nc.vector.tensor_tensor(S[:, pairs[g], :], S[:, pairs[g], :], pc, ALU.mult).then_inc(s_ready.handle, 1)

            def clear_z(c):
                if c + 2 < NC:
                    nc.vector.memset(heads(z[c], 0)[LO], 0.0)
                    nc.vector.memset(heads(z[c], 1)[HI], 0.0).then_inc(z_cleared.handle, 1)

            for k in range(KT + 1):
                if k < KT:
                    nc.vector.tensor_tensor(dx[:, k, :], xt[:, k, 0:T], xt[:, k, 1:T + 1], ALU.subtract)\
                        .then_inc(dx_ready.handle, 1)
                if k > 0:
                    dve.wait_ge(dx_ready.handle, dx_ready.at(k))
                    mix("k", (k - 1,))
            link(nc.vector.tensor_scalar(omka, m.view(prm + RW_KA, 8), -1.0, 1.0, ALU.mult, ALU.add))
            nc.vector.memset(S, 0.0)
            for j in range(KT + 1):
                if j < KT:
                    dve.wait_ge(act_done.handle, act_done.at(place["k", j] + 1))
                    link(nc.vector.tensor_scalar(KK[:, j, :], K[:, j, :], col(RW_KK, j), None, ALU.mult))
                    if j >= 2:
                        dve.wait_ge(tile_done.handle, tile_done.at(place["n2", j - 2] + 1))
                    nc.vector.tensor_tensor(sq[j % 2], KK[:, j, :], KK[:, j, :], ALU.mult).then_inc(kk_squared.handle, 1)
                    mix("w", (j,))
                    mix("a", (j,))
                if j > 0:
                    i = j - 1
                    dve.wait_ge(act_done.handle, act_done.at(place["n2", i] + 1))
                    link(nc.vector.tensor_scalar(rt, rt, 1e-12, None, ALU.max))
                    link(nc.vector.reciprocal(rt, rt))
                    nc.vector.tensor_tensor(KK[:, i, :], KK[:, i, :], rt, ALU.mult).then_inc(root_used.handle, 1)
            dve.wait_ge(tile_done.handle, tile_done.at(place["lora", 0] + 1))
            mix("r")
            dve.wait_ge(aux.handle, aux.at(48))
            for j in range(KT):
                dve.wait_ge(act_done.handle, act_done.at(place["decay", j] + 1))
                nc.vector.tensor_tensor_scan(out=L[:, j, :], data0=reset, data1=sig[j % 2], initial=0.0,
                                             op0=ALU.mult, op1=ALU.add).then_inc(sig_used.handle, 1)
            mix("v")
            dve.wait_ge(act_done.handle, act_done.at(place["a", KT - 1] + 1))
            dve.wait_ge(root_used.handle, root_used.at(KT))
            for j in range(KT):
                link(nc.vector.tensor_scalar(sq[j % 2], BB[:, j, :], col(RW_KA, j), omka[:, j:j + 1], ALU.mult, ALU.add))
                nc.vector.tensor_tensor(K[:, j, :], K[:, j, :], sq[j % 2], ALU.mult)
                last = nc.vector.tensor_tensor(BB[:, j, :], BB[:, j, :], KK[:, j, :], ALU.mult)
            last.then_inc(keys_ready.handle, 1)
            mix("g")
            scale(0)
            stage_ar(0)
            stage_k(0)
            for c in range(BC):
                mask_g(c, BC)
                if c + 1 < BC:
                    stage_k(c + 1)
            invert_begin(0)
            invert(0, Q - 1)
            invert_end()
            scale(BC)
            stage_k(BC)
            for j in range(KT):
                dve.wait_ge(act_done.handle, act_done.at(place["g", j] + 1))
                nc.vector.tensor_tensor(G[:, j, :], tile_bank(place["g", j])[:, :], G[:, j, :], ALU.mult)\
                    .then_inc(gated.handle, 1)
                if j >= KT - SLOTS:
                    last = nc.vector.memset(m.view(m.slot(n0 + 25 + j), 1024), 0.0)
            last.then_inc(tu_cleared.handle, 1)
            place_transpose(0)
            dve.wait_ge(carry_cleared.handle, carry_cleared.at(2))
            mask_x(0)
            complete_u(0)
            stage_ar(BC)
            for c in range(NC):
                if c == 0:
                    mask_g(4, NC)
                if c == 1:
                    mask_g(6, NC)
                if c == 3:
                    invert(FIRST, Q - 1)
                    invert_end()
                advance(c)
                if c < 2:
                    stage_k((5, 7)[c])
                if c == 3:
                    place_transpose(1)
                if c + 1 < NC:
                    mask_x(c + 1)
                    complete_u(c + 1)
                clear_z(c)
                if c == 0:
                    mask_g(5, NC)
                    stage_k(6)
                if c == 1:
                    mask_g(7, NC)
                    invert_begin(1)
                    invert(0, FIRST)

        @block.tensor
        def _(pe):
            mm = lambda out, a, b, start=True, stop=True: nc.tensor.matmul(out, a, b, start=start, stop=stop,
                                                                          skip_group_check=True)
            slot_used = [n0]

            def project(n):
                what, j = tiles[n]
                bank = tile_bank(n)
                if what == "g" and j >= 2:
                    pe.wait_ge(gated.handle, gated.at(j - 1))
                elif what in "vg":
                    pe.wait_ge(act_done.handle, act_done.at(n - 1 if j >= 2 or what == "g" else place["r", KT - 1] + 1))
                elif n >= 8:
                    pe.wait_ge(act_done.handle, act_done.at(n - 8 + 1))
                if what in ("decay", "a"):
                    if (what, j) == ("decay", 0):
                        pe.wait_ge(act_done.handle, act_done.at(place["lora", 0] + 1))
                        pe.wait_ge(aux.handle, aux.at(48))
                    h = slice(0, 64) if what == "decay" else slice(64, 128)
                    last = nc.tensor.matmul(bank[:, :], w2a2_sb[h, j * P:(j + 1) * P], lora[h, :], start=True, stop=True)
                elif what == "n2":
                    pe.wait_ge(kk_squared.handle, kk_squared.at(j + 1))
                    last = nc.tensor.matmul(bank[:, :], bones, sq[j % 2], start=True, stop=True)
                else:
                    m.weights_arrived(pe, slot_used[0])
                    slot = m.view(m.slot(slot_used[0]), KT, P)
                    slot_used[0] += 1
                    if what == "lora":
                        pe.wait_ge(mixed.handle, mixed.at(3 * KT))
                    for k in range(KT):
                        if what == "lora":
                            mm(bank[0:64, :], slot[:, k, 0:64], mix_at["w"][:, k, :], k == 0, k == KT - 1)
                            last = mm(bank[64:128, :], slot[:, k, 64:128], mix_at["a"][:, k, :], k == 0, k == KT - 1)
                            continue
                        if j == 0:
                            pe.wait_ge(mixed.handle, mixed.at(KT * mixes.index(what) + k + 1))
                        last = nc.tensor.matmul(bank[:, :], slot[:, k, :], mix_at[what][:, k, :], start=k == 0,
                                                stop=k == KT - 1)
                last.then_inc(tile_done.handle, 1)

            given = {"values": 0, "x": 0, "xu": 0, "pairs": 0, "turned": 0}

            def banks_01_read():
                pe.wait_ge(v_evac.handle, v_evac.at(2 * given["values"]))
                pe.wait_ge(xs_ready.handle, xs_ready.at(2 * given["x"]))
                pe.wait_ge(g_evac.handle, g_evac.at(4 * given["pairs"]))

            def banks_23_read():
                pe.wait_ge(us_ready.handle, us_ready.at(2 * given["xu"]))
                pe.wait_ge(g_evac.handle, g_evac.at(4 * given["pairs"]))
                pe.wait_ge(bkt_evac.handle, bkt_evac.at(2 * given["turned"]))

            def multiply_pairs(c, qs):
                for q in qs:
                    if c < BC and c > 0:
                        pe.wait_ge(g_evac.handle, g_evac.at(4 * (c - 1) + q + 1))
                    for k in range(2):
                        last = mm(g_bank(c, q)[:, 256 * k:256 * k + 256], bk[:, 2 * q + k, :],
                                  arz[:, 4 * q + 2 * k:4 * q + 2 * k + 2, :])
                    last.then_inc(g_done.handle, 1)

            def turn_bk(c):
                for q in range(2):
                    if c < BC and c > 0:
                        pe.wait_ge(bkt_evac.handle, bkt_evac.at(2 * (c - 1) + q + 1))
                    for k in range(4):
                        last = nc.tensor.transpose(t_bank(c, q)[:, P * k:P * k + P], bk[:, 4 * q + k, :], ident)
                    last.then_inc(bkt_done.handle, 1)

            def staged(c):
                pe.wait_ge(ar_staged.handle, ar_staged.at(c + 1))
                pe.wait_ge(k_staged.handle, k_staged.at(c + 1))
                pe.wait_ge(b_staged.handle, b_staged.at(c + 1))

            def pairs_first(c):
                staged(c)
                banks_23_read()
                multiply_pairs(c, (0, 1))

            def pairs_second(c):
                banks_01_read()
                multiply_pairs(c, (2, 3))
                given["pairs"] = c + 1

            def pairs_turned(c):
                banks_23_read()
                turn_bk(c)
                given["turned"] = c + 1

            def turn_values(c):
                banks_01_read()
                for q in range(2):
                    for k in range(4):
                        last = nc.tensor.transpose(m.bank[q][LO, P * k:P * k + P], V[:, 4 * q + k, span(c)], ident)
                    last.then_inc(v_done.handle, 1)
                given["values"] = c + 1

            def x(c):
                banks_01_read()
                pe.wait_ge(t_placed.handle, t_placed.at(c + 1))
                for g in range(2):
                    for k in range(4):
                        p = 4 * g + k
                        for par, rows in SIDES:
                            last = mm(m.bank[g][rows, C * k:C * k + C], gs[c][rows, 0, 2 * p + par, :], tu[c][rows, p, 0:C])
                    last.then_inc(x_done.handle, 1)
                given["x"] = c + 1

            def xu(c):
                banks_23_read()
                pe.wait_ge(u_placed.handle, u_placed.at(c + 1))
                for g in range(2):
                    pe.wait_ge(xs_ready.handle, xs_ready.at(2 * c + g + 1))
                    for k in range(4):
                        p = 4 * g + k
                        last = mm(m.bank[2 + g][:, C * k:C * k + C], xs[:, p, :], tu[c][:, p, C:P])
                    last.then_inc(xu_done.handle, 1)
                given["xu"] = c + 1

            def right_side(c):
                for g in range(2):
                    pe.wait_ge(v_evac.handle, v_evac.at(2 * c + g + 1))
                    if c >= 2:
                        pe.wait_ge(z_cleared.handle, z_cleared.at(c - 1))
                    if c >= 1:
                        pe.wait_ge(y_evac.handle, y_evac.at(2 * (c - 1) + g + 1))
                    bank = m.bank[4 + g]
                    for p in range(4 * g, 4 * g + 4):
                        at = P * (p % 4)
                        mm(bank[:, at:at + P], gs[c][:, 0, 2 * p:2 * p + 2, :], z[c][:, 2 * p:2 * p + 2, :], p % 4 == 0, False)
                    if c >= 1:
                        pe.wait_ge(s_ready.handle, s_ready.at(2 * (c - 1) + g + 1))
                    for p in range(4 * g, 4 * g + 4):
                        for par, rows in SIDES:
                            at = P * (p % 4) + C * par
                            last = mm(bank[rows, at:at + C], KK[rows, p, span(c)], S[rows, p, :], False, p % 4 == 3)
                    last.then_inc(rhs_done.handle, 1)

            def solve(c):
                for g in range(2):
                    pe.wait_ge(rhs_evac.handle, rhs_evac.at(2 * c + g + 1))
                    pe.wait_ge(us_ready.handle, us_ready.at(2 * c + g + 1))
                    for k in range(4):
                        p = 4 * g + k
                        last = mm(m.bank[6 + g][:, C * k:C * k + C], us[:, p, :], rhs[:, p, :])
                    last.then_inc(sa_done.handle, 1)

            def outputs(c):
                for g in range(2):
                    bank = m.bank[4 + g]
                    for p in range(4 * g, 4 * g + 4):
                        for par, rows in SIDES:
                            at = P * (p % 4) + C * par
                            mm(bank[rows, at:at + C], S[rows, p, :], L[rows, p, span(c)], p % 4 == 0, False)
                    pe.wait_ge(sa_evac.handle, sa_evac.at(2 * c + g + 1))
                    for p in range(4 * g, 4 * g + 4):
                        at = P * (p % 4)
                        last = mm(bank[:, at:at + P], z[c][:, 2 * p:2 * p + 2, :], gs[c][:, 1, 2 * p:2 * p + 2, :], False, p % 4 == 3)
                    last.then_inc(y_done.handle, 1)
                    for k in range(4):
                        p = 4 * g + k
                        for par, rows in SIDES:
                            last = mm(m.bank[6 + g][rows, C * k:C * k + C], (BB, K)[par][:, p, span(c)], z[c][:, 2 * p + par, :])
                    last.then_inc(s_done.handle, 1)

            for n in range(place["v", 0]):
                project(n)
            pe.wait_ge(act_done.handle, act_done.at(place["v", 0]))
            for c in range(BC):
                project(place["v", c])
                staged(c)
                multiply_pairs(c, range(4))
                turn_bk(c)
            given.update(pairs=BC, turned=BC)
            for n in range(place["v", BC], len(tiles)):
                project(n)
            turn_values(0)
            pe.wait_ge(gated.handle, gated.at(KT))
            for c in range(NC):
                right_side(c)
                if c % BC == 0:
                    x(c)
                    xu(c)
                if c + 1 < NC:
                    turn_values(c + 1)
                extra = {0: 4, 1: 6}.get(c)
                if c == 0:
                    solve(c)
                    pairs_first(extra)
                elif extra:
                    pairs_first(extra)
                    solve(c)
                else:
                    solve(c)
                if extra:
                    pairs_second(extra)
                outputs(c)
                if extra:
                    pairs_turned(extra)
                if (c + 1) % BC:
                    x(c + 1)
                    xu(c + 1)
                if extra:
                    pairs_first(extra + 1)
                    pairs_second(extra + 1)
                    pairs_turned(extra + 1)
    for s, n in ((dx_ready, KT), (mixed, 6 * KT), (tile_done, len(tiles)), (act_done, len(tiles)), (gated, KT), (kk_squared, KT),
                 (chain, links[0]), (act_chain, 1), (aux, 48), (root_used, KT), (sig_used, KT), (keys_ready, 1),
                 (h_spilled, 16), (g_spilled, 16), (reloaded, 32), (ep_cleared, 1), (exp_ready, NC), (ar_scaled, NC),
                 (ar_staged, NC), (k_staged, NC), (b_scaled, NC), (k_scaled, NC), (b_staged, NC), (g_done, 4 * NC), (g_evac, 4 * NC),
                 (bkt_done, 2 * NC), (bkt_evac, 2 * NC), (gathered, 2), (step, steps[0]), (t_turned, 2), (u_turned, 2),
                 (tu_cleared, 1), (t_placed, NC), (u_placed, NC), (carry_cleared, 2), (z_cleared, NC - 2)):
        s.base += n
    for s in (v_done, v_evac, x_done, xs_ready, xu_done, us_ready, s_added, rhs_done, rhs_evac, sa_done, sa_evac, y_done,
              y_evac, s_done, s_ready):
        s.base += 2 * NC


RW_OUT_BANKS = ((1, 2, 3, 4), (5, 6, 0, 7))


def rw_gate_out(m, prm, w_out, pick_src, norm, final_g=None, out=None):
    nc = m.nc
    R, V, G, Y, sq = (m.view(b, KT, T) for b in (B_R, B_V, B_G, B_KK, B_L))
    W = m.view(B_K, KT, D)
    bones_rk = m.view(A_XT, KT, P)
    pick = m.view(A_XT + KT * P, D)
    rstd = m.view(A_DX, T)
    bones, centre = m.view(A_CONST + C_BONES, P), m.view(A_CONST + C_CENTRE, P)
    compact = lambda j: m.view(A_CONST + C_COMPACT + 14 - 2 * j, NH)
    fg = m.view(B_R, D)
    eps = m.view(A_SMALL + 40, 1)
    col = lambda at, k: m.view(prm + at + k, 1)
    ready, centred_done, centred, squared, var_done, root, inverse, pick_loaded = (m.sem(n) for n in (
        "weights_rk_ready", "centred_done", "centred", "squared", "var_done", "root_ready", "rstd_ready", "pick_loaded"))
    bonus_done, bonus_used, spread_done, spread_used, finished, out_done, out_read, chain = (m.sem(n) for n in (
        "bonus_done", "bonus_used", "spread_done", "spread_used", "y_finished", "out_done", "out_read", "dve_chain"))
    w_loaded = [m.sem(f"w_out{k}_loaded") for k in range(KT)]
    spread_bank = lambda j: m.bank[(0, 7)[j % 2]]
    bonus_bank = lambda j: m.bank[1 + j if j < 6 else j - 1]
    added, fg_loaded, stored = m.sem("h_added"), m.sem("final_g_loaded"), m.sem("stored")
    links = [0]

    with nc.Block() as block:
        @block.sync
        def _(sp):
            sp.dma_start(pick[0:NH, :], pick_src).then_inc(pick_loaded.handle, 16)
            for k in range(KT):
                sp.dma_start(W[:, k, :], w_out[k * P:(k + 1) * P, :]).then_inc(w_loaded[k].handle, 16)
            if out is not None:
                sp.wait_ge(bonus_done.handle, bonus_done.at(KT))
                sp.dma_start(fg, final_g.unsqueeze(0).to_broadcast([P, D])).then_inc(fg_loaded.handle, 16)
                for a in range(NT):
                    sp.wait_ge(norm.scaled.handle, norm.scaled.at(a + 1))
                    sp.dma_start(out[0, a * P:(a + 1) * P, :], norm.h[:, a, :]).then_inc(stored.handle, 16)
                sp.wait_ge(stored.handle, 16 * NT)

        @block.scalar
        def _(act):
            act.wait_ge(ready.handle, ready.at(1))
            for j in range(KT):
                act.wait_ge(centred_done.handle, centred_done.at(j + 1))
                nc.scalar.activation(sq[:, j, :], m.bank[j][:, :], ACT.Square).then_inc(squared.handle, 1)
            act.wait_ge(var_done.handle, var_done.at(1))
            nc.scalar.activation(rstd[0:NH, :], m.bank[0][0:NH, :], ACT.Sqrt, bias=eps[0:NH, :], scale=1.0 / C)\
                .then_inc(root.handle, 1)
            norm.act_steps(act, lambda act, a: act.wait_ge(added.handle, added.at(NT + a + 1)))

        @block.vector
        def _(dve):
            def link(ins):
                links[0] += 1
                ins.then_inc(chain.handle, 1)
                dve.wait_ge(chain.handle, chain.at(links[0]))

            def add_bonus(j):
                dve.wait_ge(bonus_done.handle, bonus_done.at(j + 1))
                nc.vector.tensor_tensor(V[:, j, :], bonus_bank(j)[:, :], V[:, j, :], ALU.mult).then_inc(bonus_used.handle, 1)

            nc.vector.memset(eps, 64e-5).then_inc(ready.handle, 1)
            for j in range(KT):
                dve.wait_ge(squared.handle, squared.at(j + 1))
                nc.vector.tensor_copy(Y[:, j, :], m.bank[j][:, :]).then_inc(centred.handle, 1)
                nc.vector.tensor_scalar(bones_rk[:, j, :], bones, col(RW_RK, j), None, ALU.mult).then_inc(ready.handle, 1)
            dve.wait_ge(root.handle, root.at(1))
            nc.vector.reciprocal(rstd[0:NH, :], rstd[0:NH, :]).then_inc(inverse.handle, 1)
            for j in range(4):
                add_bonus(j)
            for j in range(KT):
                dve.wait_ge(spread_done.handle, spread_done.at(j + 1))
                nc.vector.scalar_tensor_tensor(out=Y[:, j, :], in0=Y[:, j, :], scalar=col(RW_LNG, j),
                                               in1=spread_bank(j)[:, :], op0=ALU.mult, op1=ALU.mult)\
                    .then_inc(spread_used.handle, 1)
                dve.wait_ge(spread_used.handle, spread_used.at(j + 1))
                dve.wait_ge(bonus_used.handle, bonus_used.at(j + 1))
                link(nc.vector.scalar_tensor_tensor(out=Y[:, j, :], in0=Y[:, j, :], scalar=col(RW_LNB, j), in1=V[:, j, :],
                                                    op0=ALU.add, op1=ALU.add))
                nc.vector.tensor_tensor(Y[:, j, :], Y[:, j, :], G[:, j, :], ALU.mult).then_inc(finished.handle, 1)
                if j + 4 < KT:
                    add_bonus(j + 4)

            def add(dve, n):
                dve.wait_ge(out_done.handle, out_done.at(n + 1))
                part = norm.h[:, n % NT, 512 * (n // NT):512 * (n // NT) + 512]
                nc.vector.tensor_tensor(part, part, m.bank[RW_OUT_BANKS[n // NT][n % NT]][:, :], ALU.add)\
                    .then_inc(added.handle, 1)

            for a in range(NT):
                add(dve, a)
            if out is None:
                nc.vector.memset(norm.xt[:, :, 0:1], 0.0)
                norm.dve_steps(dve, lambda dve, a: add(dve, NT + a))
            else:
                dve.wait_ge(fg_loaded.handle, fg_loaded.at(16))
                norm.dve_steps(dve, lambda dve, a: add(dve, NT + a), fg)

        @block.tensor
        def _(pe):
            def spread(j):
                if j >= 2:
                    pe.wait_ge(spread_used.handle, spread_used.at(j - 1))
                nc.tensor.matmul(spread_bank(j)[:, :], pick[0:NH, j * P:(j + 1) * P], rstd[0:NH, :], start=True, stop=True)\
                    .then_inc(spread_done.handle, 1)

            def bonus(j):
                pe.wait_ge(ready.handle, ready.at(j + 2))
                if j < 6:
                    pe.wait_ge(centred.handle, centred.at(j + 2))
                else:
                    pe.wait_ge(bonus_used.handle, bonus_used.at(j - 1))
                nc.tensor.matmul(bonus_bank(j)[:, :], bones_rk[:, j, :], R[:, j, :], start=True, stop=True)\
                    .then_inc(bonus_done.handle, 1)

            def out_product(half, a, k):
                nc_out = m.bank[RW_OUT_BANKS[half][a]]
                return nc.tensor.matmul(nc_out[:, :], Y[:, k, a * P:(a + 1) * P], W[:, k, 512 * half:512 * half + 512],
                                        start=k == 0, stop=k == KT - 1)

            for j in range(KT):
                nc.tensor.matmul(m.bank[j][:, :], centre, Y[:, j, :], start=True, stop=True).then_inc(centred_done.handle, 1)
            pe.wait_ge(centred.handle, centred.at(1))
            for j in range(KT):
                pe.wait_ge(squared.handle, squared.at(j + 1))
                last = nc.tensor.matmul(m.bank[0][0:NH, :], compact(j), sq[:, j, :], start=j == 0, stop=j == KT - 1)
            last.then_inc(var_done.handle, 1)
            for j in range(6):
                bonus(j)
            pe.wait_ge(inverse.handle, inverse.at(1))
            pe.wait_ge(pick_loaded.handle, pick_loaded.at(16))
            pe.wait_ge(centred.handle, centred.at(KT))
            spread(0)
            spread(1)
            for k in range(KT):
                pe.wait_ge(finished.handle, finished.at(k + 1))
                pe.wait_ge(w_loaded[k].handle, w_loaded[k].at(16))
                for a in range(NT):
                    if k == 0:
                        pe.wait_ge(bonus_used.handle, bonus_used.at(a + 1))
                    last = out_product(0, a, k)
                    if k == KT - 1:
                        last.then_inc(out_done.handle, 1)
                if k < 2:
                    bonus(6 + k)
                if k + 2 < KT:
                    spread(k + 2)
            for a in range(NT):
                for k in range(KT):
                    last = out_product(1, a, k)
                last.then_inc(out_done.handle, 1)
            if out is None:
                for a in range(NT):
                    norm.turn(pe, a)
    for s, n in ((ready, KT + 1), (centred_done, KT), (centred, KT), (squared, KT), (var_done, 1), (root, 1), (inverse, 1),
                 (pick_loaded, 16), (bonus_done, KT), (bonus_used, KT), (spread_done, KT), (spread_used, KT),
                 (finished, KT), (out_done, 8), (added, 8), (chain, links[0])):
        s.base += n
    norm.finish(out is not None)
    for s in w_loaded:
        s.base += 16


S_QKV = B_R
S_VS = S_QKV + 6144
S_QT = S_VS + 768
S_KT = S_QT + 4096
S_G = S_KT + 1024
S_Y = S_G + 4096
S_P = S_Y + 4096
S_PT = S_P + 2048
S_SK = S_PT + 2048
S_ROPE = S_SK + 64
SW_KV = 4


def sw_project(m, sinks, n0):
    nc = m.nc
    xt = m.view(A_XT, KT, T + 1)
    qkv = m.view(S_QKV, NT, 1536)
    vs = m.view(S_VS, 3, 256)
    qt, kt, G = m.view(S_QT, 8, T), m.view(S_KT, 2, T), m.view(S_G, KT, T)
    sk = m.view(S_SK, 8)
    rope = [m.view(S_ROPE + 160 * n, 20, 8) for n in range(4)]
    rtab = m.view(A_CONST + C_ROPE, 2, NT, 8)
    ident = m.view(A_CONST + C_ID, P)
    rows_used, q_done, qkv_evac, g_done, sig_done, g_used, turned, turn_evac, chain, sink, rotated = (m.sem(n) for n in (
        "sw_rows_used", "qkv_done", "qkv_evac", "tile_done", "act_evacuated", "g_gated", "qk_turned", "qk_evac",
        "dve_chain", "sinks_loaded", "rotated"))
    m.used_by += [(rows_used.handle, rows_used.at(k + 1)) for k in range(7)] + [(q_done.handle, q_done.at(8))]
    m.used_by += [(rows_used.handle, rows_used.at(7 + k + 1)) for k in range(3)] + [(q_done.handle, q_done.at(12))]
    m.used_by += [(g_done.handle, g_done.at(k + 1)) for k in range(KT)]
    count = [0]
    with nc.Block() as block:
        @block.sync
        def _(sp):
            sp.dma_start(sk[0:64, :], sinks[0:8].unsqueeze(0).to_broadcast([64, 8])).then_inc(sink.handle, 16)
            sp.dma_start(sk[64:128, :], sinks[8:16].unsqueeze(0).to_broadcast([64, 8])).then_inc(sink.handle, 16)
            m.load_weights(sp, n0 + 20 + SLOTS)

        @block.tensor
        def _(pe):
            w = n0
            for k in range(KT):
                m.weights_arrived(pe, w)
                slot = m.view(m.slot(w), D)
                for n in range(8):
                    last = nc.tensor.matmul(m.bank[n][:, :], xt[:, k, 1 + (n // 2) * P:1 + (n // 2 + 1) * P],
                                            slot[:, 512 * (n % 2):512 * (n % 2) + 512], start=k == 0, stop=k == KT - 1)
                    if k == KT - 1:
                        last.then_inc(q_done.handle, 1)
                if k < KT - 1:
                    last.then_inc(rows_used.handle, 1)
                w += 1
            for k2 in range(KT // 2):
                m.weights_arrived(pe, w)
                slot = m.view(m.slot(w), 2, 512)
                for n in range(NT):
                    if k2 == 0:
                        pe.wait_ge(qkv_evac.handle, qkv_evac.at(n + 1))
                    for k in range(2):
                        last = nc.tensor.matmul(m.bank[n][:, :], xt[:, 2 * k2 + k, 1 + n * P:1 + (n + 1) * P], slot[:, k, :],
                                                start=(k2, k) == (0, 0), stop=(k2, k) == (KT // 2 - 1, 1))
                    if k2 == KT // 2 - 1:
                        last.then_inc(q_done.handle, 1)
                if k2 < KT // 2 - 1:
                    last.then_inc(rows_used.handle, 1)
                w += 1
            for j in range(KT):
                m.weights_arrived(pe, w)
                slot = m.view(m.slot(w), KT, P)
                if j < 4:
                    pe.wait_ge(qkv_evac.handle, qkv_evac.at(4 + j + 1))
                else:
                    pe.wait_ge(g_used.handle, g_used.at(j - 3))
                for k in range(KT):
                    last = nc.tensor.matmul(m.bank[4 + j % 4][:, :], slot[:, k, :], xt[:, k, 1:T + 1], start=k == 0,
                                            stop=k == KT - 1)
                last.then_inc(g_done.handle, 1)
                w += 1
            for n in range(10):
                if n < 4:
                    pe.wait_ge(qkv_evac.handle, qkv_evac.at(12))
                    pe.wait_ge(rotated.handle, rotated.at(NT))
                else:
                    pe.wait_ge(turn_evac.handle, turn_evac.at(n - 3))
                for a in range(NT):
                    last = nc.tensor.transpose(m.bank[n % 4][:, a * P:(a + 1) * P], qkv[:, a, n * P:(n + 1) * P], ident)
                last.then_inc(turned.handle, 1)

        @block.scalar
        def _(act):
            for n in range(8):
                act.wait_ge(q_done.handle, q_done.at(n + 1))
                nc.scalar.activation(qkv[:, n // 2, 0:D].rearrange("p (h f c) -> p h f c", f=2, c=C)[:, :, n % 2, :],
                                     m.bank[n][:, :].rearrange("p (h c) -> p h c", c=C), ACT.Copy).then_inc(qkv_evac.handle, 1)
            for n in range(4):
                act.wait_ge(q_done.handle, q_done.at(8 + n + 1))
                for f in range(2):
                    nc.scalar.activation(qkv[:, n, D:D + 256].rearrange("p (h f c) -> p h f c", f=2, c=C)[:, :, f, :],
                                         m.bank[n][:, P * f:P * f + P].rearrange("p (h c) -> p h c", c=C), ACT.Copy)
                nc.scalar.activation(qkv[:, n, D + 256:D + 512], m.bank[n][:, 256:512], ACT.Copy).then_inc(qkv_evac.handle, 1)
            for j in range(KT):
                act.wait_ge(g_done.handle, g_done.at(j + 1))
                nc.scalar.activation(G[:, j, :], m.bank[4 + j % 4][:, :], ACT.Sigmoid).then_inc(sig_done.handle, 1)
            for n in range(10):
                act.wait_ge(turned.handle, turned.at(n + 1))
                nc.scalar.activation(qt[:, n, :] if n < 8 else kt[:, n - 8, :], m.bank[n % 4][:, :], ACT.Copy)\
                    .then_inc(turn_evac.handle, 1)

        @block.vector
        def _(dve):
            def link(ins):
                count[0] += 1
                ins.then_inc(chain.handle, 1)
                dve.wait_ge(chain.handle, chain.at(count[0]))

            for a in range(NT):
                dve.wait_ge(qkv_evac.handle, qkv_evac.at(8 + a + 1))
                qk = qkv[:, a, 0:1280].rearrange("p (h c) -> p h c", c=C)
                x1, x2 = qk[:, :, 0:8], qk[:, :, 8:16]
                cos, sin = (rtab[:, n, a, :].unsqueeze(1).to_broadcast([P, 20, 8]) for n in range(2))
                for n, (u, v) in enumerate(((x1, cos), (x2, sin), (x2, cos), (x1, sin))):
                    ins = nc.vector.tensor_tensor(rope[n], u, v, ALU.mult)
                link(ins)
                nc.vector.tensor_tensor(x1, rope[0], rope[1], ALU.subtract)
                nc.vector.tensor_tensor(x2, rope[2], rope[3], ALU.add).then_inc(rotated.handle, 1)
                dve.wait_ge(rotated.handle, rotated.at(a + 1))
            for i in range(3):
                nc.vector.tensor_copy(vs[0:64, i, :], qkv[64:128, i, 1280:1536])
                nc.vector.tensor_copy(vs[64:128, i, :], qkv[0:64, i + 1, 1280:1536])
            for j in range(KT):
                dve.wait_ge(sig_done.handle, sig_done.at(j + 1))
                nc.vector.tensor_tensor(G[:, j, :], m.bank[4 + j % 4][:, :], G[:, j, :], ALU.mult).then_inc(g_used.handle, 1)
    for s, n in ((rows_used, 10), (q_done, 12), (qkv_evac, 12), (g_done, KT), (sig_done, KT), (g_used, KT), (turned, 10),
                 (turn_evac, 10), (chain, count[0]), (sink, 32), (rotated, NT)):
        s.base += n


def sw_attend(m):
    nc = m.nc
    qkv = m.view(S_QKV, NT, 1536)
    vs = m.view(S_VS, 3, 256)
    qt, kt, G, Y = m.view(S_QT, 8, T), m.view(S_KT, 2, T), m.view(S_G, KT, T), m.view(S_Y, KT, T)
    prob = [m.view(S_P + 1024 * n, 8, P) for n in range(2)]
    pt = [m.view(S_PT + 1024 * n, 8, P) for n in range(2)]
    sk = m.view(S_SK, 8)
    small = [m.view(S_ROPE + 64 * n, 8, 8) for n in range(2)]
    ident = m.view(A_CONST + C_ID, P)
    s_done, s_max, s_exp, es_done, normed, p_turned, p_evac, o_done, o_evac, chain, sink = (m.sem(n) for n in (
        "scores_done", "score_max", "scores_exp", "sink_exp", "probs_normed", "probs_turned", "probs_evac", "o_done",
        "o_evac", "dve_chain", "sinks_loaded"))
    count = [0]
    keys = lambda c: C if c == 0 else P
    with nc.Block() as block:
        def gate(dve, c):
            dve.wait_ge(o_done.handle, o_done.at(c + 1))
            nc.vector.tensor_tensor(Y[:, :, c * C:(c + 1) * C], m.bank[6 + c % 2][:, :].rearrange("p (k t) -> p k t", t=C),
                                    G[:, :, c * C:(c + 1) * C], ALU.mult).then_inc(o_evac.handle, 1)

        def evac(act, c):
            for q in range(2):
                act.wait_ge(p_turned.handle, p_turned.at(2 * c + q + 1))
                if q == 0 and c >= 2:
                    act.wait_ge(o_done.handle, o_done.at(c - 1))
                nc.scalar.activation(pt[c % 2][0:keys(c), 4 * q:4 * q + 4, :], m.bank[4 + q][0:keys(c), :], ACT.Copy)\
                    .then_inc(p_evac.handle, 1)

        @block.tensor
        def _(pe):
            def scores(c):
                if c >= 2:
                    pe.wait_ge(s_exp.handle, s_exp.at(c - 1))
                for h in range(8):
                    bank = m.bank[2 * (c % 2) + h // 4]
                    for f, rows in ((0, slice(0, 64)), (1, slice(64, 128))):
                        last = nc.tensor.matmul(bank[rows, P * (h % 4):P * (h % 4) + keys(c)], qt[rows, h, c * C:(c + 1) * C],
                                                kt[rows, h // 4, (c + 1) * C - keys(c):(c + 1) * C], start=True, stop=True,
                                                skip_group_check=True)
                last.then_inc(s_done.handle, 1)

            def turn(c):
                pe.wait_ge(normed.handle, normed.at(c + 1))
                for q in range(2):
                    if c >= 1:
                        pe.wait_ge(p_evac.handle, p_evac.at(2 * c - 1 + q))
                    for k in range(4):
                        last = nc.tensor.transpose(m.bank[4 + q][0:keys(c), P * k:P * k + P], prob[c % 2][:, 4 * q + k, 0:keys(c)],
                                                   ident)
                    last.then_inc(p_turned.handle, 1)

            def outputs(c):
                if c >= 2:
                    pe.wait_ge(o_evac.handle, o_evac.at(c - 1))
                v = qkv[:, c // 2, 1280:1536] if c % 2 or c == 0 else vs[:, c // 2 - 1, :]
                pe.wait_ge(p_evac.handle, p_evac.at(2 * c + 2))
                for h in range(8):
                    for f in range(2):
                        out = slice(64 * (h % 2), 64 * (h % 2) + 64)
                        kv = h // 4 + 2 * f
                        at = C * (h // 2 + 4 * f)
                        last = nc.tensor.matmul(m.bank[6 + c % 2][out, at:at + C], v[0:keys(c), C * kv:C * kv + C],
                                                pt[c % 2][0:keys(c), h, C * f:C * f + C], start=True, stop=True,
                                                skip_group_check=True)
                last.then_inc(o_done.handle, 1)

            scores(0)
            scores(1)
            for c in range(NC):
                if c + 2 < NC:
                    scores(c + 2)
                turn(c)
                if c >= 1:
                    outputs(c - 1)
            outputs(NC - 1)

        @block.scalar
        def _(act):
            def exps(c):
                p, st = prob[c % 2], small[c % 2]
                act.wait_ge(s_max.handle, s_max.at(c + 1))
                if c >= 2:
                    act.wait_ge(p_turned.handle, p_turned.at(2 * (c - 1)))
                nc.scalar.activation(st[:, 2, :], st[:, 1, :], ACT.Exp)
                for h in range(8):
                    bank = m.bank[2 * (c % 2) + h // 4]
                    last = nc.scalar.activation(p[:, h, 0:keys(c)], bank[:, P * (h % 4):P * (h % 4) + keys(c)], ACT.Exp,
                                                bias=st[:, 0, h:h + 1], scale=C ** -0.5, accum_out=st[:, 3, h:h + 1])
                last.then_inc(s_exp.handle, 1)

            exps(0)
            for c in range(NC):
                if c + 1 < NC:
                    exps(c + 1)
                evac(act, c)

        @block.vector
        def _(dve):
            def link(ins):
                count[0] += 1
                ins.then_inc(chain.handle, 1)
                dve.wait_ge(chain.handle, chain.at(count[0]))

            def maxima(c):
                st = small[c % 2]
                dve.wait_ge(s_done.handle, s_done.at(c + 1))
                for q in range(2):
                    bank = m.bank[2 * (c % 2) + q][:, :].rearrange("p (h k) -> p h k", k=P)[:, :, 0:keys(c)]
                    ins = nc.vector.tensor_reduce(st[:, 0, 4 * q:4 * q + 4], bank, AX.X, ALU.max)
                link(ins)
                link(nc.vector.tensor_scalar(st[:, 0, :], st[:, 0, :], C ** -0.5, None, ALU.mult))
                link(nc.vector.tensor_tensor(st[:, 0, :], st[:, 0, :], sk, ALU.max))
                link(nc.vector.tensor_tensor(st[:, 1, :], sk, st[:, 0, :], ALU.subtract))
                nc.vector.tensor_scalar(st[:, 0, :], st[:, 0, :], -1.0, None, ALU.mult).then_inc(s_max.handle, 1)

            dve.wait_ge(sink.handle, sink.at(0))
            maxima(0)
            for c in range(NC):
                st, p = small[c % 2], prob[c % 2]
                if c + 1 < NC:
                    maxima(c + 1)
                dve.wait_ge(s_exp.handle, s_exp.at(c + 1))
                link(nc.vector.tensor_tensor(st[:, 3, :], st[:, 3, :], st[:, 2, :], ALU.add))
                link(nc.vector.reciprocal(st[:, 3, :], st[:, 3, :]))
                nc.vector.tensor_tensor(p[:, :, 0:keys(c)], p[:, :, 0:keys(c)], st[:, 3, :].unsqueeze(2).to_broadcast([P, 8, keys(c)]),
                                        ALU.mult).then_inc(normed.handle, 1)
                if c >= 2:
                    gate(dve, c - 2)
            gate(dve, NC - 2)
            gate(dve, NC - 1)

    for s, n in ((s_done, NC), (s_max, NC), (s_exp, NC), (normed, NC), (p_turned, 2 * NC), (p_evac, 2 * NC), (o_done, NC),
                 (o_evac, NC), (chain, count[0])):
        s.base += n


ML_H, ML_V = 4, 256
M_U = B_R
M_C = M_U + KT * (T + 3)
M_Z = M_C + 4096
M_V = M_Z + 4096
M_HM = M_V + NT * ML_H * (ML_V + 1)
M_Q = M_HM + 4096
M_K = M_Q + 2048
M_QS = M_K + 2048
M_E = M_QS + 2048
M_SI = M_E + 2048
M_KTOK = M_SI + 2048
M_STATE = M_KTOK + 2048
M_SM = M_STATE + ML_H * (ML_V + 1)
M_XT = A_END - KT * (T + 1)
M_ROWS = M_HM
M_Y = M_U


def ml_project(m, w_if, i_bias, f_bias, rows_src, n0):
    nc = m.nc
    xt = m.view(M_XT, KT, T + 1)
    U = m.view(M_U, KT, T + 3)
    cc, Z = m.view(M_C, KT, T), m.view(M_Z, KT, T)
    V = m.view(M_V, NT * ML_H, ML_V + 1)
    q, k = m.view(M_Q, ML_H, T), m.view(M_K, ML_H, T)
    qs, E, SI = m.view(M_QS, ML_H, T), m.view(M_E, ML_H, T), m.view(M_SI, ML_H, T)
    sig = [m.view(M_SI + 512 * n, T) for n in range(2)]
    gw = m.view(M_ROWS, KT, 8)
    gates = m.view(M_SM, NT, 8)
    bias = m.view(M_SM + 32, 2, rows=slice(0, 4))
    consts = m.view(M_ROWS + 64, 3, T, rows=slice(0, 4))
    li, lf, b, mx = (m.view(M_ROWS + 64 + (3 + n) * T, T, rows=slice(0, 4)) for n in range(4))
    sel = consts[:, 2, :].rearrange("p (h n) -> p h n", n=P)
    small = m.view(M_SM + 40, 20, rows=slice(0, 4))
    m0 = small[:, 0:5]
    last_of = lambda x: x.rearrange("p (c t) -> p c t", t=P)[:, :, P - 1]
    by_chunk = lambda x: x.rearrange("p (c t) -> p c t", t=P)
    tri = m.view(A_CONST + C_TRI, P)
    ident = m.view(A_CONST + C_ID, P)
    prm = A_PT + 128
    col = lambda at, j: m.view(prm + at + j, 1)
    done, act_done, z_used, conv_done, sig_ready, rows_used, aux, v_done, chain, c_ready, sig_free = (m.sem(n) for n in (
        "tile_done", "act_evacuated", "g_gated", "conv_done", "sig_ready", "out_rows_used", "aux_loaded", "v_rows_done",
        "dve_chain", "c_ready", "sig_used"))
    rows_ready, softplus, cols_ready, mu_used = (m.sem(n) for n in ("rows_ready", "softplus", "cols_ready", "mu_used"))
    tiles = [("gates", 0), ("gates_t", 0)] + [("u", j) for j in range(KT)] + [("z", j) for j in range(KT)]
    tiles += [(w, h) for w in "qk" for h in range(ML_H)] + [("cols", 0)]
    tiles += [(w, h) for w in ("mu", "init") for h in range(ML_H)]
    place = {t: n for n, t in enumerate(tiles)}
    m.used_by += [(done.handle, done.at(place["u", j] + 1)) for j in range(KT)]
    m.used_by += [(done.handle, done.at(place["z", j] + 1)) for j in range(KT)]
    m.used_by += [(done.handle, done.at(place[w, 3] + 1)) for w in "qk"]
    m.used_by += [(rows_used.handle, rows_used.at(n + 1)) for n in range(7)] + [(v_done.handle, v_done.at(8))]
    count = [0]
    with nc.Block() as block:
        def conv_sig(act, j):
            act.wait_ge(conv_done.handle, conv_done.at(j + 1))
            if j >= 2:
                act.wait_ge(c_ready.handle, c_ready.at(j - 1))
            nc.scalar.activation(sig[j % 2], cc[:, j, :], ACT.Sigmoid, bias=col(ML_CB, j)).then_inc(sig_ready.handle, 1)

        @block.sync
        def _(sp):
            with nc.allow_non_contiguous_dma(reason="eight columns of gate weights, four biases"):
                sp.dma_start(gw, w_if.rearrange("(k p) n -> p k n", p=P)).then_inc(aux.handle, 16)
                sp.dma_start(bias[:, 0:1], i_bias.unsqueeze(1)).then_inc(aux.handle, 16)
                sp.dma_start(bias[:, 1:2], f_bias.unsqueeze(1)).then_inc(aux.handle, 16)
            sp.dma_start(consts, rows_src).then_inc(aux.handle, 16)
            m.load_weights(sp, n0 + 26 + SLOTS)

        @block.tensor
        def _(pe):
            w = n0
            pe.wait_ge(aux.handle, aux.at(64))
            for n, (what, j) in enumerate(tiles):
                bank = m.bank[n % 8]
                if n >= 8:
                    before = tiles[n - 8]
                    if before[0] == "z":
                        pe.wait_ge(z_used.handle, z_used.at(before[1] + 1))
                    else:
                        pe.wait_ge(act_done.handle, act_done.at(n - 7))
                if what == "gates":
                    for a in range(NT):
                        for c in range(KT):
                            last = nc.tensor.matmul(bank[:, 8 * a:8 * a + 8], xt[:, c, 1 + a * P:1 + (a + 1) * P], gw[:, c, :],
                                                    start=c == 0, stop=c == KT - 1)
                elif what == "gates_t":
                    pe.wait_ge(act_done.handle, act_done.at(1))
                    for f in range(2):
                        for a in range(NT):
                            last = nc.tensor.transpose((bank if f == 0 else m.bank[7])[0:4, a * P:(a + 1) * P],
                                                       gates[:, a, 4 * f:4 * f + 4], ident)
                elif what in "uz":
                    if (what, j) == ("u", 5):
                        pe.wait_ge(act_done.handle, act_done.at(2))
                    m.weights_arrived(pe, w)
                    slot = m.view(m.slot(w), KT, P)
                    for c in range(KT):
                        last = nc.tensor.matmul(bank[:, :], slot[:, c, :], xt[:, c, 1:T + 1], start=c == 0, stop=c == KT - 1)
                    w += 1
                elif what == "cols":
                    pe.wait_ge(rows_ready.handle, rows_ready.at(2))
                    for c in range(NT):
                        for f, row in enumerate((li, b)):
                            last = nc.tensor.transpose(bank[:, 8 * c + 4 * f:8 * c + 4 * f + 4], row[:, c * P:(c + 1) * P],
                                                       ident[0:4, 0:4])
                elif what in ("mu", "init"):
                    last = nc.tensor.matmul(bank[:, :], sel[:, j, :], mx if what == "mu" else lf, start=True, stop=True)
                else:
                    if j == 0:
                        m.weights_arrived(pe, w)
                        slot = m.view(m.slot(w), KT, P)
                        w += 1
                    pe.wait_ge(c_ready.handle, c_ready.at(KT))
                    for e in range(2):
                        last = nc.tensor.matmul(bank[:, :], slot[:, 2 * j + e, :], cc[:, 2 * j + e, :], start=e == 0, stop=e == 1)
                last.then_inc(done.handle, 1)
            pe.wait_ge(act_done.handle, act_done.at(len(tiles)))
            pe.wait_ge(z_used.handle, z_used.at(KT))
            for c in range(KT):
                m.weights_arrived(pe, w)
                slot = m.view(m.slot(w), D)
                for n in range(8):
                    last = nc.tensor.matmul(m.bank[n][:, :], xt[:, c, 1 + (n // 2) * P:1 + (n // 2 + 1) * P],
                                            slot[:, 512 * (n % 2):512 * (n % 2) + 512], start=c == 0, stop=c == KT - 1)
                    if c == KT - 1:
                        last.then_inc(v_done.handle, 1)
                if c < KT - 1:
                    last.then_inc(rows_used.handle, 1)
                w += 1

        @block.scalar
        def _(act):
            for n, (what, j) in enumerate(tiles):
                bank = m.bank[n % 8]
                act.wait_ge(done.handle, done.at(n + 1))
                if what == "gates":
                    out = nc.scalar.activation(m.view(M_SM, 32), bank[:, 0:32], ACT.Copy)
                elif what == "gates_t":
                    act.wait_ge(aux.handle, aux.at(64))
                    nc.scalar.activation(li, bank[0:4, :], ACT.Identity, bias=bias[:, 0:1])
                    out = nc.scalar.activation(lf, m.bank[7][0:4, :], ACT.Identity, bias=bias[:, 1:2])
                elif what == "u":
                    out = nc.scalar.activation(U[:, j, 3:T + 3], bank[:, :], ACT.Copy)
                elif what == "z":
                    if j >= 1:
                        conv_sig(act, j - 1)
                    out = nc.scalar.activation(Z[:, j, :], bank[:, :], ACT.Sigmoid)
                elif what == "cols":
                    cols = bank[:, 0:32].rearrange("p (c n) -> p c n", n=8)
                    nc.scalar.activation(gates[:, :, 0:4], cols[:, :, 0:4], ACT.Copy).then_inc(cols_ready.handle, 1)
                    out = nc.scalar.activation(gates[:, :, 4:8], cols[:, :, 4:8], ACT.Exp)
                    act.wait_ge(cols_ready.handle, cols_ready.at(1))
                elif what == "mu":
                    act.wait_ge(mu_used.handle, mu_used.at(j + 1))
                    for c in range(NT):
                        out = nc.scalar.activation(E[:, j, c * P:(c + 1) * P], E[:, j, c * P:(c + 1) * P], ACT.Exp,
                                                   bias=gates[:, c, j:j + 1])
                elif what == "init":
                    if j == 0:
                        act.wait_ge(c_ready.handle, c_ready.at(KT))
                    out = nc.scalar.activation(SI[:, j, :], bank[:, :], ACT.Exp)
                elif what == "q":
                    out = nc.scalar.activation(q[:, j, :], bank[:, :], ACT.Copy)
                else:
                    out = nc.scalar.activation(k[:, j, :], bank[:, :], ACT.Copy, scale=P ** -0.5)
                out.then_inc(act_done.handle, 1)
                if (what, j) == ("u", KT - 1):
                    act.wait_ge(rows_ready.handle, rows_ready.at(1))
                    nc.scalar.activation(mx, b, ACT.Exp, scale=-1.0).then_inc(softplus.handle, 1)
                    act.wait_ge(softplus.handle, softplus.at(1))
                    nc.scalar.activation(mx, mx, ACT.Ln, bias=1.0).then_inc(softplus.handle, 1)
                if (what, j) == ("z", KT - 1):
                    conv_sig(act, KT - 1)
            for n in range(8):
                act.wait_ge(v_done.handle, v_done.at(n + 1))
                nc.scalar.activation(V[:, 2 * n:2 * n + 2, 0:ML_V], m.bank[n][:, :].rearrange("p (h c) -> p h c", h=2), ACT.Copy)


        @block.vector
        def _(dve):
            def link(ins):
                count[0] += 1
                ins.then_inc(chain.handle, 1)
                dve.wait_ge(chain.handle, chain.at(count[0]))

            nc.vector.memset(V[:, :, ML_V:ML_V + 1], 1.0)
            link(nc.vector.memset(U[:, :, 0:3], 0.0))

            def gate(j):
                dve.wait_ge(sig_ready.handle, sig_ready.at(j + 1))
                nc.vector.scalar_tensor_tensor(out=cc[:, j, :], in0=cc[:, j, :], scalar=col(ML_CB, j), in1=sig[j % 2],
                                               op0=ALU.add, op1=ALU.mult).then_inc(c_ready.handle, 1)

            def z_gate(j):
                n = place["z", j]
                dve.wait_ge(act_done.handle, act_done.at(n + 1))
                nc.vector.tensor_tensor(Z[:, j, :], m.bank[n % 8][:, :], Z[:, j, :], ALU.mult).then_inc(z_used.handle, 1)

            dve.wait_ge(act_done.handle, act_done.at(2))
            nc.vector.scalar_tensor_tensor(out=b, in0=lf, scalar=-1.0, in1=lf, op0=ALU.mult, op1=ALU.max)\
                .then_inc(rows_ready.handle, 1)
            for j in range(KT):
                dve.wait_ge(act_done.handle, act_done.at(place["u", j] + 1))
                link(nc.vector.tensor_scalar(cc[:, j, :], U[:, j, 0:T], col(ML_CW, j), None, ALU.mult))
                for i in range(1, 4):
                    ins = nc.vector.scalar_tensor_tensor(out=cc[:, j, :], in0=U[:, j, i:i + T], scalar=col(ML_CW + 8 * i, j),
                                                         in1=cc[:, j, :], op0=ALU.mult, op1=ALU.add)
                    if i < 3:
                        link(ins)
                ins.then_inc(conv_done.handle, 1)
            link(nc.vector.tensor_scalar(lf, lf, 0.0, None, ALU.min))
            dve.wait_ge(softplus.handle, softplus.at(2))
            link(nc.vector.tensor_tensor(lf, lf, mx, ALU.subtract))
            link(nc.vector.tensor_tensor_scan(out=b, data0=consts[:, 0, :], data1=lf, initial=0.0, op0=ALU.mult, op1=ALU.add))
            link(nc.vector.tensor_tensor(li, li, b, ALU.subtract))
            link(nc.vector.tensor_tensor_scan(out=mx, data0=consts[:, 1, :], data1=li, initial=NEG, op0=ALU.add, op1=ALU.max))
            nc.vector.memset(m0[:, 0:1], 0.0)
            nc.vector.tensor_copy(small[:, 5:9], last_of(mx))
            link(nc.vector.tensor_copy(small[:, 9:13], last_of(b)))
            link(nc.vector.tensor_tensor_scan(out=m0[:, 1:5], data0=small[:, 5:9], data1=small[:, 9:13], initial=0.0,
                                              op0=ALU.max, op1=ALU.add))
            m0w = m0[:, 0:4].unsqueeze(2).to_broadcast([4, NT, P])
            link(nc.vector.tensor_tensor(by_chunk(mx), by_chunk(mx), m0w, ALU.max))
            nc.vector.tensor_tensor(by_chunk(lf), m0w, by_chunk(mx), ALU.subtract)
            link(nc.vector.scalar_tensor_tensor(out=b, in0=b, scalar=-1.0, in1=mx, op0=ALU.mult, op1=ALU.subtract))
            nc.vector.tensor_scalar(mx, mx, -1.0, None, ALU.mult).then_inc(rows_ready.handle, 1)
            for j in range(KT):
                z_gate(j)
                gate(j)
            for h in range(ML_H):
                n = place["mu", h]
                dve.wait_ge(done.handle, done.at(n + 1))
                nc.vector.tensor_tensor(by_chunk(E[:, h, :]), by_chunk(m.bank[n % 8][:, :]),
                                        tri.unsqueeze(1).to_broadcast([P, NT, P]), ALU.add).then_inc(mu_used.handle, 1)
            for h in range(ML_H):
                dve.wait_ge(act_done.handle, act_done.at(place["init", h] + 1))
                nc.vector.tensor_tensor(qs[:, h, :], q[:, h, :], SI[:, h, :], ALU.mult)
            for j in range(KT):
                nc.vector.tensor_scalar(cc[:, j, :], cc[:, j, :], col(ML_SKIP, j), None, ALU.mult)
    for s, n in ((done, len(tiles)), (act_done, len(tiles)), (z_used, KT), (conv_done, KT), (sig_ready, KT), (rows_used, 7),
                 (aux, 64), (v_done, 8), (chain, count[0]), (c_ready, KT), (rows_ready, 2), (softplus, 2), (cols_ready, 1),
                 (mu_used, ML_H)):
        s.base += n


def ml_chunks(m):
    nc = m.nc
    W1 = ML_V + 1
    V = m.view(M_V, NT * ML_H, W1)
    hm = m.view(M_HM, NT, D)
    q, k, qs = m.view(M_Q, ML_H, T), m.view(M_K, ML_H, T), m.view(M_QS, ML_H, T)
    E, SI = m.view(M_E, ML_H, T), m.view(M_SI, ML_H, T)
    ktok = m.view(M_KTOK, NT * ML_H, P)
    state = m.view(M_STATE, ML_H, W1)
    cols = m.view(M_SM, NT, 8)
    stats = m.view(M_SM + 64, 16, 6)
    den = m.view(M_SM + 40, 16)
    ident = m.view(A_CONST + C_ID, P)
    kt_done, kt_evac, qk_done, p_ready, num_done, num_evac, ds_done, st_ready, chain, zero = (m.sem(n) for n in (
        "ktok_turned", "ktok_evac", "qk_done", "p_ready", "num_done", "num_evac", "ds_done", "state_ready", "dve_chain",
        "state_zeroed"))
    count = [0]
    units = [(c, h) for c in range(NT) for h in range(ML_H)]
    num_bank = lambda n: m.bank[(2, 3, 6, 7)[n % 4]]
    inverse = m.sem("den_inverse")
    with nc.Block() as block:
        @block.tensor
        def _(pe):
            for h in range(ML_H):
                if h >= 2:
                    pe.wait_ge(kt_evac.handle, kt_evac.at(h - 1))
                for c in range(NT):
                    last = nc.tensor.transpose(m.bank[h % 2][:, c * P:(c + 1) * P], k[:, h, c * P:(c + 1) * P], ident)
                last.then_inc(kt_done.handle, 1)
            pe.wait_ge(kt_evac.handle, kt_evac.at(ML_H))
            pe.wait_ge(zero.handle, zero.at(1))

            def product(n):
                c, h = units[n]
                if n >= 2:
                    pe.wait_ge(p_ready.handle, p_ready.at(n - 1))
                t = slice(c * P, (c + 1) * P)
                nc.tensor.matmul(m.bank[n % 2][:, 0:P], k[:, h, t], q[:, h, t], start=True, stop=True).then_inc(qk_done.handle, 1)

            product(0)
            product(1)
            for n, (c, h) in enumerate(units):
                t = slice(c * P, (c + 1) * P)
                if n + 2 < len(units):
                    product(n + 2)
                if n >= 2:
                    pe.wait_ge(st_ready.handle, st_ready.at(n - 1))
                nc.tensor.matmul(m.bank[4 + n % 2][:, 0:W1], ktok[:, ML_H * c + h, :], V[:, n, :], start=True, stop=True)\
                    .then_inc(ds_done.handle, 1)
                pe.wait_ge(p_ready.handle, p_ready.at(n + 1))
                if n >= 4:
                    pe.wait_ge(num_evac.handle, num_evac.at(n - 3))
                if c >= 1:
                    pe.wait_ge(st_ready.handle, st_ready.at(n - ML_H + 1))
                nc.tensor.matmul(num_bank(n)[:, 0:W1], E[:, h, t], V[:, n, :], start=True, stop=False)
                nc.tensor.matmul(num_bank(n)[:, 0:W1], qs[:, h, t], state[:, h, :], start=False, stop=True)\
                    .then_inc(num_done.handle, 1)

        @block.scalar
        def _(act):
            for h in range(ML_H):
                act.wait_ge(kt_done.handle, kt_done.at(h + 1))
                for c in range(NT):
                    last = nc.scalar.activation(ktok[:, ML_H * c + h, :], m.bank[h % 2][:, c * P:(c + 1) * P], ACT.Copy,
                                                scale=E[:, h, c * P + P - 1:c * P + P])
                last.then_inc(kt_evac.handle, 1)
            for n, (c, h) in enumerate(units):
                act.wait_ge(inverse.handle, inverse.at(n // 2 + 1))
                nc.scalar.activation(hm[:, c, ML_V * h:ML_V * (h + 1)], num_bank(n)[:, 0:ML_V], ACT.Copy,
                                     scale=den[:, n:n + 1]).then_inc(num_evac.handle, 1)

        @block.vector
        def _(dve):
            def link(ins):
                count[0] += 1
                ins.then_inc(chain.handle, 1)
                dve.wait_ge(chain.handle, chain.at(count[0]))

            nc.vector.memset(state[:, :, :], 0.0).then_inc(zero.handle, 1)
            dve.wait_ge(kt_evac.handle, kt_evac.at(ML_H))
            dve.wait_ge(zero.handle, zero.at(1))

            def weigh(n):
                c, h = units[n]
                dve.wait_ge(qk_done.handle, qk_done.at(n + 1))
                t = slice(c * P, (c + 1) * P)
                nc.vector.tensor_tensor(E[:, h, t], m.bank[n % 2][:, 0:P], E[:, h, t], ALU.mult).then_inc(p_ready.handle, 1)

            def moments(n):
                c, h = units[n]
                dve.wait_ge(num_evac.handle, num_evac.at(n + 1))
                nc.vector.bn_stats(stats[:, n, :], hm[:, c, ML_V * h:ML_V * (h + 1)])

            weigh(0)
            weigh(1)
            for first in range(0, len(units), 2):
                pair = (first, first + 1)
                for n in pair:
                    if n + 2 < len(units):
                        weigh(n + 2)
                for n in pair:
                    dve.wait_ge(num_done.handle, num_done.at(n + 1))
                    ins = nc.vector.tensor_scalar(den[:, n:n + 1], num_bank(n)[:, ML_V:W1], -1.0, None, ALU.mult)
                link(ins)
                for n in pair:
                    c, h = units[n]
                    ins = nc.vector.scalar_tensor_tensor(out=den[:, n:n + 1], in0=num_bank(n)[:, ML_V:W1],
                                                         scalar=cols[:, c, 4 + h:5 + h], in1=den[:, n:n + 1],
                                                         op0=ALU.max, op1=ALU.max)
                link(ins)
                nc.vector.reciprocal(den[:, first:first + 2], den[:, first:first + 2]).then_inc(inverse.handle, 1)
                for n in pair:
                    c, h = units[n]
                    dve.wait_ge(ds_done.handle, ds_done.at(n + 1))
                    nc.vector.scalar_tensor_tensor(out=state[:, h, :], in0=state[:, h, :], scalar=SI[:, h, c * P + P - 1:c * P + P],
                                                   in1=m.bank[4 + n % 2][:, 0:W1], op0=ALU.mult, op1=ALU.add)\
                        .then_inc(st_ready.handle, 1)
                if first >= 2:
                    moments(first - 2)
                    moments(first - 1)
                dve.wait_ge(st_ready.handle, st_ready.at(first + 2))
            moments(14)
            moments(15)
    for s, n in ((kt_done, ML_H), (kt_evac, ML_H), (qk_done, 16), (p_ready, 16), (num_done, 16), (num_evac, 16), (ds_done, 16),
                 (st_ready, 16), (chain, count[0]), (zero, 1), (inverse, 8)):
        s.base += n


def ml_gate(m):
    nc = m.nc
    hm = m.view(M_HM, NT, D)
    cc, Z, Y = m.view(M_C, KT, T), m.view(M_Z, KT, T), m.view(M_Y, KT, T)
    stats = m.view(M_SM + 64, 16, 6)
    mv = m.view(M_SM + 160, 16, 2)
    ident = m.view(A_CONST + C_ID, P)
    prm = A_PT + 128
    col = lambda at, j: m.view(prm + at + j, 1)
    var, root, normed, turned, y_used, chain = (m.sem(n) for n in (
        "norm_inverse", "norm_root", "hm_normed", "norm_turned", "y_evac", "dve_chain"))
    count = [0]
    with nc.Block() as block:
        @block.vector
        def _(dve):
            def link(ins):
                count[0] += 1
                ins.then_inc(chain.handle, 1)
                dve.wait_ge(chain.handle, chain.at(count[0]))

            for n in range(16):
                ins = nc.vector.bn_aggr(mv[:, n, :], stats[:, n, :])
            link(ins)
            nc.vector.tensor_scalar(mv[:, :, 1], mv[:, :, 1], 1e-6, None, ALU.add).then_inc(var.handle, 1)
            dve.wait_ge(root.handle, root.at(1))
            link(nc.vector.reciprocal(mv[:, :, 1], mv[:, :, 1]))
            for n in range(16):
                part = hm[:, n // 4, ML_V * (n % 4):ML_V * (n % 4 + 1)]
                nc.vector.tensor_scalar(part, part, mv[:, n, 0:1], mv[:, n, 1:2], ALU.subtract, ALU.mult).then_inc(normed.handle, 1)
            for j in range(KT + 1):
                if j < KT:
                    dve.wait_ge(turned.handle, turned.at(j + 1))
                    nc.vector.scalar_tensor_tensor(out=Y[:, j, :], in0=m.bank[j][:, :], scalar=col(ML_GN, j), in1=cc[:, j, :],
                                                   op0=ALU.mult, op1=ALU.add).then_inc(y_used.handle, 1)
                if j > 0:
                    dve.wait_ge(y_used.handle, y_used.at(j))
                    nc.vector.tensor_tensor(Y[:, j - 1, :], Y[:, j - 1, :], Z[:, j - 1, :], ALU.mult)

        @block.scalar
        def _(act):
            act.wait_ge(var.handle, var.at(1))
            nc.scalar.activation(mv[:, :, 1], mv[:, :, 1], ACT.Sqrt).then_inc(root.handle, 1)

        @block.tensor
        def _(pe):
            for a in range(NT):
                pe.wait_ge(normed.handle, normed.at(4 * a + 4))
                for j in range(KT):
                    last = nc.tensor.transpose(m.bank[j][:, a * P:(a + 1) * P], hm[:, a, j * P:(j + 1) * P], ident)
                    if a == NT - 1:
                        last.then_inc(turned.handle, 1)
    for s, n in ((var, 1), (root, 1), (normed, 16), (turned, KT), (chain, count[0]), (y_used, KT)):
        s.base += n


LAYERS = "rsmr"


def encoder(nc, x, norm_g, final_g, rw_w_in, rw_mu, rw_w0, rw_w2, rw_a0, rw_a2, rw_k_k, rw_k_a, rw_r_k, rw_ln_g,
            rw_ln_b, rw_w_out, sw_w_in, sw_sinks, sw_w_out, ml_w_in, ml_conv_w, ml_conv_b, ml_w_q, ml_w_k, ml_i_bias,
            ml_f_bias, ml_gn_g, ml_skip, ml_w_out, consts, consts2, out, spill):
    rows = lambda ap: ap.rearrange("(k c) -> k c", c=P)
    heads = lambda ap: ap.rearrange("h c -> (h c)").rearrange("(k c) -> k c", c=P)
    rw_rows = []
    for j, layer in ((0, 0), (1, 3)):
        rw_rows.append([(RW_NORM, rows(norm_g[layer])),
                        (RW_MU, rw_mu[j].rearrange("g d -> (g d)").rearrange("(k c) -> k c", c=P)),
                        (RW_W0, rows(rw_w0[j])), (RW_A0, rows(rw_a0[j])), (RW_KK, heads(rw_k_k[j])),
                        (RW_KA, heads(rw_k_a[j])), (RW_RK, heads(rw_r_k[j])), (RW_LNG, heads(rw_ln_g[j])),
                        (RW_LNB, heads(rw_ln_b[j]))])
    sw_ml = [(SW_NORM, rows(norm_g[1])), (ML_NORM, rows(norm_g[2])),
             (ML_CW, ml_conv_w[0].rearrange("t d -> (t d)").rearrange("(k c) -> k c", c=P)),
             (ML_CB, rows(ml_conv_b[0])), (ML_GN, heads(ml_gn_g[0])), (ML_SKIP, rows(ml_skip[0]))]
    with ExitStack() as ctx:
        m = Machine(nc, ctx)
        tile = lambda w, at, n=P: (w[:, at:at + n].rearrange("(k p) n -> p k n", p=P), (KT, n))
        row = lambda w, k: (w[k * P:(k + 1) * P, :], (D,))
        plan = []
        for n, kind in enumerate(LAYERS):
            plan.append(len(m.weights))
            if kind == "r":
                j = 1 if n == 3 else 0
                w = rw_w_in[j]
                m.weights += [tile(w, D + k * P) for k in range(KT)]
                m.weights.append(tile(w, 4 * D))
                for g in (0, 2, 3):
                    m.weights += [tile(w, g * D + k * P) for k in range(KT)]
                plan.append(len(m.weights))
            elif kind == "s":
                w = sw_w_in[0]
                m.weights += [row(w[:, 0:D], k) for k in range(KT)]
                m.weights += [(w[2 * k * P:2 * (k + 1) * P, D:D + 512].rearrange("(k p) n -> p k n", p=P), (2, 512))
                              for k in range(KT // 2)]
                m.weights += [tile(w, D + 512 + k * P) for k in range(KT)]
                plan.append(len(m.weights))
                m.weights += [row(sw_w_out[0], k) for k in range(KT)]
            else:
                w = ml_w_in[0]
                m.weights += [tile(w, k * P) for k in range(KT)] + [tile(w, 2 * D + k * P) for k in range(KT)]
                m.weights += [(v.rearrange("h (e p) d -> p (h e) d", p=P), (KT, P)) for v in (ml_w_q[0], ml_w_k[0])]
                m.weights += [row(w[:, D:2 * D], k) for k in range(KT)]
                plan.append(len(m.weights))
                m.weights += [row(ml_w_out[0], k) for k in range(KT)]
        gcol = {"s": P + SW_NORM, "m": P + ML_NORM}
        pairs_of_banks = [(m.bank[2 * a], m.bank[2 * a + 1]) for a in range(NT)]
        rw_banks = [tuple(m.bank[half[a]] for half in RW_OUT_BANKS) for a in range(NT)]

        def next_norm(n, banks, xn_at):
            if n == len(LAYERS):
                return Norm(m, banks, xn_at)
            kind = LAYERS[n]
            return Norm(m, banks, xn_at, M_XT if kind == "m" else A_XT, gcol.get(kind, 256 * (n == 3) + RW_NORM))

        stage_load(m, x, consts, rw_rows, sw_ml, next_norm(0, pairs_of_banks, B_R))
        for n, kind in enumerate(LAYERS):
            a, b = plan[2 * n:2 * n + 2]
            if kind == "r":
                j = 1 if n == 3 else 0
                prm = A_PT + 256 * j
                rw_mix(m, prm, (rw_w2[j], rw_a2[j]), consts2[:, 0:T], a, spill)
                norm = next_norm(n + 1, rw_banks, B_L)
                if n + 1 == len(LAYERS):
                    rw_gate_out(m, prm, rw_w_out[j], consts2[0:NH, 5 * T:7 * T], norm, final_g, out)
                else:
                    rw_gate_out(m, prm, rw_w_out[j], consts2[0:NH, 5 * T:7 * T], norm)
            elif kind == "s":
                sw_project(m, sw_sinks[0], a)
                sw_attend(m)
                stage_out(m, S_Y, b, next_norm(n + 1, pairs_of_banks, B_R))
            else:
                ml_project(m, ml_w_in[0][:, 3 * D:3 * D + 8], ml_i_bias[0], ml_f_bias[0],
                           consts2[0:4, T:4 * T].rearrange("p (a t) -> p a t", a=3), a)
                ml_chunks(m)
                ml_gate(m)
                stage_out(m, M_Y, b, next_norm(n + 1, pairs_of_banks, M_C))


_INS = ["x", "norm_g", "final_g", "rw_w_in", "rw_mu", "rw_w0", "rw_w2", "rw_a0", "rw_a2", "rw_k_k", "rw_k_a", "rw_r_k",
        "rw_ln_g", "rw_ln_b", "rw_w_out", "sw_w_in", "sw_sinks", "sw_w_out", "ml_w_in", "ml_conv_w", "ml_conv_b",
        "ml_w_q", "ml_w_k", "ml_i_bias", "ml_f_bias", "ml_gn_g", "ml_skip", "ml_w_out"]


def kernel(**inputs):
    import numpy as _np
    import concourse.bacc as _bacc
    from concourse import mybir as _mybir
    from concourse.bass_utils import run_bass_kernel_spmd as _run

    nc = _bacc.Bacc("TRN2", target_bir_lowering=False, num_devices=1)
    arrays, args = {}, []
    given = {name: _np.ascontiguousarray(inputs[name]) for name in _INS}
    given["masks"], given["rows"] = constants(), more_constants()
    for name, a in given.items():
        arrays[f"in_{name}"] = a
        args.append(nc.dram_tensor(f"in_{name}", a.shape, _mybir.dt.from_np(a.dtype), kind="ExternalInput").ap())
    args.append(nc.dram_tensor("out_h", (1, T, D), _mybir.dt.float32, kind="ExternalOutput").ap())
    args.append(nc.dram_tensor("spill", (2, P, 4096), _mybir.dt.float32).ap())
    encoder(nc, *args)
    r = _run(nc, [arrays], core_ids=[0])
    return r.results[0]["out_h"]
```
